# Optimizing a Trainium2 kernel written in Bass

```python
import jax, jax.numpy as jnp
from jax import lax
import numpy as np

D_MODEL = 1024
BATCH = 1
SEQ = 1024
DEPTH = 1
DEC_BATCH = 1
DEC_SEQ = 64
PAST_LEN = 128

CHUNK = 64
HEAD_DIM = 64
MIX_WIDTH = D_MODEL
W_A = MIX_WIDTH // 2
W_B = MIX_WIDTH - W_A
H_A = W_A // HEAD_DIM
H_B = W_B // HEAD_DIM
N_PREV_CHUNKS = 8
BAND_CHUNKS = N_PREV_CHUNKS + 1
BAND_PAST = N_PREV_CHUNKS * CHUNK
REL_CLIP = 128
N_REL = 2 * REL_CLIP + 1
Q_BLOCK = 128
N_GROUPS = 4
EXPERTS_PER_GROUP = 8
N_EXPERTS = N_GROUPS * EXPERTS_PER_GROUP
TOP_K_IN_GROUP = 2
D_EXPERT = D_MODEL // 4
IN_COLS = 3 * W_A + H_A + 3 * W_B
SPLITS = (W_A, 2 * W_A, 3 * W_A, 3 * W_A + H_A, 3 * W_A + H_A + W_B, 3 * W_A + H_A + 2 * W_B)
N_MOD = 6
RMS_EPS = 1e-6
ATTN_SCALE = HEAD_DIM ** -0.5
FORGET_BIAS_INIT = 3.0

kernel_name = 'hymba_fox_chunkband_hmoe_stream_step'

def rmsnorm(x, g):
    xf = x.astype(jnp.float32)
    y = xf * lax.rsqrt(jnp.mean(xf * xf, axis=-1, keepdims=True) + RMS_EPS)
    return (y * g.astype(jnp.float32)).astype(x.dtype)

def head_rmsnorm(o, g):
    n, l, h, d = o.shape
    return rmsnorm(o, g.reshape(h, d)).reshape(n, l, h * d)

def modulation(c, w_ada, b_ada):
    m = jax.nn.silu(c) @ w_ada + b_ada
    return jnp.split(m[:, None, :], N_MOD, axis=-1)

def modulate(x, g, shift, scale):
    return rmsnorm(x, g) * (1 + scale) + shift

def project(h, w_in, b_f):
    n, l, _ = h.shape
    qa, ka, va, fa, qb, kb, vb = jnp.split(h @ w_in, SPLITS, axis=-1)
    heads_a = lambda t: t.reshape(n, l, H_A, HEAD_DIM)
    heads_b = lambda t: t.reshape(n, l, H_B, HEAD_DIM)
    logf = jax.nn.log_sigmoid((fa + b_f).astype(jnp.float32))
    return heads_a(qa), heads_a(ka), heads_a(va), logf, heads_b(qb), heads_b(kb), heads_b(vb)

def merge(o_a, o_b, g_a, g_b, w_out):
    return jnp.concatenate([head_rmsnorm(o_a, g_a), head_rmsnorm(o_b, g_b)], axis=-1) @ w_out

def fox_attend(q, fq, qpos, k, v, fk, kpos):
    s = jnp.einsum('nqhd,nkhd->nhqk', q, k).astype(jnp.float32) * ATTN_SCALE
    s = s + jnp.swapaxes(fq, 1, 2)[:, :, :, None] - jnp.swapaxes(fk, 1, 2)[:, :, None, :]
    s = jnp.where(kpos[None, :] <= qpos[:, None], s, -jnp.inf)
    p = jax.nn.softmax(s, axis=-1).astype(v.dtype)
    return jnp.einsum('nhqk,nkhd->nqhd', p, v)

def fox_prompt(q, k, v, logf):
    n, s, h, d = q.shape
    nb = s // Q_BLOCK
    f = jnp.cumsum(logf, axis=1)
    pos = jnp.arange(s)
    blocks = (q.reshape(n, nb, Q_BLOCK, h, d).swapaxes(0, 1),
              f.reshape(n, nb, Q_BLOCK, h).swapaxes(0, 1),
              pos.reshape(nb, Q_BLOCK))
    o = lax.map(lambda b: fox_attend(b[0], b[1], b[2], k, v, f, pos), blocks)
    return o.swapaxes(0, 1).reshape(n, s, h, d)

def fox_sample(q, k, v, logf, cache_k, cache_v, cache_logf):
    p_len, t = cache_k.shape[1], q.shape[1]
    k_all = jnp.concatenate([cache_k, k], axis=1)
    v_all = jnp.concatenate([cache_v, v], axis=1)
    f = jnp.cumsum(jnp.concatenate([cache_logf.astype(jnp.float32), logf], axis=1), axis=1)
    kpos = jnp.arange(p_len + t)
    return fox_attend(q, f[:, p_len:], kpos[p_len:], k_all, v_all, f, kpos)

def band_mask(qpos, kpos):
    qc = (qpos // CHUNK)[:, :, None]
    kc = (kpos // CHUNK)[:, None, :]
    return (kpos[:, None, :] >= 0) & (kc <= qc) & (kc >= qc - N_PREV_CHUNKS)

def band_attend(q, k, v, rel, mask, rel_bias):
    s = jnp.einsum('ncqhd,nckhd->nchqk', q, k).astype(jnp.float32) * ATTN_SCALE
    bias = rel_bias.astype(jnp.float32)[:, jnp.clip(rel, -REL_CLIP, REL_CLIP) + REL_CLIP]
    s = jnp.where(mask[None, :, None], s + bias[None, None], -jnp.inf)
    p = jax.nn.softmax(s, axis=-1).astype(v.dtype)
    return jnp.einsum('nchqk,nckhd->ncqhd', p, v)

def band_prompt(q, k, v, rel_bias):
    n, s, h, d = q.shape
    nc = s // CHUNK

    def gather_band(x):
        xc = jnp.pad(x, ((0, 0), (BAND_PAST, 0), (0, 0), (0, 0))).reshape(n, nc + N_PREV_CHUNKS, CHUNK, h, d)
        xb = jnp.stack([xc[:, j:j + nc] for j in range(BAND_CHUNKS)], axis=2)
        return xb.reshape(n, nc, BAND_CHUNKS * CHUNK, h, d)

    start = jnp.arange(nc)[:, None] * CHUNK
    qpos = start + jnp.arange(CHUNK)[None, :]
    kpos = start - BAND_PAST + jnp.arange(BAND_CHUNKS * CHUNK)[None, :]
    rel = qpos[0][:, None] - kpos[0][None, :]
    o = band_attend(q.reshape(n, nc, CHUNK, h, d), gather_band(k), gather_band(v),
                    rel, band_mask(qpos, kpos), rel_bias)
    return o.reshape(n, s, h, d)

def band_sample(q, k, v, cache_k, cache_v, p_len, rel_bias):
    lb, t = cache_k.shape[1], q.shape[1]
    qpos = p_len + jnp.arange(t)
    kpos = p_len - lb + jnp.arange(lb + t)
    k_all = jnp.concatenate([cache_k, k], axis=1)[:, None]
    v_all = jnp.concatenate([cache_v, v], axis=1)[:, None]
    o = band_attend(q[:, None], k_all, v_all, qpos[:, None] - kpos[None, :],
                    band_mask(qpos[None], kpos[None]), rel_bias)
    return o[:, 0]

def mixer_prompt(h, w_in, b_f, rel_bias, g_a, g_b, w_out):
    qa, ka, va, logf, qb, kb, vb = project(h, w_in, b_f)
    y = merge(fox_prompt(qa, ka, va, logf), band_prompt(qb, kb, vb, rel_bias), g_a, g_b, w_out)
    lb = min(BAND_PAST, h.shape[1])
    return y, (ka, va, logf, kb[:, -lb:], vb[:, -lb:])

def mixer_sample(h, cache_k_a, cache_v_a, cache_logf_a, cache_k_b, cache_v_b, w_in, b_f, rel_bias, g_a, g_b, w_out):
    qa, ka, va, logf, qb, kb, vb = project(h, w_in, b_f)
    p_len = cache_k_a.shape[1]
    o_a = fox_sample(qa, ka, va, logf, cache_k_a, cache_v_a, cache_logf_a)
    o_b = band_sample(qb, kb, vb, cache_k_b, cache_v_b, p_len, rel_bias)
    return merge(o_a, o_b, g_a, g_b, w_out), (ka, va, logf, kb, vb)

def hier_moe(h, w_rg, b_rg, w_re, b_re, w_gate, w_up, w_down):
    n, l, d = h.shape
    x = h.reshape(n * l, d)
    g_logits = (x @ w_rg + b_rg).astype(jnp.float32)
    g_idx = jnp.argmax(g_logits, axis=-1)
    g_w = jnp.take_along_axis(jax.nn.softmax(g_logits, axis=-1), g_idx[:, None], axis=1)[:, 0]
    e_logits = (x @ w_re + b_re).astype(jnp.float32).reshape(-1, N_GROUPS, EXPERTS_PER_GROUP)
    e_in = jnp.take_along_axis(e_logits, g_idx[:, None, None], axis=1)[:, 0]
    e_val, e_idx = lax.top_k(e_in, TOP_K_IN_GROUP)
    e_w = jax.nn.softmax(e_val, axis=-1) * g_w[:, None]
    expert_id = g_idx[:, None] * EXPERTS_PER_GROUP + e_idx
    combine = jnp.einsum('tke,tk->te', jax.nn.one_hot(expert_id, N_EXPERTS, dtype=jnp.float32), e_w)

    def expert_step(acc, args):
        wg, wu, wd, cw = args
        hh = jax.nn.silu(x @ wg) * (x @ wu)
        return acc + (hh * cw[:, None].astype(hh.dtype)) @ wd, None

    y, _ = lax.scan(expert_step, jnp.zeros_like(x), (w_gate, w_up, w_down, combine.T))
    return y.reshape(n, l, d)

def setup_inputs(seed: int = 0) -> dict:
    key = jax.random.key(seed)
    ks = jax.random.split(key, 32)
    f32 = jnp.float32

    def nrm(k, shape, s=1.0):
        return s * jax.random.normal(k, shape, f32)

    lb = min(BAND_PAST, PAST_LEN)
    return {
        'x_prompt': nrm(ks[0], (BATCH, SEQ, D_MODEL)),
        'x_sample': nrm(ks[1], (DEC_BATCH, DEC_SEQ, D_MODEL)),
        'cache_k_a': nrm(ks[2], (DEPTH, DEC_BATCH, PAST_LEN, H_A, HEAD_DIM)),
        'cache_v_a': nrm(ks[3], (DEPTH, DEC_BATCH, PAST_LEN, H_A, HEAD_DIM)),
        'cache_logf_a': jax.nn.log_sigmoid(FORGET_BIAS_INIT + nrm(ks[4], (DEPTH, DEC_BATCH, PAST_LEN, H_A))),
        'cache_k_b': nrm(ks[5], (DEPTH, DEC_BATCH, lb, H_B, HEAD_DIM)),
        'cache_v_b': nrm(ks[6], (DEPTH, DEC_BATCH, lb, H_B, HEAD_DIM)),
        'c_prompt': nrm(ks[7], (BATCH, D_MODEL)),
        'c_sample': nrm(ks[8], (DEC_BATCH, D_MODEL)),
        'w_ada': nrm(ks[9], (DEPTH, D_MODEL, N_MOD * D_MODEL), 0.5 * D_MODEL ** -0.5),
        'b_ada': nrm(ks[10], (DEPTH, N_MOD * D_MODEL), 0.02),
        'norm_mix': 1.0 + nrm(ks[11], (DEPTH, D_MODEL), 0.1),
        'norm_ffn': 1.0 + nrm(ks[12], (DEPTH, D_MODEL), 0.1),
        'w_in': nrm(ks[13], (DEPTH, D_MODEL, IN_COLS), D_MODEL ** -0.5),
        'b_fgate': FORGET_BIAS_INIT + nrm(ks[14], (DEPTH, H_A), 0.5),
        'rel_bias': nrm(ks[15], (DEPTH, H_B, N_REL), 0.5),
        'onorm_a': 1.0 + nrm(ks[16], (DEPTH, W_A), 0.1),
        'onorm_b': 1.0 + nrm(ks[17], (DEPTH, W_B), 0.1),
        'w_out': nrm(ks[18], (DEPTH, MIX_WIDTH, D_MODEL), MIX_WIDTH ** -0.5),
        'w_router_group': nrm(ks[19], (DEPTH, D_MODEL, N_GROUPS), D_MODEL ** -0.5),
        'b_router_group': nrm(ks[20], (DEPTH, N_GROUPS), 0.01),
        'w_router_expert': nrm(ks[21], (DEPTH, D_MODEL, N_EXPERTS), D_MODEL ** -0.5),
        'b_router_expert': nrm(ks[22], (DEPTH, N_EXPERTS), 0.01),
        'w_gate': nrm(ks[23], (DEPTH, N_EXPERTS, D_MODEL, D_EXPERT), D_MODEL ** -0.5),
        'w_up': nrm(ks[24], (DEPTH, N_EXPERTS, D_MODEL, D_EXPERT), D_MODEL ** -0.5),
        'w_down': nrm(ks[25], (DEPTH, N_EXPERTS, D_EXPERT, D_MODEL), D_EXPERT ** -0.5),
        'norm_final': 1.0 + nrm(ks[26], (D_MODEL,), 0.1),
    }

def reference(x_prompt, x_sample, cache_k_a, cache_v_a, cache_logf_a, cache_k_b, cache_v_b,
              c_prompt, c_sample, w_ada, b_ada, norm_mix, norm_ffn, w_in, b_fgate, rel_bias,
              onorm_a, onorm_b, w_out, w_router_group, b_router_group, w_router_expert,
              b_router_expert, w_gate, w_up, w_down, norm_final):
    xp, xs = x_prompt, x_sample
    st_p, st_s = [], []
    for l in range(DEPTH):
        mix_w = (w_in[l], b_fgate[l], rel_bias[l], onorm_a[l], onorm_b[l], w_out[l])
        moe_w = (w_router_group[l], b_router_group[l], w_router_expert[l], b_router_expert[l],
                 w_gate[l], w_up[l], w_down[l])
        sh1, sc1, g1, sh2, sc2, g2 = modulation(c_prompt, w_ada[l], b_ada[l])
        y, st = mixer_prompt(modulate(xp, norm_mix[l], sh1, sc1), *mix_w)
        xp = xp + g1 * y
        xp = xp + g2 * hier_moe(modulate(xp, norm_ffn[l], sh2, sc2), *moe_w)
        st_p.append(st)
        sh1, sc1, g1, sh2, sc2, g2 = modulation(c_sample, w_ada[l], b_ada[l])
        y, st = mixer_sample(modulate(xs, norm_mix[l], sh1, sc1), cache_k_a[l], cache_v_a[l],
                             cache_logf_a[l], cache_k_b[l], cache_v_b[l], *mix_w)
        xs = xs + g1 * y
        xs = xs + g2 * hier_moe(modulate(xs, norm_ffn[l], sh2, sc2), *moe_w)
        st_s.append(st)

    def stack(sts, i):
        return jnp.stack([st[i] for st in sts], axis=0)

    y_prompt = rmsnorm(xp, norm_final)
    y_sample = rmsnorm(xs, norm_final)
    return (y_prompt, y_sample,
            stack(st_p, 0), stack(st_p, 1), stack(st_p, 2), stack(st_p, 3), stack(st_p, 4),
            stack(st_s, 0), stack(st_s, 1), stack(st_s, 2), stack(st_s, 3), stack(st_s, 4))


_drawn_inputs = setup_inputs


def setup_inputs(seed=0):
    import zlib

    import numpy as np

    out = dict(_drawn_inputs(seed))
    spreads = {}
    factors = {'cache_logf_a': 10.923,
     'b_router_group': 26.079,
     'b_router_expert': 31.726,
     'onorm_b': 2.743}
    for name, (base, spread) in spreads.items():
        noise = np.random.default_rng([zlib.crc32(name.encode()), seed]).standard_normal(out[name].shape)
        drawn = base * np.exp(spread * noise) if base else spread * noise
        out[name] = __import__('jax').numpy.asarray(drawn.astype(out[name].dtype))
    for name, factor in factors.items():
        out[name] = (out[name] * factor).astype(out[name].dtype)
    return out
```

```python
from contextlib import ExitStack

import concourse.bass as bass
from concourse import mybir

F32 = mybir.dt.float32
I32 = mybir.dt.int32
ALU = mybir.AluOpType
ACT = mybir.ActivationFunctionType
AX = mybir.AxisListType

P = 128
D = 1024
NC = D // P
SEQ, DEC, PAST = 1024, 64, 128
NT = SEQ // P
TOK = SEQ + DEC
HD = 64
PAIRS = 4
UNITS = 2 * (NT + 1)
KEYS = SEQ + PAST + DEC
BAND_TILES = 5
BAND = BAND_TILES * P
NG, EPG, NE = 4, 8, 32
NR = NG + NE
DE = 256
NBLK = (2 * TOK + NE * (P - 1)) // P
REGION = 9 * P
DUMMY = NE * REGION
LISTS = DUMMY + P
TABLE = NBLK + 4
SCALE = HD ** -0.5
EPS = 1e-6
NEG = -1e30 / SCALE
FAR = 1 << 20
BIG = 1e38

V_C, V_BADA, V_NMIX, V_ONORM, V_NFFN, V_END = 0, 16, 64, 72, 80, 88
K_ID, K_CAUSAL, K_BEFORE, K_ONES = 0, P, 2 * P, 3 * P
K_PRIG = 4 * P
K_PRIE = K_PRIG + NG
K_BASE = K_PRIE + NE
K_THR = K_BASE + NE
K_BLK = K_THR + 9
K_TOK = K_BLK + TABLE
K_END = K_TOK + 4
SH1, SC1, G1, SH2, SC2, G2 = range(6)


def rows_of(t):
    return DEC if isinstance(t, int) and t == NT else P


def cond_of(t):
    return 1 if isinstance(t, int) and t == NT else 0


def alone(eng, sem, value, begun):
    eng.wait_ge(sem, value)
    eng.sem_inc(begun, 1)


def ahead(i, j, m):
    return (j + m) % 2, i + (j + m) // 2


def rep(ap, dim, n):
    a = ap.unsqueeze(dim)
    shape = list(a.shape)
    shape[dim] = n
    return a.to_broadcast(shape)


class Scope:

    def __init__(self, nc, ctx, name):
        self.nc, self.ctx, self.name = nc, ctx, name

    def sb(self, name, shape, dt=F32):
        return self.ctx.enter_context(self.nc.sbuf_tensor(f"{self.name}_{name}_sb", shape, dt))

    def ps(self, name, shape, dt=F32):
        return self.ctx.enter_context(self.nc.psum_tensor(f"{self.name}_{name}_ps", shape, dt))

    def sem(self, name):
        return self.ctx.enter_context(self.nc.semaphore(f"{self.name}_{name}_sem"))


class Own:

    def __init__(self, eng, sem, base=0):
        self.eng, self.sem, self.base, self.n = eng, sem, base, 0

    def __call__(self, ins, wait=True):
        ins.then_inc(self.sem, 1)
        self.n += 1
        if wait:
            self.eng.wait_ge(self.sem, self.base + self.n)


def build(nc, a, o):
    with ExitStack() as ctx:
        keep = Scope(nc, ctx, "keep")
        consts = keep.sb("consts", [P, K_END])
        vecs = keep.sb("vecs", [P, V_END])
        mod = keep.sb("mod", [P, 6, NC, 2])
        sc = keep.sb("silu_c", [P, NC, 2])
        rows_all = keep.sb("rows_all", [P, NT + 1, D])
        table = keep.sb("table", [1, 2 + 2 * TABLE], I32)
        begun = keep.sem("begun")
        k = dict(
            begun=begun,
            consts=consts, vecs=vecs, mod=mod, sc=sc, rows_all=rows_all, table=table,
            forget=nc.dram_tensor("forget_bias", (8, KEYS), F32, kind="Internal").ap(),
            h2=nc.dram_tensor("h2_rows", (TOK, D), F32, kind="Internal").ap(),
            lists=nc.dram_tensor("lists", (LISTS, 4), I32, kind="Internal").ap(),
            yrows=nc.dram_tensor("expert_rows", (2 * TOK, D), F32, kind="Internal").ap(),
        )
        with ExitStack() as attention:
            hT = attention.enter_context(nc.sbuf_tensor("hT", [P, NC, TOK], F32))
            with ExitStack() as c:
                modulate_in(nc, Scope(nc, c, "in"), a, o, k, hT)
            for group in ("fox", "band"):
                with ExitStack() as c:
                    attend(nc, Scope(nc, c, group), group, a, o, k, hT)
        with ExitStack() as c:
            g2 = c.enter_context(nc.sbuf_tensor("gate2_rows", [P, 2, D], F32))
            with ExitStack() as c2:
                mix_out(nc, Scope(nc, c2, "mix"), a, o, k, g2)
            with ExitStack() as c2:
                experts(nc, Scope(nc, c2, "moe"), a, k)
            with ExitStack() as c2:
                finish(nc, Scope(nc, c2, "fin"), a, o, k, g2)


def modulation_half(pe, w, sc, out, c0, c1):
    for c in range(c0, c1):
        for kc in range(NC):
            ins = pe.matmul(out[:, 2 * c:2 * c + 2], w[:, kc, (c - c0) * P:(c - c0 + 1) * P], sc[:, kc, :],
                            start=(kc == 0), stop=(kc == NC - 1))
    return ins


def modulate_in(nc, s, a, o, k, hT):
    consts, vecs, mod, sc = k["consts"], k["vecs"], k["mod"], k["sc"]
    w_ada = [s.sb(f"w_ada{j}", [P, NC, D]) for j in range(2)]
    x = [s.sb(f"x{j}", [P, D]) for j in range(2)]
    squares = s.sb("squares", [P, D])
    ssq = s.sb("ssq", [P, 2])
    rstd = s.sb("rstd", [P, 2])
    half = s.sb("minus_half", [P, 1])
    a1 = s.sb("a1", [P, NC, 2])
    w_f = s.sb("w_f", [P, NC, 8])
    b_f = s.sb("b_f", [8, 1])
    z = s.sb("z", [8, TOK])
    e = s.sb("e", [8, TOK])
    logf = s.sb("logf", [8, TOK])
    logf_s = s.sb("logf_s", [8, PAST + DEC])
    cum = s.sb("cum", [8, KEYS])
    logf_rows = s.sb("logf_rows", [P, NT + 1, 8])
    far = s.sb("far", [P, LISTS // P * 4], I32)
    xT_ps = [s.ps(f"xT{j}", [P, NC, P]) for j in range(2)]
    mod_ps = s.ps("mod", [P, 512])
    f_ps = s.ps("f", [8, 3 * 512])

    vec_ld, c_ld, wf_ld = s.sem("vec_ld"), s.sem("c_ld"), s.sem("wf_ld")
    w_ld = [s.sem(f"w_ld{j}") for j in range(2)]
    x_ld = [s.sem(f"x_ld{j}") for j in range(2)]
    silu_done, mod_ready, mod_out = s.sem("silu_done"), s.sem("mod_ready"), s.sem("mod_out")
    a1_done = s.sem("a1_done")
    sq_done, ms_done, rstd_done, xn_done = s.sem("sq_done"), s.sem("ms_done"), s.sem("rstd_done"), s.sem("xn_done")
    xT_ready, xT_out_act, xT_out_dve = s.sem("xT_ready"), s.sem("xT_out_act"), s.sem("xT_out_dve")
    half_set, far_set = s.sem("half_set"), s.sem("far_set")
    f_ready, z_done, e_done, logf_done = s.sem("f_ready"), s.sem("z_done"), s.sem("e_done"), s.sem("logf_done")
    rows_ready, rows_out, cum_done, stored = s.sem("rows_ready"), s.sem("rows_out"), s.sem("cum_done"), s.sem("stored")
    own_dve, own_act = s.sem("own_dve"), s.sem("own_act")
    xp, xs = a["x_prompt"][0], a["x_sample"][0]
    block = s.ctx.enter_context(nc.Block())

    def over_tiles(eng, step):
        with eng.Fori(0, NT // 2) as i:
            for j in range(2):
                step(2 * i + j, j)
        step(NT, 0)

    @block.sync
    def _(sp):
        sp.dma_start(vecs[:, :], a["vecs"]).then_inc(vec_ld, 16)
        sp.dma_start(consts[:, :], a["consts"]).then_inc(c_ld, 16)
        for j, sec in enumerate((SH1, SC1)):
            sp.dma_start(w_ada[j][:, :, :], a["w_ada"][sec]).then_inc(w_ld[j], 16)
        sp.dma_start(w_f[:, :, :], a["w_f"]).then_inc(wf_ld, 16)
        sp.dma_start(b_f[:, :], a["b_f"]).then_inc(wf_ld, 16)
        sp.dma_start(logf_s[:, 0:PAST], a["cache_logf"]).then_inc(wf_ld, 16)
        sp.wait_ge(far_set, 1)
        sp.dma_start(k["lists"].rearrange("(p n) c -> p (n c)", p=P), far[:, :]).then_inc(stored, 16)
        sp.wait_ge(rows_out, 1)
        sp.dma_start(o["logf_prompt"].rearrange("(t p) h -> p t h", p=P), logf_rows[:, 0:NT, :]).then_inc(stored, 16)
        sp.dma_start(o["logf_sample"], logf_rows[0:DEC, NT, :]).then_inc(stored, 16)
        sp.wait_ge(cum_done, 1)
        sp.dma_start(k["forget"], cum[:, :]).then_inc(stored, 16)
        sp.wait_ge(stored, 64)

    @block.gpsimd
    def _(pool):
        pool.sem_inc(k["begun"], 1)
        pool.memset(half[:, :], -0.5).then_inc(half_set, 1)
        pool.memset(far[:, :], FAR).then_inc(far_set, 1)
        pool.wait_ge(half_set, 1)

        def step(t, j):
            r = rows_of(t)
            pool.wait_ge(ms_done, t + 1)
            pool.tensor_tensor(rstd[0:r, j:j + 1], ssq[0:r, j:j + 1], half[0:r, :], ALU.pow).then_inc(rstd_done, 1)

        over_tiles(pool, step)

    @block.scalar
    def _(act):
        act.wait_ge(vec_ld, 16)
        act.activation(sc[:, :, :], vecs[:, V_C:V_C + 16].rearrange("p (k n) -> p k n", n=2), ACT.Silu)\
           .then_inc(silu_done, 1)

        def load(t, j):
            r = rows_of(t)
            src = xs if r == DEC else xp[bass.ds(t * P, P), :]
            act.dma_start(x[j][0:r, :], src).then_inc(x_ld[j], 16)

        for t in range(2):
            load(t, t)
        own = Own(act, own_act)

        def square(t, j, nth):
            r = rows_of(t)
            act.wait_ge(sq_done, t)
            act.wait_ge(x_ld[j], 16 * (nth + 1))
            act.activation(squares[0:r, :], x[j][0:r, :], ACT.Square, accum_out=ssq[0:r, j:j + 1]).then_inc(sq_done, 1)

        def move(t, j, more):
            r, n = rows_of(t), cond_of(t)
            act.wait_ge(xT_ready, t + 1)
            for c in range(0, NC // 2):
                ins = act.activation(hT[:, c, bass.ds(t * P, r)], xT_ps[j][:, c, 0:r], ACT.Identity,
                                     bias=mod[:, SH1, c, n:n + 1], scale=a1[:, c, n:n + 1])
            ins.then_inc(xT_out_act, 1)
            if more:
                load(*more)

        square(0, 0, 0)
        act.wait_ge(a1_done, 1)
        with act.Fori(0, NT // 2 - 1) as i:
            for j in range(2):
                square(2 * i + j + 1, 1 - j, i + j)
                move(2 * i + j, j, (2 * i + j + 2, j))
        square(NT - 1, 1, NT // 2 - 1)
        move(NT - 2, 0, (NT, 0))
        square(NT, 0, NT // 2)
        move(NT - 1, 1, None)
        move(NT, 0, None)
        act.wait_ge(z_done, 1)
        own(act.activation(e[:, :], z[:, :], ACT.Abs))
        own(act.activation(e[:, :], e[:, :], ACT.Exp, scale=-1.0))
        act.activation(e[:, :], e[:, :], ACT.Ln, bias=1.0).then_inc(e_done, 1)

    @block.tensor
    def _(pe):
        pe.wait_ge(silu_done, 1)
        for j in range(2):
            pe.wait_ge(w_ld[j], 16)
            modulation_half(pe, w_ada[j], sc, mod_ps[:, 16 * j:16 * j + 16], 0, NC).then_inc(mod_ready, 1)
        pe.wait_ge(c_ld, 16)
        ident = consts[:, K_ID:K_ID + P]

        def step(t, j):
            r = rows_of(t)
            pe.wait_ge(xn_done, t + 1)
            pe.wait_ge(xT_out_act, t)
            pe.wait_ge(xT_out_dve, t)
            for c in range(NC):
                ins = pe.transpose(xT_ps[j][:, c, 0:r], x[j][0:r, c * P:(c + 1) * P], ident[0:r, 0:r])
            ins.then_inc(xT_ready, 1)

        over_tiles(pe, step)
        pe.wait_ge(wf_ld, 48)
        pe.wait_ge(xT_out_act, NT + 1)
        pe.wait_ge(xT_out_dve, NT + 1)
        for n0, n in ((0, 512), (512, 512), (SEQ, DEC)):
            for kc in range(NC):
                ins = pe.matmul(f_ps[:, n0:n0 + n], w_f[:, kc, :], hT[:, kc, n0:n0 + n],
                                start=(kc == 0), stop=(kc == NC - 1))
        ins.then_inc(f_ready, 1)
        pe.wait_ge(logf_done, 1)
        for t in range(NT + 1):
            r = rows_of(t)
            ins = pe.transpose(mod_ps[0:r, 64 + 8 * t:72 + 8 * t], logf[:, t * P:t * P + r], ident[0:8, 0:8])
        ins.then_inc(rows_ready, 1)

    @block.vector
    def _(dve):
        own = Own(dve, own_dve)

        def normalise(t, j):
            r = rows_of(t)
            dve.wait_ge(sq_done, t + 1)
            dve.tensor_scalar(ssq[0:r, j:j + 1], ssq[0:r, j:j + 1], 1.0 / D, EPS, ALU.mult, ALU.add).then_inc(ms_done, 1)
            dve.wait_ge(rstd_done, t + 1)
            dve.tensor_scalar(x[j][0:r, :], x[j][0:r, :], rstd[0:r, j:j + 1], None, ALU.mult).then_inc(xn_done, 1)

        def move(t, j):
            r, n = rows_of(t), cond_of(t)
            dve.wait_ge(xT_ready, t + 1)
            for c in range(NC // 2, NC):
                ins = dve.tensor_scalar(hT[:, c, bass.ds(t * P, r)], xT_ps[j][:, c, 0:r], a1[:, c, n:n + 1],
                                        mod[:, SH1, c, n:n + 1], ALU.mult, ALU.add)
            ins.then_inc(xT_out_dve, 1)

        dve.wait_ge(vec_ld, 16)
        for sec in (SH1, SC1):
            dve.wait_ge(mod_ready, 2)
            bias = vecs[:, V_BADA + 8 * sec:V_BADA + 8 * sec + 8]
            own(dve.tensor_tensor(mod[:, sec, :, :], mod_ps[:, 16 * sec:16 * sec + 16].rearrange("p (c n) -> p c n", n=2),
                                  rep(bias, 2, 2), ALU.add))
        dve.scalar_tensor_tensor(a1[:, :, :], mod[:, SC1, :, :], 1.0, rep(vecs[:, V_NMIX:V_NMIX + 8], 2, 2),
                                 ALU.add, ALU.mult).then_inc(a1_done, 1)
        dve.wait_ge(a1_done, 1)
        normalise(0, 0)
        with dve.Fori(0, NT // 2 - 1) as i:
            for j in range(2):
                normalise(2 * i + j + 1, 1 - j)
                move(2 * i + j, j)
        normalise(NT - 1, 1)
        move(NT - 2, 0)
        normalise(NT, 0)
        move(NT - 1, 1)
        move(NT, 0)

        dve.wait_ge(f_ready, 1)
        dve.wait_ge(wf_ld, 48)
        dve.tensor_scalar(z[:, :], f_ps[:, 0:TOK], b_f[:, 0:1], None, ALU.add).then_inc(z_done, 1)
        dve.wait_ge(e_done, 1)
        dve.scalar_tensor_tensor(logf[:, :], z[:, :], 0.0, e[:, :], ALU.min, ALU.subtract).then_inc(logf_done, 1)
        dve.wait_ge(logf_done, 1)
        own(dve.tensor_copy(logf_s[:, PAST:PAST + DEC], logf[:, SEQ:TOK]))
        one = consts[0:8, K_ONES:K_ONES + 1]
        own(dve.tensor_tensor_scan(cum[:, 0:SEQ], one.to_broadcast([8, SEQ]), logf[:, 0:SEQ], 0.0, ALU.mult, ALU.add))
        own(dve.tensor_tensor_scan(cum[:, SEQ:KEYS], one.to_broadcast([8, PAST + DEC]), logf_s[:, :], 0.0,
                                   ALU.mult, ALU.add))
        dve.tensor_scalar(cum[:, :], cum[:, :], -1.0 / SCALE, None, ALU.mult).then_inc(cum_done, 1)
        dve.wait_ge(rows_ready, 1)
        dve.tensor_copy(logf_rows[:, 0:NT, :], mod_ps[:, 64:64 + 8 * NT].rearrange("p (t h) -> p t h", h=8))
        dve.tensor_copy(logf_rows[0:DEC, NT, :], mod_ps[0:DEC, 64 + 8 * NT:72 + 8 * NT]).then_inc(rows_out, 1)


def unit_keys(group, t):
    if t == NT:
        return [(SEQ, PAST, "cache"), (SEQ + PAST, DEC, NT)]
    first = max(0, t - BAND_TILES + 1) if group == "band" else 0
    return [(b * P, P, b) for b in range(first, t + 1)]


def attend(nc, s, group, a, o, k, hT):
    fox = group == "fox"
    consts, vecs, mod, sc, rows_all, begun = k["consts"], k["vecs"], k["mod"], k["sc"], k["rows_all"], k["begun"]
    g = 0 if fox else 1
    ident = consts[:, K_ID:K_ID + P]
    w = s.sb("w", [P, NC, 3 * P])
    qT = s.sb("qT", [P, TOK])
    kT = s.sb("kT", [P, KEYS])
    kv = s.sb("kv", [P, NT + 1, 2, P])
    cache = s.sb("cache", [P, 2, P])
    probs = [s.sb(f"probs{j}", [P, SEQ]) for j in range(2)]
    pT = s.sb("pT", [P, NT, P])
    nmax = s.sb("nmax", [P, UNITS])
    nmax_off = s.sb("nmax_off", [P, UNITS])
    denom = s.sb("denom", [P, UNITS])
    rden = s.sb("rden", [P, UNITS])
    if fox:
        w_ada = s.sb("w_ada", [P, NC, D // 2])
        forget = s.sb("forget", [P, 2, KEYS])
        own_tile = s.sb("own_tile", [P, 2, NT, P])
        own_sample = s.sb("own_sample", [DEC, 2, DEC])
    else:
        bias_all = s.sb("bias_all", [P, 8, BAND])
        bias = s.sb("bias", [P, 2, BAND])
    s_ps = [s.ps(f"s{j}", [P, 1024]) for j in range(2)]
    pT_ps = s.ps("pT", [P, NT, P])
    o_ps = [s.ps(f"o{j}", [P, 512]) for j in range(2)]
    mod_ps = o_ps[1]
    ring = [s_ps[n // 2][:, 512 * (n % 2):512 * (n % 2) + 512] for n in range(4)]

    w_ld, cache_ld, bias_ld, ada_ld = s.sem("w_ld"), s.sem("cache_ld"), s.sem("bias_ld"), s.sem("ada_ld")
    proj_ready, qk_out, kv_out = s.sem("proj_ready"), s.sem("qk_out"), s.sem("kv_out")
    mod_ready, mod_out = s.sem("mod_ready"), s.sem("mod_out")
    bias_ready = s.sem("bias_ready")
    s_ready, off_done, max_done, exp_done = s.sem("s_ready"), s.sem("off_done"), s.sem("max_done"), s.sem("exp_done")
    pT_ready, pT_out, o_ready, rden_done, o_out = (s.sem(n) for n in ("pT_ready", "pT_out", "o_ready", "rden_done", "o_out"))
    stored, masked = s.sem("stored"), s.sem("masked")
    block = s.ctx.enter_context(nc.Block())

    units = [(u // 2, u % 2) for u in range(UNITS)]
    keys = [unit_keys(group, t) for t, _ in units]
    Q = [(0, 512), (512, 512), (SEQ, DEC)]
    JOBS = ["q"] * 3 + ["kv"] * (NT + 1) + ["t"] * 3
    QK_JOBS, KV_JOBS = 6, NT + 1
    out_before = [(sum(x != "kv" for x in JOBS[:j]), sum(x == "kv" for x in JOBS[:j])) for j in range(len(JOBS) + 1)]
    chunks = [[(b, min(b + 4, len(kb))) for b in range(0, len(kb), 4)] for kb in keys]
    chunk0 = [sum(len(c) for c in chunks[:u]) for u in range(UNITS + 1)]
    off0 = [sum(1 for v in range(u) if len(keys[v]) > 1) for u in range(UNITS + 1)]
    STORES = 64 if fox else 64

    @block.sync
    def _(sp):
        if not fox:
            sp.dma_start(bias_all[:, :, :], a["rel"]).then_inc(bias_ld, 16)
        with sp.Fori(0, PAIRS) as i:
            sp.wait_ge(proj_ready, i * len(JOBS))
            sp.dma_start(w[:, :, :], a["w_qkv"][g, bass.ds(i, 1)].rearrange("a p k n -> p (a k) n")).then_inc(w_ld, 16)
            if fox:
                sp.wait_ge(mod_ready, 2 * i)
                sp.dma_start(w_ada[:, :, :], a["w_ada"][bass.ds(i + 2, 1), :, :, 0:512]
                             .rearrange("a p k n -> p (a k) n")).then_inc(ada_ld, 16)
            sp.wait_ge(o_ready, UNITS * i)
            sp.wait_ge(max_done, UNITS * i)
            if fox:
                f = k["forget"][bass.ds(2 * i, 2), :]
                sp.dma_start(forget[:, :, :], rep(f, 0, P)).then_inc(bias_ld, 16)
            for n, name in enumerate(("k", "v")):
                sp.dma_start(cache[:, n, :], a[f"cache_{name}_{'a' if fox else 'b'}"][:, bass.ds(i * P, P)])\
                  .then_inc(cache_ld, 16)
            if fox:
                sp.wait_ge(mod_ready, 2 * i + 1)
                sp.dma_start(w_ada[:, :, :], a["w_ada"][bass.ds(i + 2, 1), :, :, 512:1024]
                             .rearrange("a p k n -> p (a k) n")).then_inc(ada_ld, 16)
            sp.wait_ge(kv_out, KV_JOBS * (i + 1))
            t0 = 0 if fox else NT - o["k_b_prompt"].shape[0] // P
            for n, name in enumerate(("k", "v")):
                dst = o[f"{name}_{'a' if fox else 'b'}_prompt"][:, bass.ds(i * P, P)]
                sp.dma_start(dst.rearrange("(t p) n -> p t n", p=P), kv[:, t0:NT, n, :]).then_inc(stored, 16)
                dst = o[f"{name}_{'a' if fox else 'b'}_sample"][:, bass.ds(i * P, P)]
                sp.dma_start(dst, kv[0:DEC, NT, n, :]).then_inc(stored, 16)
        sp.wait_ge(stored, STORES * PAIRS)

    @block.gpsimd
    def _(pool):
        if not fox:
            pool.wait_ge(bias_ld, 16)
            pool.wait_ge(masked, 3)
        with pool.Fori(0, PAIRS) as i:
            pool.wait_ge(max_done, UNITS * i)
            if fox:
                pool.wait_ge(bias_ld, 16 * (i + 1))
                causal = consts[:, K_CAUSAL:K_CAUSAL + P]
                for h in range(2):
                    pool.tensor_tensor(own_tile[:, h, :, :], forget[:, h, 0:SEQ].rearrange("p (t n) -> p t n", n=P),
                                       rep(causal, 1, NT), ALU.add).then_inc(bias_ready, 1)
                    pool.tensor_tensor(own_sample[:, h, :], forget[0:DEC, h, SEQ + PAST:KEYS],
                                       causal[0:DEC, 0:DEC], ALU.add).then_inc(bias_ready, 1)
            else:
                for h in range(2):
                    pool.tensor_copy(bias[:, h, :], bias_all[:, bass.ds(2 * i + h, 1), :]
                                     .rearrange("p a n -> p (a n)")).then_inc(bias_ready, 2)

    @block.tensor
    def _(pe):
        with pe.Fori(0, PAIRS) as i:
            def mod_half(n):
                pe.wait_ge(ada_ld, 32 * i + 16 * (n + 1))
                if n == 0:
                    pe.wait_ge(o_out, UNITS * i)
                pe.wait_ge(mod_out, 2 * i + n)
                modulation_half(pe, w_ada, sc, mod_ps[:, 0:16], 4 * n, 4 * n + 4).then_inc(mod_ready, 1)

            def slot_free(j):
                if j >= 4:
                    qk, kvs = out_before[j - 3]
                    if JOBS[j - 4] == "kv":
                        pe.wait_ge(kv_out, KV_JOBS * i + kvs)
                    else:
                        pe.wait_ge(qk_out, QK_JOBS * i + qk)
                return ring[j % 4]

            if fox:
                mod_half(0)
            pe.wait_ge(w_ld, 16 * (i + 1))
            for j, (n0, n) in enumerate(Q):
                dst = slot_free(j)
                for kc in range(NC):
                    ins = pe.matmul(dst[:, 0:n], w[:, kc, 0:P], hT[:, kc, n0:n0 + n], start=(kc == 0), stop=(kc == NC - 1))
                ins.then_inc(proj_ready, 1)
            for t in range(NT + 1):
                r, dst = rows_of(t), slot_free(3 + t)
                for kc in range(NC):
                    ins = pe.matmul(dst[0:r, 0:2 * P], hT[:, kc, t * P:t * P + r], w[:, kc, P:3 * P],
                                    start=(kc == 0), stop=(kc == NC - 1))
                ins.then_inc(proj_ready, 1)
            for n in range(3):
                j = 3 + NT + 1 + n
                dst = slot_free(j)
                pe.wait_ge(kv_out, KV_JOBS * i + (4, 8, 9)[n])
                if n < 2:
                    for t in range(4 * n, 4 * n + 4):
                        ins = pe.transpose(dst[:, (t % 4) * P:(t % 4 + 1) * P], kv[:, t, 0, :], ident)
                else:
                    pe.wait_ge(cache_ld, 32 * (i + 1))
                    pe.transpose(dst[:, 0:PAST], cache[:, 0, :], ident)
                    ins = pe.transpose(dst[:, PAST:PAST + DEC], kv[0:DEC, NT, 0, :], ident[0:DEC, 0:DEC])
                ins.then_inc(proj_ready, 1)

            def scores(u):
                (t, h), kb = units[u], keys[u]
                r, lo = rows_of(t), HD * h
                if u >= 2:
                    alone(pe, max_done, UNITS * i + u - 1, begun)
                k0, n = kb[0][0], sum(b[1] for b in kb)
                for c in range(0, n, 512):
                    m = min(512, n - c)
                    ins = pe.matmul(s_ps[u % 2][0:r, c:c + m], qT[lo:lo + HD, t * P:t * P + r],
                                    kT[lo:lo + HD, k0 + c:k0 + c + m], start=True, stop=True)
                ins.then_inc(s_ready, 1)

            def transpose(u):
                (t, h), kb = units[u], keys[u]
                r = rows_of(t)
                alone(pe, exp_done, UNITS * i + u + 1, begun)
                for b0, b1 in chunks[u]:
                    for b in range(b0, b1):
                        m = kb[b][1]
                        ins = pe.transpose(pT_ps[0:m, b, 0:r], probs[u % 2][0:r, b * P:b * P + m], ident[0:r, 0:r])
                    ins.then_inc(pT_ready, 1)

            def values(u):
                (t, h), kb = units[u], keys[u]
                r = rows_of(t)
                pe.wait_ge(o_out, UNITS * i + max(u - 1, 0))
                if fox and u == 1:
                    pe.wait_ge(mod_out, 2 * i + 2)
                for n, (b0, b1) in enumerate(chunks[u]):
                    pe.wait_ge(pT_out, chunk0[UNITS] * i + chunk0[u] + n + 1)
                    for b in range(b0, b1):
                        _, m, vt = kb[b]
                        v = cache[0:m, 1, HD * h:HD * h + HD] if vt == "cache" else kv[0:m, vt, 1, HD * h:HD * h + HD]
                        ins = pe.matmul(o_ps[u % 2][0:r, 0:HD], pT[0:m, b, 0:r], v,
                                        start=(b == 0), stop=(b == len(kb) - 1))
                ins.then_inc(o_ready, 1)

            pe.wait_ge(qk_out, QK_JOBS * (i + 1))
            pe.wait_ge(kv_out, KV_JOBS * (i + 1))
            scores(0)
            scores(1)
            if fox:
                mod_half(1)
            for u in range(UNITS):
                transpose(u)
                if u + 2 < UNITS:
                    scores(u + 2)
                values(u)

    @block.vector
    def _(dve):
        if not fox:
            dve.wait_ge(bias_ld, 16)
            dve.tensor_scalar(bias_all[:, :, :], bias_all[:, :, :], 1.0 / SCALE, None, ALU.mult).then_inc(masked, 1)
            dve.wait_ge(masked, 1)
            dve.memset(bias_all[P // 2:P, :, 0:HD], NEG).then_inc(masked, 1)
            dve.memset(bias_all[0:P // 2, :, BAND - HD:BAND], NEG).then_inc(masked, 1)
        with dve.Fori(0, PAIRS) as i:
            def mod_half(n):
                dve.wait_ge(mod_ready, 2 * i + n + 1)
                cols = slice(8 * n, 8 * n + 8)
                bada = vecs[:, V_BADA:V_BADA + 48].rearrange("p (s c) -> p s c", c=NC)
                dve.tensor_tensor(mod[:, bass.ds(i + 2, 1), 4 * n:4 * n + 4, :].rearrange("p a c n -> p (a c) n"),
                                  mod_ps[:, cols].rearrange("p (c n) -> p c n", n=2),
                                  rep(bada[:, bass.ds(i + 2, 1), 4 * n:4 * n + 4].rearrange("p a c -> p (a c)"), 2, 2),
                                  ALU.add).then_inc(mod_out, 1)

            if fox:
                mod_half(0)
            dve.wait_ge(stored, STORES * i)
            for t in range(NT + 1):
                r, j = rows_of(t), 3 + t
                dve.wait_ge(proj_ready, len(JOBS) * i + j + 1)
                dve.tensor_copy(kv[0:r, t, :, :], ring[j % 4][0:r, 0:2 * P].rearrange("p (a n) -> p a n", a=2))\
                   .then_inc(kv_out, 1)

            def row_max(u):
                (t, h), kb = units[u], keys[u]
                r, n = rows_of(t), sum(b[1] for b in kb)
                if u == 0:
                    dve.wait_ge(bias_ready, 4 * (i + 1))
                alone(dve, s_ready, UNITS * i + u + 1, begun)
                src, dst = s_ps[u % 2], probs[u % 2]
                if not fox:
                    j0 = (BAND_TILES - 1) * P - PAST if t == NT else BAND - n
                    dve.tensor_tensor_reduce(dst[0:r, 0:n], src[0:r, 0:n], bias[0:r, h, j0:j0 + n], -SCALE, BIG,
                                             ALU.add, ALU.min, nmax[0:r, u:u + 1]).then_inc(max_done, 1)
                    return
                off = n - kb[-1][1]
                start = BIG
                if off:
                    k0 = kb[0][0]
                    dve.tensor_tensor_reduce(dst[0:r, 0:off], src[0:r, 0:off], forget[0:r, h, k0:k0 + off], -SCALE, BIG,
                                             ALU.add, ALU.min, nmax_off[0:r, u:u + 1]).then_inc(off_done, 1)
                    alone(dve, off_done, off0[UNITS] * i + off0[u + 1], begun)
                    start = nmax_off[0:r, u:u + 1]
                own = own_sample[:, h, :] if t == NT else own_tile[:, h, t, :]
                dve.tensor_tensor_reduce(dst[0:r, off:n], src[0:r, off:n], own, -SCALE, start,
                                         ALU.add, ALU.min, nmax[0:r, u:u + 1]).then_inc(max_done, 1)

            def move_pT(u):
                (t, h), kb = units[u], keys[u]
                r = rows_of(t)
                for n, (b0, b1) in enumerate(chunks[u]):
                    dve.wait_ge(pT_ready, chunk0[UNITS] * i + chunk0[u] + n + 1)
                    if t == NT:
                        dve.tensor_copy(pT[:, 0, 0:r], pT_ps[:, 0, 0:r])
                        ins = dve.tensor_copy(pT[0:DEC, 1, 0:r], pT_ps[0:DEC, 1, 0:r])
                    else:
                        ins = dve.tensor_copy(pT[:, b0:b1, :], pT_ps[:, b0:b1, :])
                    ins.then_inc(pT_out, 1)
                if u == 0:
                    dve.wait_ge(o_out, UNITS * i)
                dve.reciprocal(rden[0:r, u:u + 1], denom[0:r, u:u + 1]).then_inc(rden_done, 1)

            row_max(0)
            row_max(1)
            if fox:
                mod_half(1)
            for u in range(UNITS):
                move_pT(u)
                if u + 2 < UNITS:
                    row_max(u + 2)

    @block.scalar
    def _(act):
        with act.Fori(0, PAIRS) as i:
            for j, kind in enumerate(JOBS):
                if kind == "kv":
                    continue
                act.wait_ge(proj_ready, len(JOBS) * i + j + 1)
                if kind == "q":
                    n0, n = Q[j]
                    dst = qT[:, n0:n0 + n]
                else:
                    n0, n = [(0, 512), (512, 512), (SEQ, PAST + DEC)][j - 3 - KV_JOBS]
                    dst = kT[:, n0:n0 + n]
                act.activation(dst, ring[j % 4][:, 0:n], ACT.Copy).then_inc(qk_out, 1)

            def exp(u):
                r, n = rows_of(units[u][0]), sum(b[1] for b in keys[u])
                act.wait_ge(max_done, UNITS * i + u + 1)
                act.activation(probs[u % 2][0:r, 0:n], probs[u % 2][0:r, 0:n], ACT.Exp, bias=nmax[0:r, u:u + 1],
                               scale=-1.0, accum_out=denom[0:r, u:u + 1]).then_inc(exp_done, 1)

            def output(u):
                (t, h), r = units[u], rows_of(units[u][0])
                act.wait_ge(o_ready, UNITS * i + u + 1)
                act.wait_ge(rden_done, UNITS * i + u + 1)
                act.activation(rows_all[0:r, t, bass.ds(i * P + (512 * g + HD * h), HD)],
                               o_ps[u % 2][0:r, 0:HD], ACT.Copy, scale=rden[0:r, u:u + 1])\
                   .then_inc(o_out, 1)

            exp(0)
            exp(1)
            for u in range(UNITS):
                if u + 2 < UNITS:
                    exp(u + 2)
                output(u)


def mix_out(nc, s, a, o, k, g2):
    consts, vecs, mod, rows_all, table = k["consts"], k["vecs"], k["mod"], k["rows_all"], k["table"]
    begun = k["begun"]
    ident = consts[:, K_ID:K_ID + P]
    ones = consts[:, K_ONES:K_ONES + P]
    w_out = s.sb("w_out", [P, NC, D])
    w_r = s.sb("w_r", [P, NC, NR])
    b_r = s.sb("b_r", [P, NR])
    g1, sh2, a2 = (s.sb(n, [P, 2, D]) for n in ("gate1_rows", "shift2_rows", "scale2_rows"))
    a2col = s.sb("a2col", [P, NC, 2])
    half = s.sb("minus_half", [P, 2 * NG * 2])
    x = s.sb("x", [P, D])
    osq = s.sb("osq", [P, D])
    hs, hr = s.sb("head_ms", [P, 16]), s.sb("head_rstd", [P, 16])
    on = s.sb("on", [P, D])
    oT = s.sb("oT", [P, NC, P])
    y = s.sb("y", [P, D])
    xsq = s.sb("xsq", [P, D])
    ms, rstd = s.sb("ms", [P, 1]), s.sb("rstd", [P, 1])
    h2 = s.sb("h2", [P, D])
    h2T = s.sb("h2T", [P, NC, P])
    lg = s.sb("lg", [P, NR])
    gmax = s.sb("gmax", [P, 1])
    dg = s.sb("dg", [P, NG])
    eg = s.sb("eg", [P, NG])
    gsum = s.sb("gsum", [P, 1])
    pri_g = s.sb("pri_g", [P, NG])
    best_g = s.sb("best_g", [P, 1])
    pen = s.sb("pen", [P, NG])
    em = s.sb("em", [P, NE])
    em2 = s.sb("em2", [P, NE])
    top = s.sb("top", [P, 8])
    pri_e = s.sb("pri_e", [P, NE])
    best_e = s.sb("best_e", [P, 1])
    oh = s.sb("oh", [P, 2, NE])
    dv, ev, den = s.sb("dv", [P, 1]), s.sb("ev", [P, 1]), s.sb("den", [P, 1])
    picked = s.sb("picked", [P, NE])
    before = s.sb("before", [P, NE])
    slot = s.sb("slot", [P, NE])
    junk = s.sb("junk", [P, NE])
    slot_f = s.sb("slot_f", [P, 2])
    slot_i = s.sb("slot_i", [P, 2], I32)
    tok = s.sb("tok", [P, 2, 2])
    entry = s.sb("entry", [P, 2, 4], I32)
    cnt = s.sb("cnt", [1, NE])
    need = s.sb("need", [1, NE, 9])
    nb, cb = s.sb("nb", [1, NE]), s.sb("cb", [1, NE])
    done = s.sb("done", [1, TABLE, NE])
    eb, bb, start = s.sb("eb", [1, TABLE]), s.sb("bb", [1, TABLE]), s.sb("start", [1, TABLE])
    pairs = s.sb("pairs", [1, NBLK // 2])
    steps = s.sb("steps", [1, 1])

    oT_ps, h2T_ps = s.ps("oT", [P, NC, P]), s.ps("h2T", [P, NC, P])
    y_ps = s.ps("y", [P, D])
    lg_ps, pos_ps = s.ps("lg", [P, 512]), s.ps("pos", [P, 512])

    ld, gate_cols, gate_ready, gate_out = s.sem("ld"), s.sem("gate_cols"), s.sem("gate_ready"), s.sem("gate_out")
    half_set, scaled, zeroed = s.sem("half_set"), s.sem("scaled"), s.sem("zeroed")
    osq_done, hms_done, hr_done, on_ready = s.sem("osq_done"), s.sem("hms_done"), s.sem("hr_done"), s.sem("on_ready")
    oT_ready, oT_out, y_ready, y_used = s.sem("oT_ready"), s.sem("oT_out"), s.sem("y_ready"), s.sem("y_used")
    x_ld, x1_done, xsq_done, ms_done, rstd_done = (s.sem(n) for n in ("x_ld", "x1_done", "xsq_done", "ms_done", "rstd_done"))
    scaled_h2, h2_ready, h2_stored = s.sem("scaled_h2"), s.sem("h2_ready"), s.sem("h2_stored")
    h2T_ready, h2T_out, lg_ready, lg_used = s.sem("h2T_ready"), s.sem("h2T_out"), s.sem("lg_ready"), s.sem("lg_used")
    dg_done, eg_done, dv_done, ev_done = s.sem("dg_done"), s.sem("eg_done"), s.sem("dv_done"), s.sem("ev_done")
    picked_done, pos_ready, slots_done, listed = (s.sem(n) for n in ("picked_done", "pos_ready", "slots_done", "listed"))
    cnt_ready, own_dve, w_own, g_own = s.sem("cnt_ready"), s.sem("own_dve"), s.sem("w_own"), s.sem("g_own")
    xp, xs = a["x_prompt"][0], a["x_sample"][0]
    block = s.ctx.enter_context(nc.Block())
    GATES = [(G1, g1), (SH2, sh2), (SC2, a2), (G2, g2)]

    LOOP = range(0, NT - 3)

    def over_steps(eng, step):
        for n in range(-3, 0):
            step(n)
        with eng.Fori(LOOP.start, LOOP.stop) as n:
            step(n)
        for n in range(LOOP.stop, NT + 1):
            step(n)

    def live(t):
        return not isinstance(t, int) or 0 <= t <= NT

    def tile_rows(t, r):
        return rows_all[0:r, bass.ds(t, 1), :].rearrange("p a n -> p (a n)")

    @block.sync
    def _(sp):
        sp.dma_start(w_out[:, :, :], a["w_out"]).then_inc(ld, 16)
        sp.dma_start(w_r[:, :, :], a["w_r"]).then_inc(ld, 16)
        sp.dma_start(b_r[:, :], rep(a["b_r"], 0, P)).then_inc(ld, 16)

        def step(n):
            t = n + 1
            if live(t):
                r = rows_of(t)
                sp.wait_ge(x1_done, t)
                sp.dma_start(x[0:r, :], xs if r == DEC else xp[bass.ds(t * P, P), :]).then_inc(x_ld, 16)
            if live(n):
                r = rows_of(n)
                sp.wait_ge(h2_ready, n + 1)
                sp.dma_start(k["h2"][bass.ds(n * P, r), :], h2[0:r, :]).then_inc(h2_stored, 16)

        over_steps(sp, step)
        sp.wait_ge(h2_stored, 16 * (NT + 1))

    @block.gpsimd
    def _(pool):
        pool.memset(half[:, :], -0.5).then_inc(half_set, 1)
        pool.memset(entry[:, :, :], 0).then_inc(zeroed, 1)
        pool.memset(before[:, :], 0.0).then_inc(zeroed, 1)
        pool.wait_ge(half_set, 1)

        def step(n):
            if live(n + 1):
                t, r = n + 1, rows_of(n + 1)
                pool.wait_ge(x_ld, 16 * (t + 1))
                pool.wait_ge(y_used, t + 1)
                pool.tensor_tensor(tile_rows(t, r), y[0:r, :], x[0:r, :], ALU.add).then_inc(x1_done, 1)
            if live(n + 3):
                t, r = n + 3, rows_of(n + 3)
                pool.wait_ge(hms_done, t + 1)
                pool.tensor_tensor(hr[0:r, :], hs[0:r, :], half[0:r, :], ALU.pow).then_inc(hr_done, 1)
            if live(n + 1):
                t, r = n + 1, rows_of(n + 1)
                pool.wait_ge(ms_done, t + 1)
                pool.tensor_tensor(rstd[0:r, :], ms[0:r, :], half[0:r, 0:1], ALU.pow).then_inc(rstd_done, 1)
                pool.wait_ge(scaled_h2, t + 1)
                pool.tensor_tensor(h2[0:r, :], h2[0:r, :], sh2[0:r, cond_of(t), :], ALU.add).then_inc(h2_ready, 1)
            if live(n):
                r = rows_of(n)
                alone(pool, slots_done, n + 1, begun)
                for pick in range(2):
                    pool.indirect_dma_start(k["lists"], bass.IndirectOffsetOnAxis(ap=slot_i[0:r, pick:pick + 1], axis=0),
                                            entry[0:r, pick, :], None, bounds_check=LISTS - 1, oob_is_err=False)\
                        .then_inc(listed, 16)

        over_steps(pool, step)
        pool.wait_ge(listed, 32 * (NT + 1))

    @block.tensor
    def _(pe):
        pe.wait_ge(gate_cols, 1)
        for n, (sec, _) in enumerate(GATES):
            for cond in range(2):
                m = 2 * n + cond
                dst = (oT_ps, h2T_ps)[m % 2]
                if m >= 2:
                    pe.wait_ge(gate_out, m - 1)
                for c in range(NC):
                    col = a2col[:, c, cond:cond + 1] if sec == SC2 else mod[:, sec, c, cond:cond + 1]
                    ins = pe.matmul(dst[:, c, :], col.to_broadcast([P, P]), ident, start=True, stop=True)
                ins.then_inc(gate_ready, 1)
        pe.wait_ge(gate_out, 2 * len(GATES))
        pe.wait_ge(scaled, NC)
        pe.wait_ge(ld, 48)

        def transpose_o(t):
            r = rows_of(t)
            pe.wait_ge(on_ready, t + 1)
            for c in range(NC):
                ins = pe.transpose(oT_ps[:, c, 0:r], on[0:r, c * P:(c + 1) * P], ident[0:r, 0:r])
            ins.then_inc(oT_ready, 1)

        def project(t):
            r = rows_of(t)
            pe.wait_ge(oT_out, t + 1)
            pe.wait_ge(y_used, t)
            for n in range(2):
                for c in range(NC):
                    ins = pe.matmul(y_ps[0:r, 512 * n:512 * n + 512], oT[:, c, 0:r], w_out[:, c, 512 * n:512 * n + 512],
                                    start=(c == 0), stop=(c == NC - 1))
            ins.then_inc(y_ready, 1)

        def transpose_h(t):
            r = rows_of(t)
            pe.wait_ge(h2_ready, t + 1)
            for c in range(NC):
                ins = pe.transpose(h2T_ps[:, c, 0:r], h2[0:r, c * P:(c + 1) * P], ident[0:r, 0:r])
            ins.then_inc(h2T_ready, 1)

        def route(t):
            r = rows_of(t)
            pe.wait_ge(h2T_out, t + 1)
            pe.wait_ge(lg_used, t)
            for c in range(NC):
                ins = pe.matmul(lg_ps[0:r, 0:NR], h2T[:, c, 0:r], w_r[:, c, :], start=(c == 0), stop=(c == NC - 1))
            ins.then_inc(lg_ready, 1)

        def positions(t):
            r = rows_of(t)
            pe.wait_ge(picked_done, t + 1)
            pe.wait_ge(slots_done, t)
            pe.matmul(pos_ps[0:r, 0:NE], consts[0:r, K_BEFORE:K_BEFORE + r], picked[0:r, :], start=True, stop=False)
            pe.matmul(pos_ps[0:r, 0:NE], ones[:, 0:r], before[:, :], start=False, stop=True).then_inc(pos_ready, 1)

        def step(n):
            if live(n):
                transpose_h(n)
            if live(n + 2):
                transpose_o(n + 2)
            if live(n):
                route(n)
            if live(n + 2):
                project(n + 2)
            if live(n):
                positions(n)

        over_steps(pe, step)
        pe.wait_ge(slots_done, NT + 1)
        pe.matmul(pos_ps[:, 64:64 + NE], ones, before[:, :], start=True, stop=True).then_inc(cnt_ready, 1)

    @block.scalar
    def _(act):
        for m in range(2 * len(GATES)):
            _, dst = GATES[m // 2]
            src = (oT_ps, h2T_ps)[m % 2]
            act.wait_ge(gate_ready, m + 1)
            act.activation(dst[:, m % 2, :], src[:, :, :].rearrange("p c n -> p (c n)"), ACT.Copy).then_inc(gate_out, 1)

        def step(n):
            if live(n):
                r = rows_of(n)
                act.wait_ge(h2T_ready, n + 1)
                act.activation(h2T[:, :, 0:r], h2T_ps[:, :, 0:r], ACT.Copy).then_inc(h2T_out, 1)
            if live(n + 2):
                r = rows_of(n + 2)
                act.wait_ge(oT_ready, n + 3)
                act.activation(oT[:, :, 0:r], oT_ps[:, :, 0:r], ACT.Copy).then_inc(oT_out, 1)
            if live(n + 3):
                t, r = n + 3, rows_of(n + 3)
                act.wait_ge(hms_done, t)
                act.activation(osq[0:r, :], tile_rows(t, r), ACT.Square).then_inc(osq_done, 1)
            if live(n + 1):
                t, r = n + 1, rows_of(n + 1)
                act.wait_ge(x1_done, t + 1)
                act.wait_ge(rstd_done, t)
                act.activation(xsq[0:r, :], tile_rows(t, r), ACT.Square, accum_out=ms[0:r, :]).then_inc(xsq_done, 1)
            if live(n):
                r = rows_of(n)
                act.wait_ge(dg_done, n + 1)
                act.activation(eg[0:r, :], dg[0:r, :], ACT.Exp, accum_out=gsum[0:r, :]).then_inc(eg_done, 1)
                act.wait_ge(dv_done, n + 1)
                act.activation(ev[0:r, :], dv[0:r, :], ACT.Exp).then_inc(ev_done, 1)

        over_steps(act, step)

    @block.vector
    def _(dve):
        dve.scalar_tensor_tensor(a2col[:, :, :], mod[:, SC2, :, :], 1.0, rep(vecs[:, V_NFFN:V_NFFN + 8], 2, 2),
                                 ALU.add, ALU.mult).then_inc(gate_cols, 1)
        dve.wait_ge(ld, 48)
        for c in range(NC):
            dve.tensor_scalar(w_out[:, c, :], w_out[:, c, :], vecs[:, V_ONORM + c:V_ONORM + c + 1], None, ALU.mult)\
               .then_inc(scaled, 1)
        dve.tensor_copy(tok[:, :, :], consts[:, K_TOK:K_TOK + 4].rearrange("p (a b) -> p a b", a=2)).then_inc(w_own, 1)
        dve.wait_ge(w_own, 1)
        dve.wait_ge(half_set, 1)
        dve.wait_ge(zeroed, 2)
        dve.wait_ge(gate_out, 2 * len(GATES))

        def gated(t):
            r = rows_of(t)
            dve.wait_ge(y_ready, t + 1)
            dve.wait_ge(x1_done, t)
            dve.tensor_tensor(y[0:r, :], y_ps[0:r, :], g1[0:r, cond_of(t), :], ALU.mult).then_inc(y_used, 1)

        def head_sums(t):
            r = rows_of(t)
            dve.wait_ge(osq_done, t + 1)
            dve.tensor_reduce(hs[0:r, :], osq[0:r, :].rearrange("p (h n) -> p h n", n=HD), AX.X, ALU.add)\
               .then_inc(w_own, 1)
            dve.wait_ge(w_own, t + 2)
            dve.tensor_scalar(hs[0:r, :], hs[0:r, :], 1.0 / HD, EPS, ALU.mult, ALU.add).then_inc(hms_done, 1)

        def mean_square(t):
            r = rows_of(t)
            dve.wait_ge(xsq_done, t + 1)
            dve.tensor_scalar(ms[0:r, :], ms[0:r, :], 1.0 / D, EPS, ALU.mult, ALU.add).then_inc(ms_done, 1)

        def scale_h2(t):
            r = rows_of(t)
            dve.wait_ge(rstd_done, t + 1)
            dve.wait_ge(h2_stored, 16 * t)
            dve.wait_ge(h2T_ready, t)
            dve.scalar_tensor_tensor(h2[0:r, :], tile_rows(t, r), rstd[0:r, 0:1], a2[0:r, cond_of(t), :],
                                     ALU.mult, ALU.mult).then_inc(scaled_h2, 1)

        def normalise_o(t):
            r = rows_of(t)
            dve.wait_ge(hr_done, t + 1)
            dve.wait_ge(oT_ready, t)
            dve.tensor_tensor(on[0:r, :].rearrange("p (h n) -> p h n", n=HD),
                              tile_rows(t, r).rearrange("p (h n) -> p h n", n=HD), rep(hr[0:r, :], 2, HD),
                              ALU.mult).then_inc(on_ready, 1)

        PICK = 20

        def pick(t):
            r = rows_of(t)
            own = Own(dve, own_dve, PICK * t)
            dve.wait_ge(lg_ready, t + 1)
            dve.tensor_tensor(lg[0:r, :], lg_ps[0:r, 0:NR], b_r[0:r, :], ALU.add).then_inc(lg_used, 1)
            dve.wait_ge(lg_used, t + 1)
            own(dve.tensor_reduce(gmax[0:r, :], lg[0:r, 0:NG], AX.X, ALU.max))
            dve.tensor_scalar(dg[0:r, :], lg[0:r, 0:NG], gmax[0:r, 0:1], None, ALU.subtract).then_inc(dg_done, 1)
            dve.wait_ge(dg_done, t + 1)
            own(dve.scalar_tensor_tensor(pri_g[0:r, :], dg[0:r, :], 0.0, consts[0:r, K_PRIG:K_PRIG + NG],
                                         ALU.is_equal, ALU.mult))
            own(dve.tensor_reduce(best_g[0:r, :], pri_g[0:r, :], AX.X, ALU.max))
            own(dve.tensor_scalar(pen[0:r, :], pri_g[0:r, :], best_g[0:r, 0:1], -1.0, ALU.is_equal, ALU.add))
            own(dve.scalar_tensor_tensor(em[0:r, :].rearrange("p (g e) -> p g e", g=NG), rep(pen[0:r, :], 2, EPG), 1e30,
                                         lg[0:r, NG:NR].rearrange("p (g e) -> p g e", g=NG), ALU.mult, ALU.add),
                wait=False)
            alone(dve, own_dve, PICK * t + own.n, begun)
            own(dve.max(top[0:r, :], em[0:r, :]))
            dve.tensor_scalar(dv[0:r, :], top[0:r, 1:2], top[0:r, 0:1], None, ALU.subtract).then_inc(dv_done, 1)
            src = em
            for n in range(2):
                own(dve.scalar_tensor_tensor(pri_e[0:r, :], src[0:r, :], top[0:r, n:n + 1],
                                             consts[0:r, K_PRIE:K_PRIE + NE], ALU.is_equal, ALU.mult))
                own(dve.tensor_reduce(best_e[0:r, :], pri_e[0:r, :], AX.X, ALU.max))
                own(dve.tensor_scalar(oh[0:r, n, :], pri_e[0:r, :], best_e[0:r, 0:1], None, ALU.is_equal))
                if n == 0:
                    own(dve.scalar_tensor_tensor(em2[0:r, :], oh[0:r, 0, :], -3e38, em[0:r, :], ALU.mult, ALU.add))
                    src = em2
            dve.tensor_tensor(picked[0:r, :], oh[0:r, 0, :], oh[0:r, 1, :], ALU.add).then_inc(picked_done, 1)
            dve.wait_ge(listed, 32 * t)
            dve.wait_ge(eg_done, t + 1)
            dve.wait_ge(ev_done, t + 1)
            weight = entry[0:r, :, 2].bitcast(F32)
            own(dve.tensor_scalar(den[0:r, :], ev[0:r, :], 1.0, gsum[0:r, 0:1], ALU.add, ALU.mult))
            own(dve.reciprocal(weight[:, 0:1], den[0:r, :]))
            dve.tensor_tensor(weight[:, 1:2], weight[:, 0:1], ev[0:r, :], ALU.mult)
            own(dve.tensor_copy(entry[0:r, :, 0:2], tok[0:r, :, :]))
            own(dve.tensor_scalar(tok[:, :, :], tok[:, :, :], float(P), None, ALU.add))
            dve.wait_ge(pos_ready, t + 1)
            own(dve.tensor_tensor(slot[0:r, :], pos_ps[0:r, 0:NE], consts[0:r, K_BASE:K_BASE + NE], ALU.add))
            for n in range(2):
                own(dve.tensor_tensor_reduce(junk[0:r, :], slot[0:r, :], oh[0:r, n, :], 1.0, 0.0, ALU.mult, ALU.add,
                                             slot_f[0:r, n:n + 1]))
            assert own.n == PICK, own.n
            dve.tensor_tensor(before[0:r, :], before[0:r, :], picked[0:r, :], ALU.add)
            dve.tensor_copy(slot_i[0:r, :], slot_f[0:r, :]).then_inc(slots_done, 1)

        def step(n):
            if live(n + 1):
                gated(n + 1)
            if live(n + 3):
                head_sums(n + 3)
            if live(n + 1):
                mean_square(n + 1)
                scale_h2(n + 1)
            if live(n + 3):
                normalise_o(n + 3)
            if live(n):
                pick(n)

        over_steps(dve, step)
        dve.wait_ge(slots_done, NT + 1)

        own = Own(dve, g_own)
        dve.wait_ge(cnt_ready, 1)
        own(dve.tensor_copy(cnt[:, :], pos_ps[0:1, 64:64 + NE]))
        own(dve.tensor_tensor(need[:, :, :], rep(cnt[:, :], 2, 9), rep(consts[0:1, K_THR:K_THR + 9], 1, NE), ALU.is_gt))
        own(dve.tensor_reduce(nb[:, :], need[:, :, :], AX.X, ALU.add))
        own(dve.tensor_tensor_scan(cb[:, :], ones[0:1, 0:NE], nb[:, :], 0.0, ALU.mult, ALU.add))
        blk = consts[0:1, K_BLK:K_BLK + TABLE]
        own(dve.tensor_tensor(done[:, :, :], rep(cb[:, :], 1, TABLE), rep(blk, 2, NE), ALU.is_le))
        own(dve.tensor_reduce(eb[:, :], done[:, :, :], AX.X, ALU.add))
        own(dve.tensor_tensor(done[:, :, :], done[:, :, :], rep(nb[:, :], 1, TABLE), ALU.mult))
        own(dve.tensor_reduce(bb[:, :], done[:, :, :], AX.X, ALU.add))
        own(dve.tensor_tensor(bb[:, :], blk, bb[:, :], ALU.subtract))
        own(dve.tensor_scalar(bb[:, :], bb[:, :], float(P), None, ALU.mult))
        own(dve.scalar_tensor_tensor(start[:, :], eb[:, :], float(REGION), bb[:, :], ALU.mult, ALU.add))
        own(dve.tensor_scalar(table[:, 2 + TABLE:2 + 2 * TABLE], start[:, :], float(DUMMY), None, ALU.min))
        own(dve.tensor_scalar(table[:, 2:2 + TABLE], eb[:, :], float(NE - 1), None, ALU.min))
        even = consts[0:1, K_BLK:K_BLK + NBLK].rearrange("p (n two) -> p n two", two=2)[:, :, 0]
        own(dve.tensor_scalar(pairs[:, :], even, cb[:, NE - 1:NE], None, ALU.is_lt))
        own(dve.tensor_reduce(steps[:, :], pairs[:, :], AX.X, ALU.add))
        own(dve.tensor_copy(table[:, 0:1], steps[:, :]))


def experts(nc, s, a, k):
    consts, table, begun = k["consts"], k["table"], k["begun"]
    ident = consts[:, K_ID:K_ID + P]
    w_gu = [s.sb(f"w_gu{j}", [P, NC, 2 * DE]) for j in range(2)]
    w_dn = [s.sb(f"w_dn{j}", [P, 2, D]) for j in range(2)]
    g_list = [s.sb(f"gather_list{j}", [P, 4], I32) for j in range(2)]
    s_list = [s.sb(f"scatter_list{j}", [P, 4], I32) for j in range(2)]
    x = [s.sb(f"x{j}", [P, D]) for j in range(2)]
    xT = s.sb("xT", [P, NC, P])
    gate = s.sb("gate", [P, DE])
    hidden = s.sb("hidden", [P, DE])
    hT = s.sb("hT", [P, 2, P])
    y = [s.sb(f"y{j}", [P, D]) for j in range(2)]
    xT_ps = s.ps("xT", [P, NC, P])
    gu_ps = [s.ps(f"gu{j}", [P, 512]) for j in range(2)]
    hT_ps = s.ps("hT", [P, 512])
    y_ps = s.ps("y", [P, D])

    gu_ld, dn_ld, gl_ld, sl_ld, gathered, scattered = (
        [s.sem(f"{n}{j}") for j in range(2)] for n in ("gu_ld", "dn_ld", "gl_ld", "sl_ld", "gathered", "scattered"))
    cleared, xT_ready, xT_out_act, xT_out_dve = (s.sem(n) for n in ("cleared", "xT_ready", "xT_out_act", "xT_out_dve"))
    gu_ready, gate_done, hidden_done, hT_ready, hT_out = (
        s.sem(n) for n in ("gu_ready", "gate_done", "hidden_done", "hT_ready", "hT_out"))
    y_ready, y_out_act, y_out_dve = s.sem("y_ready"), s.sem("y_out_act"), s.sem("y_out_dve")
    block = s.ctx.enter_context(nc.Block())

    def steps(eng, body):
        n = eng.value_load(table[0:1, 0:1], min_val=1, max_val=NBLK // 2)
        with eng.Fori(0, NBLK // 2) as i:
            with eng.If(i < n):
                for j in range(2):
                    body(i, j)
            with eng.Else():
                eng.nop()
        return n

    @block.sync
    def _(sp):
        def expert(b):
            return sp.value_load(table[0:1, bass.ds(b + 2, 1)], min_val=0, max_val=NE - 1)

        def start(b):
            return sp.value_load(table[0:1, bass.ds(b + (2 + TABLE), 1)], min_val=0, max_val=DUMMY)

        def gate_up(ex, j):
            sp.dma_start(w_gu[j][:, :, :], a["w_gu"][bass.ds(ex, 1)].rearrange("a p k n -> p (a k) n")).then_inc(gu_ld[j], 16)

        def down(ex, j):
            sp.dma_start(w_dn[j][:, :, :], a["w_dn"][bass.ds(ex, 1)].rearrange("a p k n -> p (a k) n")).then_inc(dn_ld[j], 16)

        def entries(first, dst, sem):
            sp.dma_start(dst[:, :], k["lists"][bass.ds(first, P), :]).then_inc(sem, 16)

        for j in range(2):
            entries(start(j), g_list[j], gl_ld[j])
            gate_up(expert(j), j)
        for j in range(2):
            first = start(2 + j)
            sp.wait_ge(gathered[j], 16)
            entries(first, g_list[j], gl_ld[j])
        down(expert(0), 0)
        entries(start(0), s_list[0], sl_ld[0])

        def body(i, j):
            b = 2 * i + j
            e2, e1, s4, s1 = expert(b + 2), expert(b + 1), start(b + 4), start(b + 1)
            alone(sp, gu_ready, b + 1, begun)
            gate_up(e2, j)
            alone(sp, y_ready, b, begun)
            down(e1, 1 - j)
            q, n = ahead(i, j, 2)
            alone(sp, gathered[q], 16 * (n + 1), begun)
            entries(s4, g_list[j], gl_ld[j])
            alone(sp, scattered[1 - j], 16 * (i + j), begun)
            entries(s1, s_list[1 - j], sl_ld[1 - j])

        n = steps(sp, body)
        alone(sp, gu_ld[0], 16 * n + 16, begun)
        alone(sp, gu_ld[1], 16 * n + 16, begun)
        alone(sp, dn_ld[0], 16 * n + 16, begun)
        alone(sp, dn_ld[1], 16 * n, begun)
        alone(sp, gl_ld[0], 16 * n + 32, begun)
        alone(sp, gl_ld[1], 16 * n + 32, begun)
        alone(sp, sl_ld[0], 16 * n + 16, begun)
        alone(sp, sl_ld[1], 16 * n, begun)

    @block.gpsimd
    def _(pool):
        for j in range(2):
            pool.memset(x[j][:, :], 0.0).then_inc(cleared, 1)
        pool.wait_ge(cleared, 2)

        def gather(j, nth):
            alone(pool, gl_ld[j], 16 * (nth + 1), begun)
            pool.indirect_dma_start(x[j][:, :], None, k["h2"], bass.IndirectOffsetOnAxis(ap=g_list[j][:, 0:1], axis=0),
                                    bounds_check=TOK - 1, oob_is_err=False).then_inc(gathered[j], 16)

        gather(0, 0)
        gather(1, 0)
        pool.wait_ge(xT_ready, 1)
        gather(0, 1)

        def body(i, j):
            b = 2 * i + j
            pool.wait_ge(xT_ready, b + 2)
            gather(*ahead(i, j, 3))
            pool.wait_ge(sl_ld[j], 16 * (i + 1))
            pool.wait_ge(y_out_act, b + 1)
            alone(pool, y_out_dve, b + 1, begun)
            pool.indirect_dma_start(k["yrows"], bass.IndirectOffsetOnAxis(ap=s_list[j][:, 1:2], axis=0), y[j][:, :], None,
                                    bounds_check=2 * TOK - 1, oob_is_err=False).then_inc(scattered[j], 16)

        n = steps(pool, body)
        alone(pool, scattered[0], 16 * n, begun)
        alone(pool, scattered[1], 16 * n, begun)
        alone(pool, gathered[0], 16 * n + 32, begun)
        alone(pool, gathered[1], 16 * n + 16, begun)

    @block.tensor
    def _(pe):
        def transpose_x(j, nth):
            pe.wait_ge(gathered[j], 16 * (nth + 1))
            for c in range(NC):
                ins = pe.transpose(xT_ps[:, c, :], x[j][:, c * P:(c + 1) * P], ident)
            ins.then_inc(xT_ready, 1)

        def gate_up(j, nth):
            b = 2 * nth + j
            pe.wait_ge(gu_ld[j], 16 * (nth + 1))
            pe.wait_ge(xT_out_act, b + 1)
            pe.wait_ge(xT_out_dve, b + 1)
            for c in range(NC):
                ins = pe.matmul(gu_ps[j][:, :], xT[:, c, :], w_gu[j][:, c, :], start=(c == 0), stop=(c == NC - 1))
            ins.then_inc(gu_ready, 1)

        def transpose_hidden(b):
            pe.wait_ge(hidden_done, b + 1)
            for c in range(2):
                ins = pe.transpose(hT_ps[:, c * P:(c + 1) * P], hidden[:, c * P:(c + 1) * P], ident)
            ins.then_inc(hT_ready, 1)

        def down(j, nth):
            b = 2 * nth + j
            pe.wait_ge(dn_ld[j], 16 * (nth + 1))
            pe.wait_ge(hT_out, b + 1)
            pe.wait_ge(y_out_act, b)
            pe.wait_ge(y_out_dve, b)
            for n in range(2):
                for c in range(2):
                    ins = pe.matmul(y_ps[:, 512 * n:512 * n + 512], hT[:, c, :], w_dn[j][:, c, 512 * n:512 * n + 512],
                                    start=(c == 0), stop=(c == 1))
            ins.then_inc(y_ready, 1)

        transpose_x(0, 0)
        gate_up(0, 0)
        transpose_x(1, 0)

        def body(i, j):
            gate_up(*ahead(i, j, 1))
            transpose_hidden(2 * i + j)
            transpose_x(*ahead(i, j, 2))
            down(j, i)

        steps(pe, body)

    @block.scalar
    def _(act):
        def move_xT(b):
            act.wait_ge(xT_ready, b + 1)
            act.activation(xT[:, 0:4, :], xT_ps[:, 0:4, :], ACT.Copy).then_inc(xT_out_act, 1)

        def silu(b, j):
            act.wait_ge(gu_ready, b + 1)
            act.wait_ge(hidden_done, b)
            act.activation(gate[:, :], gu_ps[j][:, 0:DE], ACT.Silu).then_inc(gate_done, 1)

        move_xT(0)
        silu(0, 0)
        move_xT(1)

        def body(i, j):
            b = 2 * i + j
            move_xT(b + 2)
            act.wait_ge(y_ready, b + 1)
            act.wait_ge(sl_ld[j], 16 * (i + 1))
            act.activation(y[j][:, 0:512], y_ps[:, 0:512], ACT.Copy, scale=s_list[j][:, 2:3].bitcast(F32))\
               .then_inc(y_out_act, 1)
            silu(b + 1, 1 - j)

        steps(act, body)

    @block.vector
    def _(dve):
        def move_xT(b):
            dve.wait_ge(xT_ready, b + 1)
            dve.tensor_copy(xT[:, 4:8, :], xT_ps[:, 4:8, :]).then_inc(xT_out_dve, 1)

        def gate_times_up(b, j):
            dve.wait_ge(gate_done, b + 1)
            dve.wait_ge(hT_ready, b)
            dve.tensor_tensor(hidden[:, :], gate[:, :], gu_ps[j][:, DE:2 * DE], ALU.mult).then_inc(hidden_done, 1)

        move_xT(0)
        gate_times_up(0, 0)
        move_xT(1)

        def body(i, j):
            b = 2 * i + j
            dve.wait_ge(hT_ready, b + 1)
            dve.tensor_copy(hT[:, :, :], hT_ps[:, 0:2 * P].rearrange("p (c n) -> p c n", c=2)).then_inc(hT_out, 1)
            move_xT(b + 2)
            dve.wait_ge(y_ready, b + 1)
            dve.wait_ge(sl_ld[j], 16 * (i + 1))
            dve.tensor_scalar(y[j][:, 512:1024], y_ps[:, 512:1024], s_list[j][:, 2:3].bitcast(F32), None, ALU.mult)\
               .then_inc(y_out_dve, 1)
            gate_times_up(b + 1, 1 - j)

        steps(dve, body)


def finish(nc, s, a, o, k, g2):
    rows_all = k["rows_all"]
    ya = [s.sb(f"ya{j}", [P, D]) for j in range(2)]
    yb = [s.sb(f"yb{j}", [P, D]) for j in range(2)]
    squares = s.sb("squares", [P, D])
    ms, rstd = s.sb("ms", [P, 2]), s.sb("rstd", [P, 2])
    half = s.sb("minus_half", [P, 1])
    norm = s.sb("norm", [P, D])
    norm_ld, half_set = s.sem("norm_ld"), s.sem("half_set")
    y_ld = [s.sem(f"y_ld{j}") for j in range(2)]
    stored = [s.sem(f"stored{j}") for j in range(2)]
    summed, gated, x_done, sq_done, ms_done, rstd_done, out_ready = (
        s.sem(n) for n in ("summed", "gated", "x_done", "sq_done", "ms_done", "rstd_done", "out_ready"))
    block = s.ctx.enter_context(nc.Block())

    def over_tiles(eng, step):
        with eng.Fori(0, NT // 2) as i:
            for j in range(2):
                step(2 * i + j, j, i)
        step(NT, 0, NT // 2)

    def tile_rows(t, r):
        return rows_all[0:r, bass.ds(t, 1), :].rearrange("p a n -> p (a n)")

    @block.sync
    def _(sp):
        sp.dma_start(norm[:, :], rep(a["norm_final"], 0, P)).then_inc(norm_ld, 16)

        def load(t, j):
            r = rows_of(t)
            sp.dma_start(ya[j][0:r, :], k["yrows"][bass.ds(t * P, r), :]).then_inc(y_ld[j], 16)
            sp.dma_start(yb[j][0:r, :], k["yrows"][bass.ds(t * P + TOK, r), :]).then_inc(y_ld[j], 16)

        def store(t, j):
            r = rows_of(t)
            sp.wait_ge(out_ready, t + 1)
            dst = o["y_sample"] if r == DEC else o["y_prompt"][bass.ds(t * P, P), :]
            sp.dma_start(dst, ya[j][0:r, :]).then_inc(stored[j], 16)

        load(0, 0)
        load(1, 1)
        with sp.Fori(0, NT // 2 - 1) as i:
            for j in range(2):
                store(2 * i + j, j)
                sp.wait_ge(stored[j], 16 * (i + 1))
                load(2 * i + j + 2, j)
        store(NT - 2, 0)
        sp.wait_ge(stored[0], 16 * (NT // 2))
        load(NT, 0)
        store(NT - 1, 1)
        store(NT, 0)
        sp.wait_ge(stored[0], 16 * (NT // 2 + 1))
        sp.wait_ge(stored[1], 16 * (NT // 2))

    @block.gpsimd
    def _(pool):
        pool.memset(half[:, :], -0.5).then_inc(half_set, 1)
        pool.wait_ge(half_set, 1)

        def step(t, j, i):
            r = rows_of(t)
            pool.wait_ge(y_ld[j], 32 * (i + 1))
            pool.tensor_tensor(ya[j][0:r, :], ya[j][0:r, :], yb[j][0:r, :], ALU.add).then_inc(summed, 1)
            pool.wait_ge(ms_done, t + 1)
            pool.tensor_tensor(rstd[0:r, j:j + 1], ms[0:r, j:j + 1], half[0:r, :], ALU.pow).then_inc(rstd_done, 1)

        over_tiles(pool, step)

    @block.scalar
    def _(act):
        def step(t, j, i):
            r = rows_of(t)
            act.wait_ge(x_done, t + 1)
            act.activation(squares[0:r, :], ya[j][0:r, :], ACT.Square, accum_out=ms[0:r, j:j + 1]).then_inc(sq_done, 1)

        over_tiles(act, step)

    @block.vector
    def _(dve):
        dve.wait_ge(norm_ld, 16)

        def step(t, j, i):
            r = rows_of(t)
            dve.wait_ge(summed, t + 1)
            dve.tensor_tensor(ya[j][0:r, :], ya[j][0:r, :], g2[0:r, cond_of(t), :], ALU.mult).then_inc(gated, 1)
            dve.wait_ge(gated, t + 1)
            dve.tensor_tensor(ya[j][0:r, :], ya[j][0:r, :], tile_rows(t, r), ALU.add).then_inc(x_done, 1)
            dve.wait_ge(sq_done, t + 1)
            dve.tensor_scalar(ms[0:r, j:j + 1], ms[0:r, j:j + 1], 1.0 / D, EPS, ALU.mult, ALU.add).then_inc(ms_done, 1)
            dve.wait_ge(rstd_done, t + 1)
            dve.scalar_tensor_tensor(ya[j][0:r, :], ya[j][0:r, :], rstd[0:r, j:j + 1], norm[0:r, :],
                                     ALU.mult, ALU.mult).then_inc(out_ready, 1)

        over_tiles(dve, step)


def constants():
    import numpy as np
    c = np.zeros((P, K_END), np.float32)
    i, j = np.arange(P)[:, None], np.arange(P)[None, :]
    c[:, K_ID:K_ID + P] = i == j
    c[:, K_CAUSAL:K_CAUSAL + P] = np.where(j <= i, 0.0, NEG)
    c[:, K_BEFORE:K_BEFORE + P] = i < j
    c[:, K_ONES:K_ONES + P] = 1.0
    c[:, K_PRIG:K_PRIG + NG] = NG - np.arange(NG)
    c[:, K_PRIE:K_PRIE + NE] = NE - np.arange(NE)
    c[:, K_BASE:K_BASE + NE] = REGION * np.arange(NE)
    c[:, K_THR:K_THR + 9] = P * np.arange(9)
    c[:, K_BLK:K_BLK + TABLE] = np.arange(TABLE)
    c[:, K_TOK:K_TOK + 4] = np.arange(P)[:, None] + np.array([0, 0, 0, TOK])
    return c


def kernel(**inputs):
    import numpy as np
    import concourse.bacc as bacc
    from concourse.bass_utils import run_bass_kernel_spmd

    x = {name: np.asarray(v) for name, v in inputs.items()}

    def by_partition(v):
        return v.reshape(-1, NC, P).transpose(2, 0, 1).reshape(P, -1)

    def rows(m):
        return m.reshape(-1, P, m.shape[-1]).transpose(1, 0, 2)

    w_in = x["w_in"][0]
    wa, wb = w_in[:, 0:1536], w_in[:, 1544:3080]
    qkv = np.stack([np.stack([np.concatenate([w[:, 512 * n + P * i:512 * n + P * (i + 1)] for n in range(3)], 1)
                              for i in range(PAIRS)]) for w in (wa, wb)])
    c2 = np.stack([x["c_prompt"][0], x["c_sample"][0]], 1)
    vecs = np.concatenate([
        rows(c2).reshape(P, 16), by_partition(x["b_ada"][0]), by_partition(x["norm_mix"][0]),
        by_partition(np.concatenate([x["onorm_a"][0], x["onorm_b"][0]])), by_partition(x["norm_ffn"][0])], 1)
    m = np.clip(BAND - P + np.arange(P)[:, None] - np.arange(BAND)[None, :], -128, 128) + 128
    arrays = {
        "x_prompt": x["x_prompt"], "x_sample": x["x_sample"],
        "consts": constants(), "vecs": vecs,
        "w_ada": x["w_ada"][0].reshape(NC, P, 6, D).transpose(2, 1, 0, 3),
        "w_qkv": qkv.reshape(2, PAIRS, NC, P, 3 * P).transpose(0, 1, 3, 2, 4),
        "w_f": rows(w_in[:, 1536:1544]), "b_f": x["b_fgate"].reshape(8, 1),
        "cache_logf": x["cache_logf_a"][0, 0].T,
        "rel": x["rel_bias"][0][:, m].transpose(1, 0, 2),
        "w_out": rows(x["w_out"][0]),
        "w_r": rows(np.concatenate([x["w_router_group"][0], x["w_router_expert"][0]], 1)),
        "b_r": np.concatenate([x["b_router_group"][0], x["b_router_expert"][0]]),
        "w_gu": np.concatenate([x["w_gate"][0], x["w_up"][0]], 2).reshape(NE, NC, P, 2 * DE).transpose(0, 2, 1, 3),
        "w_dn": x["w_down"][0].reshape(NE, 2, P, D).transpose(0, 2, 1, 3),
        "norm_final": x["norm_final"],
    }
    for name in ("k_a", "v_a", "k_b", "v_b"):
        arrays["cache_" + name] = x["cache_" + name][0, 0].reshape(PAST, 512)
    lb = min(512, SEQ)
    outs = {"y_prompt": (SEQ, D), "y_sample": (DEC, D),
            "k_a_prompt": (SEQ, 512), "v_a_prompt": (SEQ, 512), "logf_prompt": (SEQ, 8),
            "k_b_prompt": (lb, 512), "v_b_prompt": (lb, 512),
            "k_a_sample": (DEC, 512), "v_a_sample": (DEC, 512), "logf_sample": (DEC, 8),
            "k_b_sample": (DEC, 512), "v_b_sample": (DEC, 512)}

    nc = bacc.Bacc("TRN2", target_bir_lowering=False, num_devices=1)
    arrays = {name: np.ascontiguousarray(v) for name, v in arrays.items()}
    a = {name: nc.dram_tensor(f"in_{name}", v.shape, mybir.dt.from_np(v.dtype), kind="ExternalInput").ap()
         for name, v in arrays.items()}
    o = {name: nc.dram_tensor(f"out_{name}", shape, F32, kind="ExternalOutput").ap() for name, shape in outs.items()}
    build(nc, a, o)
    r = run_bass_kernel_spmd(nc, [{f"in_{name}": v for name, v in arrays.items()}], core_ids=[0])
    got = {name: r.results[0][f"out_{name}"] for name in outs}

    def heads(name):
        v = got[name]
        return v.reshape(1, 1, v.shape[0], 8, HD)

    return (got["y_prompt"][None], got["y_sample"][None],
            heads("k_a_prompt"), heads("v_a_prompt"), got["logf_prompt"][None, None],
            heads("k_b_prompt"), heads("v_b_prompt"),
            heads("k_a_sample"), heads("v_a_sample"), got["logf_sample"][None, None],
            heads("k_b_sample"), heads("v_b_sample"))
```

```python
from contextlib import ExitStack

import concourse.bass as bass
from concourse import mybir

F32 = mybir.dt.float32
F32R = mybir.dt.float32r
I32 = mybir.dt.int32
ALU = mybir.AluOpType
ACT = mybir.ActivationFunctionType
AX = mybir.AxisListType

P = 128
D = 1024
NC = D // P
SEQ, DEC, PAST = 1024, 64, 128
NT = SEQ // P
TOK = SEQ + DEC
HD = 64
PAIRS = 4
UNITS = 2 * (NT + 1)
KEYS = SEQ + PAST + DEC
BAND_TILES = 5
BAND = BAND_TILES * P
NG, EPG, NE = 4, 8, 32
NR = NG + NE
DE = 256
NBLK = (2 * TOK + NE * (P - 1)) // P
REGION = 9 * P
DUMMY = NE * REGION
LISTS = DUMMY + P
TABLE = NBLK + 4
SCALE = HD ** -0.5
EPS = 1e-6
NEG = -1e30 / SCALE
FAR = 1 << 20
BIG = 1e38

V_C, V_BADA, V_NMIX, V_ONORM, V_NFFN, V_END = 0, 16, 64, 72, 80, 88
K_ID, K_CAUSAL, K_BEFORE, K_ONES = 0, P, 2 * P, 3 * P
K_PRIG = 4 * P
K_PRIE = K_PRIG + NG
K_BASE = K_PRIE + NE
K_THR = K_BASE + NE
K_BLK = K_THR + 9
K_TOK = K_BLK + TABLE
K_END = K_TOK + 4
SH1, SC1, G1, SH2, SC2, G2 = range(6)
HALVES = 12


def rows_of(t):
    return DEC if isinstance(t, int) and t == NT else P


def cond_of(t):
    return 1 if isinstance(t, int) and t == NT else 0


def alone(eng, sem, value, begun):
    eng.wait_ge(sem, value)
    eng.sem_inc(begun, 1)


def ahead(i, j, m):
    return (j + m) % 2, i + (j + m) // 2


def rep(ap, dim, n):
    a = ap.unsqueeze(dim)
    shape = list(a.shape)
    shape[dim] = n
    return a.to_broadcast(shape)


class Scope:

    def __init__(self, nc, ctx, name):
        self.nc, self.ctx, self.name = nc, ctx, name

    def sb(self, name, shape, dt=F32):
        return self.ctx.enter_context(self.nc.sbuf_tensor(f"{self.name}_{name}_sb", shape, dt))

    def ps(self, name, shape, dt=F32):
        return self.ctx.enter_context(self.nc.psum_tensor(f"{self.name}_{name}_ps", shape, dt))

    def sem(self, name):
        return self.ctx.enter_context(self.nc.semaphore(f"{self.name}_{name}_sem"))


class Own:

    def __init__(self, eng, sem, base=0):
        self.eng, self.sem, self.base, self.n = eng, sem, base, 0

    def __call__(self, ins, wait=True):
        ins.then_inc(self.sem, 1)
        self.n += 1
        if wait:
            self.eng.wait_ge(self.sem, self.base + self.n)


def build(nc, a, o):
    with ExitStack() as ctx:
        keep = Scope(nc, ctx, "keep")
        consts = keep.sb("consts", [P, K_END])
        vecs = keep.sb("vecs", [P, V_END])
        mod = keep.sb("mod", [P, 6, NC, 2])
        sc = keep.sb("silu_c", [P, NC, 2])
        rows_all = keep.sb("rows_all", [P, NT + 1, D])
        table = keep.sb("table", [1, 2 + 2 * TABLE], I32)
        begun = keep.sem("begun")
        k = dict(
            begun=begun,
            consts=consts, vecs=vecs, mod=mod, sc=sc, rows_all=rows_all, table=table,
            forget=nc.dram_tensor("forget_bias", (8, KEYS), F32, kind="Internal").ap(),
            h2=nc.dram_tensor("h2_rows", (TOK, D), F32, kind="Internal").ap(),
            lists=nc.dram_tensor("lists", (LISTS, 4), I32, kind="Internal").ap(),
            yrows=nc.dram_tensor("expert_rows", (2 * TOK, D), F32, kind="Internal").ap(),
        )
        with ExitStack() as attention:
            hT = [attention.enter_context(nc.sbuf_tensor(f"hT_{n}", [P, NC, TOK], F32R)) for n in ("hi", "lo")]
            with ExitStack() as c:
                modulate_in(nc, Scope(nc, c, "in"), a, o, k, hT)
            w_scope = Scope(nc, attention, "w_qkv")
            w = dict(raw=w_scope.sb("raw", [P, NC, 3 * P]), hi=w_scope.sb("hi", [P, NC, 3 * P], F32R),
                     lo=w_scope.sb("lo", [P, NC, 3 * P], F32R))
            k["w_ld"], k["w_split"] = w_scope.sem("ld"), w_scope.sem("split")
            for group in ("fox", "band"):
                with ExitStack() as c:
                    attend(nc, Scope(nc, c, group), group, a, o, k, hT, w)
        with ExitStack() as c:
            g2 = c.enter_context(nc.sbuf_tensor("gate2_rows", [P, 2, D], F32))
            with ExitStack() as c2:
                mix_out(nc, Scope(nc, c2, "mix"), a, o, k, g2)
            with ExitStack() as c2:
                experts(nc, Scope(nc, c2, "moe"), a, k)
            with ExitStack() as c2:
                finish(nc, Scope(nc, c2, "fin"), a, o, k, g2)


def modulation_half(pe, w, sc, out):
    for c in range(NC // 2):
        for kc in range(NC):
            ins = pe.matmul(out[:, 2 * c:2 * c + 2], w[:, kc, c * P:(c + 1) * P], sc[:, kc, :],
                            start=(kc == 0), stop=(kc == NC - 1))
    return ins


def modulate_in(nc, s, a, o, k, hT):
    consts, vecs, mod, sc = k["consts"], k["vecs"], k["mod"], k["sc"]
    h_hi, h_lo = hT
    w_ada = [s.sb(f"w_ada{j}", [P, NC, D // 2]) for j in range(2)]
    x = [s.sb(f"x{j}", [P, D]) for j in range(2)]
    h = [s.sb(f"h{j}", [P, NC, P]) for j in range(2)]
    squares = s.sb("squares", [P, D])
    ssq = s.sb("ssq", [P, 2])
    rstd = s.sb("rstd", [P, 2])
    half = s.sb("minus_half", [P, 1])
    a1 = s.sb("a1", [P, NC, 2])
    w_f = s.sb("w_f", [P, NC, 8])
    w_f_hi, w_f_lo = s.sb("w_f_hi", [P, NC, 8], F32R), s.sb("w_f_lo", [P, NC, 8], F32R)
    b_f = s.sb("b_f", [8, 1])
    z = s.sb("z", [8, TOK])
    e = s.sb("e", [8, TOK])
    logf = s.sb("logf", [8, TOK])
    logf_s = s.sb("logf_s", [8, PAST + DEC])
    cum = s.sb("cum", [8, KEYS])
    logf_rows = s.sb("logf_rows", [P, NT + 1, 8])
    far = s.sb("far", [P, LISTS // P * 4], I32)
    xT_ps = [s.ps(f"xT{j}", [P, NC, P]) for j in range(2)]
    mod_ps = s.ps("mod", [P, 512])
    f_ps = s.ps("f", [8, 3 * 512])

    vec_ld, c_ld, wf_ld = s.sem("vec_ld"), s.sem("c_ld"), s.sem("wf_ld")
    w_ld = [s.sem(f"w_ld{j}") for j in range(2)]
    x_ld = [s.sem(f"x_ld{j}") for j in range(2)]
    silu_done, mod_ready, mod_out = s.sem("silu_done"), s.sem("mod_ready"), s.sem("mod_out")
    a1_done = s.sem("a1_done")
    sq_done, ms_done, rstd_done, xn_done = s.sem("sq_done"), s.sem("ms_done"), s.sem("rstd_done"), s.sem("xn_done")
    xT_ready, xT_out_act, xT_out_dve = s.sem("xT_ready"), s.sem("xT_out_act"), s.sem("xT_out_dve")
    hi_done, lo_done, wf_split = s.sem("hi_done"), s.sem("lo_done"), s.sem("wf_split")
    half_set, far_set = s.sem("half_set"), s.sem("far_set")
    f_ready, z_done, e_done, logf_done = s.sem("f_ready"), s.sem("z_done"), s.sem("e_done"), s.sem("logf_done")
    rows_ready, rows_out, cum_done, stored = s.sem("rows_ready"), s.sem("rows_out"), s.sem("cum_done"), s.sem("stored")
    own_dve, own_act = s.sem("own_dve"), s.sem("own_act")
    xp, xs = a["x_prompt"][0], a["x_sample"][0]
    block = s.ctx.enter_context(nc.Block())

    def over_tiles(eng, step):
        with eng.Fori(0, NT // 2) as i:
            for j in range(2):
                step(2 * i + j, j)
        step(NT, 0)

    @block.sync
    def _(sp):
        sp.dma_start(vecs[:, :], a["vecs"]).then_inc(vec_ld, 16)
        sp.dma_start(consts[:, :], a["consts"]).then_inc(c_ld, 16)

        def load_half(n, j):
            sp.dma_start(w_ada[j][:, :, :], a["w_ada"][bass.ds(n, 1)].rearrange("a p k n -> p (a k) n")).then_inc(w_ld[j], 16)

        for n in range(4):
            if n >= 2:
                sp.wait_ge(mod_ready, n - 1)
            load_half(n, n % 2)
        sp.dma_start(w_f[:, :, :], a["w_f"]).then_inc(wf_ld, 16)
        sp.dma_start(b_f[:, :], a["b_f"]).then_inc(wf_ld, 16)
        sp.dma_start(logf_s[:, 0:PAST], a["cache_logf"]).then_inc(wf_ld, 16)
        with sp.Fori(2, HALVES // 2) as i:
            for j in range(2):
                sp.wait_ge(mod_ready, 2 * i + (j - 1))
                load_half(2 * i + j, j)
        sp.wait_ge(far_set, 1)
        sp.dma_start(k["lists"].rearrange("(p n) c -> p (n c)", p=P), far[:, :]).then_inc(stored, 16)
        sp.wait_ge(rows_out, 1)
        sp.dma_start(o["logf_prompt"].rearrange("(t p) h -> p t h", p=P), logf_rows[:, 0:NT, :]).then_inc(stored, 16)
        sp.dma_start(o["logf_sample"], logf_rows[0:DEC, NT, :]).then_inc(stored, 16)
        sp.wait_ge(cum_done, 1)
        sp.dma_start(k["forget"], cum[:, :]).then_inc(stored, 16)
        sp.wait_ge(stored, 64)

    @block.gpsimd
    def _(pool):
        pool.sem_inc(k["begun"], 1)
        pool.memset(half[:, :], -0.5).then_inc(half_set, 1)
        pool.memset(far[:, :], FAR).then_inc(far_set, 1)
        pool.wait_ge(half_set, 1)

        def step(t, j):
            r = rows_of(t)
            pool.wait_ge(ms_done, t + 1)
            pool.tensor_tensor(rstd[0:r, j:j + 1], ssq[0:r, j:j + 1], half[0:r, :], ALU.pow).then_inc(rstd_done, 1)

        def lower(t, j):
            r = rows_of(t)
            pool.wait_ge(hi_done, t + 1)
            cols = bass.ds(t * P, r)
            pool.tensor_tensor(h_lo[:, :, cols], h[j][:, :, 0:r], h_hi[:, :, cols], ALU.subtract).then_inc(lo_done, 1)

        step(0, 0)
        with pool.Fori(0, NT // 2 - 1) as i:
            for j in range(2):
                step(2 * i + j + 1, 1 - j)
                lower(2 * i + j, j)
        step(NT - 1, 1)
        lower(NT - 2, 0)
        step(NT, 0)
        lower(NT - 1, 1)
        lower(NT, 0)

    @block.scalar
    def _(act):
        act.wait_ge(vec_ld, 16)
        act.activation(sc[:, :, :], vecs[:, V_C:V_C + 16].rearrange("p (k n) -> p k n", n=2), ACT.Silu)\
           .then_inc(silu_done, 1)

        def load(t, j):
            r = rows_of(t)
            src = xs if r == DEC else xp[bass.ds(t * P, P), :]
            act.dma_start(x[j][0:r, :], src).then_inc(x_ld[j], 16)

        for t in range(2):
            load(t, t)
        own = Own(act, own_act)

        def square(t, j, nth):
            r = rows_of(t)
            act.wait_ge(sq_done, t)
            act.wait_ge(x_ld[j], 16 * (nth + 1))
            act.activation(squares[0:r, :], x[j][0:r, :], ACT.Square, accum_out=ssq[0:r, j:j + 1]).then_inc(sq_done, 1)

        def move(t, j, more):
            r, n = rows_of(t), cond_of(t)
            act.wait_ge(xT_ready, t + 1)
            if not (isinstance(t, int) and t < 2):
                act.wait_ge(lo_done, t - 1)
            for c in range(0, NC // 2):
                ins = act.activation(h[j][:, c, 0:r], xT_ps[j][:, c, 0:r], ACT.Identity,
                                     bias=mod[:, SH1, c, n:n + 1], scale=a1[:, c, n:n + 1])
            ins.then_inc(xT_out_act, 1)
            act.wait_ge(xT_out_act, t + 1)
            act.wait_ge(xT_out_dve, t + 1)
            act.activation(h_hi[:, :, bass.ds(t * P, r)], h[j][:, :, 0:r], ACT.Copy).then_inc(hi_done, 1)
            if more:
                load(*more)

        square(0, 0, 0)
        act.wait_ge(a1_done, 1)
        for j in range(2):
            square(j + 1, 1 - j, j)
            move(j, j, (j + 2, j))
        with act.Fori(1, NT // 2 - 1) as i:
            for j in range(2):
                square(2 * i + j + 1, 1 - j, i + j)
                move(2 * i + j, j, (2 * i + j + 2, j))
        square(NT - 1, 1, NT // 2 - 1)
        move(NT - 2, 0, (NT, 0))
        square(NT, 0, NT // 2)
        move(NT - 1, 1, None)
        move(NT, 0, None)
        act.wait_ge(wf_ld, 48)
        act.activation(w_f_hi[:, :, :], w_f[:, :, :], ACT.Copy).then_inc(wf_split, 1)
        act.wait_ge(z_done, 1)
        own(act.activation(e[:, :], z[:, :], ACT.Abs))
        own(act.activation(e[:, :], e[:, :], ACT.Exp, scale=-1.0))
        act.activation(e[:, :], e[:, :], ACT.Ln, bias=1.0).then_inc(e_done, 1)

    @block.tensor
    def _(pe):
        pe.wait_ge(silu_done, 1)
        for n in range(4):
            pe.wait_ge(w_ld[n % 2], 16 * (n // 2 + 1))
            modulation_half(pe, w_ada[n % 2], sc, mod_ps[:, 8 * n:8 * n + 8]).then_inc(mod_ready, 1)
        pe.wait_ge(c_ld, 16)
        ident = consts[:, K_ID:K_ID + P]

        def step(t, j):
            r = rows_of(t)
            pe.wait_ge(xn_done, t + 1)
            pe.wait_ge(xT_out_act, t)
            pe.wait_ge(xT_out_dve, t)
            for c in range(NC):
                ins = pe.transpose(xT_ps[j][:, c, 0:r], x[j][0:r, c * P:(c + 1) * P], ident[0:r, 0:r])
            ins.then_inc(xT_ready, 1)

        with pe.Fori(0, NT // 2) as i:
            for j in range(2):
                step(2 * i + j, j)
                pe.wait_ge(w_ld[j], 16 * (i + 3))
                if j == 0:
                    pe.wait_ge(a1_done, 1)
                modulation_half(pe, w_ada[j], sc, mod_ps[:, bass.ds(16 * i + (32 + 8 * j), 8)]).then_inc(mod_ready, 1)
        step(NT, 0)
        pe.wait_ge(wf_split, 2)
        pe.wait_ge(lo_done, NT + 1)
        for n0, n in ((0, 512), (512, 512), (SEQ, DEC)):
            m = 0
            for kc in range(NC):
                for wf, h_part in ((w_f_hi, h_hi), (w_f_hi, h_lo), (w_f_lo, h_hi)):
                    ins = pe.matmul(f_ps[:, n0:n0 + n], wf[:, kc, :], h_part[:, kc, n0:n0 + n],
                                    start=(m == 0), stop=(m == 3 * NC - 1))
                    m += 1
        ins.then_inc(f_ready, 1)
        pe.wait_ge(logf_done, 1)
        pe.wait_ge(mod_out, 1)
        for t in range(NT + 1):
            r = rows_of(t)
            ins = pe.transpose(mod_ps[0:r, 128 + 8 * t:136 + 8 * t], logf[:, t * P:t * P + r], ident[0:8, 0:8])
        ins.then_inc(rows_ready, 1)

    @block.vector
    def _(dve):
        own = Own(dve, own_dve)

        def normalise(t, j):
            r = rows_of(t)
            dve.wait_ge(sq_done, t + 1)
            dve.tensor_scalar(ssq[0:r, j:j + 1], ssq[0:r, j:j + 1], 1.0 / D, EPS, ALU.mult, ALU.add).then_inc(ms_done, 1)
            dve.wait_ge(rstd_done, t + 1)
            dve.tensor_scalar(x[j][0:r, :], x[j][0:r, :], rstd[0:r, j:j + 1], None, ALU.mult).then_inc(xn_done, 1)

        def move(t, j):
            r, n = rows_of(t), cond_of(t)
            dve.wait_ge(xT_ready, t + 1)
            if not (isinstance(t, int) and t < 2):
                dve.wait_ge(lo_done, t - 1)
            for c in range(NC // 2, NC):
                ins = dve.tensor_scalar(h[j][:, c, 0:r], xT_ps[j][:, c, 0:r], a1[:, c, n:n + 1],
                                        mod[:, SH1, c, n:n + 1], ALU.mult, ALU.add)
            ins.then_inc(xT_out_dve, 1)

        dve.wait_ge(vec_ld, 16)
        for sec in (SH1, SC1):
            dve.wait_ge(mod_ready, 4)
            bias = vecs[:, V_BADA + 8 * sec:V_BADA + 8 * sec + 8]
            own(dve.tensor_tensor(mod[:, sec, :, :], mod_ps[:, 16 * sec:16 * sec + 16].rearrange("p (c n) -> p c n", n=2),
                                  rep(bias, 2, 2), ALU.add))
        dve.scalar_tensor_tensor(a1[:, :, :], mod[:, SC1, :, :], 1.0, rep(vecs[:, V_NMIX:V_NMIX + 8], 2, 2),
                                 ALU.add, ALU.mult).then_inc(a1_done, 1)
        dve.wait_ge(a1_done, 1)
        normalise(0, 0)
        for j in range(2):
            normalise(j + 1, 1 - j)
            move(j, j)
        with dve.Fori(1, NT // 2 - 1) as i:
            for j in range(2):
                normalise(2 * i + j + 1, 1 - j)
                move(2 * i + j, j)
        normalise(NT - 1, 1)
        move(NT - 2, 0)
        normalise(NT, 0)
        move(NT - 1, 1)
        move(NT, 0)

        dve.wait_ge(wf_split, 1)
        dve.tensor_tensor(w_f_lo[:, :, :], w_f[:, :, :], w_f_hi[:, :, :], ALU.subtract).then_inc(wf_split, 1)
        dve.wait_ge(mod_ready, HALVES)
        dve.tensor_tensor(mod[:, G1:G2 + 1, :, :].rearrange("p s c n -> p (s c) n"),
                          mod_ps[:, 16 * G1:16 * (G2 + 1)].rearrange("p (c n) -> p c n", n=2),
                          rep(vecs[:, V_BADA + 8 * G1:V_BADA + 8 * (G2 + 1)], 2, 2), ALU.add).then_inc(mod_out, 1)
        dve.wait_ge(f_ready, 1)
        dve.wait_ge(wf_ld, 48)
        dve.tensor_scalar(z[:, :], f_ps[:, 0:TOK], b_f[:, 0:1], None, ALU.add).then_inc(z_done, 1)
        dve.wait_ge(e_done, 1)
        dve.scalar_tensor_tensor(logf[:, :], z[:, :], 0.0, e[:, :], ALU.min, ALU.subtract).then_inc(logf_done, 1)
        dve.wait_ge(logf_done, 1)
        own(dve.tensor_copy(logf_s[:, PAST:PAST + DEC], logf[:, SEQ:TOK]))
        one = consts[0:8, K_ONES:K_ONES + 1]
        own(dve.tensor_tensor_scan(cum[:, 0:SEQ], one.to_broadcast([8, SEQ]), logf[:, 0:SEQ], 0.0, ALU.mult, ALU.add))
        own(dve.tensor_tensor_scan(cum[:, SEQ:KEYS], one.to_broadcast([8, PAST + DEC]), logf_s[:, :], 0.0,
                                   ALU.mult, ALU.add))
        dve.tensor_scalar(cum[:, :], cum[:, :], -1.0 / SCALE, None, ALU.mult).then_inc(cum_done, 1)
        dve.wait_ge(rows_ready, 1)
        dve.tensor_copy(logf_rows[:, 0:NT, :], mod_ps[:, 128:128 + 8 * NT].rearrange("p (t h) -> p t h", h=8))
        dve.tensor_copy(logf_rows[0:DEC, NT, :], mod_ps[0:DEC, 128 + 8 * NT:136 + 8 * NT]).then_inc(rows_out, 1)


def unit_keys(group, t):
    if t == NT:
        return [(SEQ, PAST, "cache"), (SEQ + PAST, DEC, NT)]
    first = max(0, t - BAND_TILES + 1) if group == "band" else 0
    return [(b * P, P, b) for b in range(first, t + 1)]


def attend(nc, s, group, a, o, k, hT, w):
    fox = group == "fox"
    consts, rows_all, begun = k["consts"], k["rows_all"], k["begun"]
    g = 0 if fox else 1
    ident = consts[:, K_ID:K_ID + P]
    h_hi, h_lo = hT
    most = SEQ if fox else BAND
    kv = s.sb("kv", [P, NT + 1, 2, P])
    cache = s.sb("cache", [P, 2, P])
    twice = s.sb("twice", [P, 2, 2, 2, HD])
    q_both = s.sb("q_both", [P, 2, TOK], F32R)
    k_hi = s.sb("k_hi", [P, 2, KEYS], F32R)
    k_lo = s.sb("k_lo", [P, 2, KEYS], F32R)
    probs = [s.sb(f"probs{j}", [P, most]) for j in range(2)]
    pT = s.sb("pT", [P, most // P, P])
    oT = s.sb("oT", [P, P])
    nmax = s.sb("nmax", [P, UNITS])
    denom = s.sb("denom", [P, UNITS])
    rden = s.sb("rden", [P, UNITS])
    if fox:
        bias = s.sb("forget", [P, 2, KEYS])
        ident_r = s.sb("ident_r", [P, P], F32R)
        causal_r = s.sb("causal_r", [P, P], F32R)
    else:
        bias = s.sb("bias", [P, 2, BAND])
    s_ps = [s.ps(f"s{j}", [P, 1024]) for j in range(2)]
    pT_ps = s.ps("pT", [P, NT, P])
    o_ps = [s.ps(f"o{j}", [P, 512]) for j in range(2)]
    banks = [s_ps[n // 2][:, 512 * (n % 2):512 * (n % 2) + 512] for n in range(4)]
    slot = [t % 4 for t in range(NT)] + [1]

    w_ld, w_split = k["w_ld"], k["w_split"]
    cache_ld, bias_ld, bias_set = s.sem("cache_ld"), s.sem("bias_ld"), s.sem("bias_set")
    rows_ready, kv_out, q_twice, k_twice = s.sem("rows_ready"), s.sem("kv_out"), s.sem("q_twice"), s.sem("k_twice")
    T_ready, hi_done, lo_done = s.sem("T_ready"), s.sem("hi_done"), s.sem("lo_done")
    s_ready, max_done, exp_done = s.sem("s_ready"), s.sem("max_done"), s.sem("exp_done")
    pT_ready, pT_out, o_ready, oT_out, back_ready, rden_done, o_out = (
        s.sem(n) for n in ("pT_ready", "pT_out", "o_ready", "oT_out", "back_ready", "rden_done", "o_out"))
    stored, masks_set = s.sem("stored"), s.sem("masks_set")
    block = s.ctx.enter_context(nc.Block())

    TILES, TS = NT + 1, NT + 2
    units = [(u // 2, u % 2) for u in range(UNITS)]
    keys = [unit_keys(group, t) for t, _ in units]
    chunks = [[(b, min(b + 4, len(kb))) for b in range(0, len(kb), 4)] for kb in keys]
    chunk0 = [sum(len(c) for c in chunks[:u]) for u in range(UNITS + 1)]

    @block.sync
    def _(sp):
        def load_w(n):
            sp.dma_start(w["raw"][:, :, :], a["w_qkv"][bass.ds(n, 1)].rearrange("a p k n -> p (a k) n")).then_inc(w_ld, 16)

        if fox:
            load_w(0)
        with sp.Fori(0, PAIRS) as i:
            sp.wait_ge(o_ready, UNITS * i)
            sp.wait_ge(max_done, UNITS * i)
            src = k["forget"][bass.ds(2 * i, 2), :] if fox else None
            sp.dma_start(bias[:, :, :], rep(src, 0, P) if fox else a["rel"][:, bass.ds(2 * i, 2), :]).then_inc(bias_ld, 16)
            for n, name in enumerate(("k", "v")):
                sp.dma_start(cache[:, n, :], a[f"cache_{name}_{'a' if fox else 'b'}"][:, bass.ds(i * P, P)])\
                  .then_inc(cache_ld, 16)
            alone(sp, w_split, 2 * (i + 1 + PAIRS * g), begun)
            if fox:
                load_w(i + 1)
            else:
                with sp.If(i < PAIRS - 1):
                    load_w(nc.s_assert_within(i + (PAIRS + 1), 0, 2 * PAIRS - 1,
                                              skip_runtime_bounds_check_because="the branch says i < PAIRS - 1"))
                with sp.Else():
                    sp.nop()
            sp.wait_ge(kv_out, TILES * (i + 1))
            t0 = 0 if fox else NT - o["k_b_prompt"].shape[0] // P
            for n, name in enumerate(("k", "v")):
                dst = o[f"{name}_{'a' if fox else 'b'}_prompt"][:, bass.ds(i * P, P)]
                sp.dma_start(dst.rearrange("(t p) n -> p t n", p=P), kv[:, t0:NT, n, :]).then_inc(stored, 16)
                dst = o[f"{name}_{'a' if fox else 'b'}_sample"][:, bass.ds(i * P, P)]
                sp.dma_start(dst, kv[0:DEC, NT, n, :]).then_inc(stored, 16)
        sp.wait_ge(stored, 64 * PAIRS)

    @block.gpsimd
    def _(pool):
        with pool.Fori(0, PAIRS) as i:
            for t in range(TS):
                r = rows_of(t) if t < TILES else PAST
                if t < TILES:
                    alone(pool, kv_out, TILES * i + t + 1, begun)
                    src = kv[0:r, t, 0, :]
                else:
                    alone(pool, cache_ld, 32 * (i + 1), begun)
                    src = cache[:, 0, :]
                alone(pool, T_ready, TS * i + t, begun)
                pool.tensor_copy(twice[0:r, 1, :, :, :], rep(src.rearrange("p (h n) -> p h n", h=2), 2, 2))\
                    .then_inc(k_twice, 1)

            def split():
                alone(pool, w_ld, 16 * (i + 2 + PAIRS * g), begun)
                alone(pool, rows_ready, TILES * (i + 1), begun)
                pool.tensor_copy(w["hi"][:, :, :], w["raw"][:, :, :]).then_inc(w_split, 1)
                alone(pool, w_split, 2 * (i + 1 + PAIRS * g) + 1, begun)
                pool.tensor_tensor(w["lo"][:, :, :], w["raw"][:, :, :], w["hi"][:, :, :], ALU.subtract).then_inc(w_split, 1)

            if fox:
                split()
            else:
                with pool.If(i < PAIRS - 1):
                    split()
                with pool.Else():
                    pool.nop()

    @block.tensor
    def _(pe):
        with pe.Fori(0, PAIRS) as i:
            def rows(t):
                r = rows_of(t)
                if t == 0:
                    alone(pe, w_split, 2 * (i + 1 + PAIRS * g), begun)
                last = max((v for v in range(t) if slot[v] == slot[t]), default=None)
                if last is not None:
                    alone(pe, q_twice, TILES * i + last + 1, begun)
                n = 0
                for kc in range(NC):
                    for h, m in ((h_hi, "hi"), (h_hi, "lo"), (h_lo, "hi")):
                        ins = pe.matmul(banks[slot[t]][0:r, 0:3 * P], h[:, kc, t * P:t * P + r], w[m][:, kc, :],
                                        start=(n == 0), stop=(n == 3 * NC - 1))
                        n += 1
                ins.then_inc(rows_ready, 1)

            def to_columns(t):
                r = rows_of(t) if t < TILES else PAST
                if t < TILES:
                    alone(pe, q_twice, TILES * i + t + 1, begun)
                alone(pe, k_twice, TS * i + t + 1, begun)
                if t >= 2:
                    alone(pe, lo_done, TS * i + t - 1, begun)
                for n in range(0 if t < TILES else 2, 4):
                    ins = pe.transpose(pT_ps[:, 4 * (t % 2) + n, 0:r],
                                       twice[0:r, n // 2, n % 2, :, :].rearrange("p a n -> p (a n)"), ident[0:r, 0:r])
                ins.then_inc(T_ready, 1)

            def scores(u):
                (t, h), kb = units[u], keys[u]
                r = rows_of(t)
                if u < 2:
                    alone(pe, q_twice, TILES * i + 7, begun)
                if h == 0:
                    alone(pe, lo_done, TS * i + (TS if t == NT else t + 1), begun)
                if u >= 2:
                    alone(pe, max_done, UNITS * i + u - 1, begun)
                k0, n = kb[0][0], sum(b[1] for b in kb)
                own = n - kb[-1][1]
                q = q_both[:, h, t * P:t * P + r]
                for c in range(0, n, 512):
                    m = min(512, n - c)
                    masked = fox and c <= own < c + m
                    pe.matmul(s_ps[u % 2][0:r, c:c + m], q, k_hi[:, h, k0 + c:k0 + c + m], start=True, stop=False)
                    ins = pe.matmul(s_ps[u % 2][0:r, c:c + m], q, k_lo[:, h, k0 + c:k0 + c + m],
                                    start=False, stop=not masked)
                    if masked:
                        ins = pe.matmul(s_ps[u % 2][0:r, own:n], ident_r[0:r, 0:r], causal_r[0:r, 0:r],
                                        start=False, stop=True)
                ins.then_inc(s_ready, 1)

            def transpose(u):
                (t, h), kb = units[u], keys[u]
                r = rows_of(t)
                alone(pe, exp_done, UNITS * i + u + 1, begun)
                for b0, b1 in chunks[u]:
                    for b in range(b0, b1):
                        m = kb[b][1]
                        ins = pe.transpose(pT_ps[0:m, b, 0:r], probs[u % 2][0:r, b * P:b * P + m], ident[0:r, 0:r])
                    ins.then_inc(pT_ready, 1)

            def values(u):
                (t, h), kb = units[u], keys[u]
                r = rows_of(t)
                if t >= 2 and h == 0:
                    alone(pe, o_out, TILES * i + t - 1, begun)
                for n, (b0, b1) in enumerate(chunks[u]):
                    alone(pe, pT_out, chunk0[UNITS] * i + chunk0[u] + n + 1, begun)
                    for b in range(b0, b1):
                        _, m, vt = kb[b]
                        v = cache[0:m, 1, HD * h:HD * h + HD] if vt == "cache" else kv[0:m, vt, 1, HD * h:HD * h + HD]
                        ins = pe.matmul(o_ps[t % 2][HD * h:HD * h + HD, 0:r], v, pT[0:m, b, 0:r],
                                        start=(b == 0), stop=(b == len(kb) - 1))
                ins.then_inc(o_ready, 1)

            def to_rows(t):
                r = rows_of(t)
                alone(pe, oT_out, TILES * i + t + 1, begun)
                pe.transpose(o_ps[t % 2][0:r, P:2 * P], oT[:, 0:r], ident).then_inc(back_ready, 1)

            rows(0)
            for t in range(1, TILES):
                rows(t)
                to_columns(t - 1)
            if fox:
                alone(pe, masks_set, 2, begun)
            scores(0)
            scores(1)
            to_columns(TILES - 1)
            to_columns(TILES)
            alone(pe, lo_done, TS * (i + 1), begun)
            for u in range(UNITS):
                transpose(u)
                if u % 2 == 0 and u >= 2:
                    to_rows(u // 2 - 1)
                if u + 2 < UNITS:
                    scores(u + 2)
                values(u)
            to_rows(TILES - 1)

    @block.vector
    def _(dve):
        if fox:
            dve.wait_ge(w_split, 1)
            dve.tensor_tensor(w["lo"][:, :, :], w["raw"][:, :, :], w["hi"][:, :, :], ALU.subtract).then_inc(w_split, 1)
        with dve.Fori(0, PAIRS) as i:
            def kv_rows(t):
                r = rows_of(t)
                dve.wait_ge(rows_ready, TILES * i + t + 1)
                dve.tensor_copy(kv[0:r, t, :, :], banks[slot[t]][0:r, P:3 * P].rearrange("p (a n) -> p a n", a=2))\
                   .then_inc(kv_out, 1)

            def lower(t):
                r = rows_of(t) if t < TILES else PAST
                k0 = t * P if t < NT else (SEQ + PAST if t == NT else SEQ)
                alone(dve, hi_done, TS * i + t + 1, begun)
                bank = pT_ps[:, 4 * (t % 2):4 * (t % 2) + 4, 0:r]
                if t < TILES:
                    low = q_both[HD:P, :, t * P:t * P + r]
                    dve.tensor_tensor(low, bank[HD:P, 0:2, :], low, ALU.subtract)
                dve.tensor_tensor(k_lo[:, :, k0:k0 + r], bank[:, 2:4, :], k_hi[:, :, k0:k0 + r], ALU.subtract)\
                   .then_inc(lo_done, 1)

            def row_max(u):
                (t, h), kb = units[u], keys[u]
                r, n = rows_of(t), sum(b[1] for b in kb)
                alone(dve, s_ready, UNITS * i + u + 1, begun)
                j0 = kb[0][0] if fox else ((BAND_TILES - 1) * P - PAST if t == NT else BAND - n)
                dve.tensor_tensor_reduce(probs[u % 2][0:r, 0:n], s_ps[u % 2][0:r, 0:n], bias[0:r, h, j0:j0 + n],
                                         -SCALE, BIG, ALU.add, ALU.min, nmax[0:r, u:u + 1]).then_inc(max_done, 1)

            def move_pT(u):
                (t, h), kb = units[u], keys[u]
                r = rows_of(t)
                for n, (b0, b1) in enumerate(chunks[u]):
                    dve.wait_ge(pT_ready, chunk0[UNITS] * i + chunk0[u] + n + 1)
                    if t == NT:
                        dve.tensor_copy(pT[:, 0, 0:r], pT_ps[:, 0, 0:r])
                        ins = dve.tensor_copy(pT[0:DEC, 1, 0:r], pT_ps[0:DEC, 1, 0:r])
                    else:
                        ins = dve.tensor_copy(pT[:, b0:b1, :], pT_ps[:, b0:b1, :])
                    ins.then_inc(pT_out, 1)
                dve.reciprocal(rden[0:r, u:u + 1], denom[0:r, u:u + 1]).then_inc(rden_done, 1)

            alone(dve, bias_ld, 16 * (i + 1), begun)
            if not fox:
                dve.tensor_scalar(bias[:, :, :], bias[:, :, :], 1.0 / SCALE, None, ALU.mult).then_inc(bias_set, 1)
                alone(dve, bias_set, i + 1, begun)
                dve.memset(bias[P // 2:P, :, 0:HD], NEG)
                dve.memset(bias[0:P // 2, :, BAND - HD:BAND], NEG).then_inc(masks_set, 1)
            alone(dve, stored, 64 * i, begun)
            kv_rows(0)
            for t in range(1, TILES):
                kv_rows(t)
                lower(t - 1)
            if not fox:
                alone(dve, masks_set, i + 1, begun)
            alone(dve, o_out, TILES * i, begun)
            row_max(0)
            row_max(1)
            lower(TILES - 1)
            lower(TILES)
            for u in range(UNITS):
                move_pT(u)
                if u + 2 < UNITS:
                    row_max(u + 2)

    @block.scalar
    def _(act):
        if fox:
            act.wait_ge(w_ld, 16)
            act.activation(w["hi"][:, :, :], w["raw"][:, :, :], ACT.Copy).then_inc(w_split, 1)
            act.activation(ident_r[:, :], ident, ACT.Copy).then_inc(masks_set, 1)
            act.activation(causal_r[:, :], consts[:, K_CAUSAL:K_CAUSAL + P], ACT.Copy).then_inc(masks_set, 1)
        with act.Fori(0, PAIRS) as i:
            def q_rows(t):
                r = rows_of(t)
                act.wait_ge(kv_out, TILES * i + t + 1)
                act.wait_ge(T_ready, TS * i + t)
                act.activation(twice[0:r, 0, :, :, :],
                               rep(banks[slot[t]][0:r, 0:P].rearrange("p (h n) -> p h n", h=2), 2, 2), ACT.Copy)\
                   .then_inc(q_twice, 1)

            def upper(t):
                r = rows_of(t) if t < TILES else PAST
                k0 = t * P if t < NT else (SEQ + PAST if t == NT else SEQ)
                act.wait_ge(T_ready, TS * i + t + 1)
                bank = pT_ps[:, 4 * (t % 2):4 * (t % 2) + 4, 0:r]
                if t < TILES:
                    act.activation(q_both[:, :, t * P:t * P + r], bank[:, 0:2, :], ACT.Copy)
                act.activation(k_hi[:, :, k0:k0 + r], bank[:, 2:4, :], ACT.Copy).then_inc(hi_done, 1)

            def exp(u):
                r, n = rows_of(units[u][0]), sum(b[1] for b in keys[u])
                act.wait_ge(max_done, UNITS * i + u + 1)
                act.activation(probs[u % 2][0:r, 0:n], probs[u % 2][0:r, 0:n], ACT.Exp, bias=nmax[0:r, u:u + 1],
                               scale=-1.0, accum_out=denom[0:r, u:u + 1]).then_inc(exp_done, 1)

            def columns_out(t):
                r = rows_of(t)
                act.wait_ge(o_ready, UNITS * i + 2 * t + 2)
                act.activation(oT[:, 0:r], o_ps[t % 2][:, 0:r], ACT.Copy).then_inc(oT_out, 1)

            def rows_out(t):
                r = rows_of(t)
                act.wait_ge(back_ready, TILES * i + t + 1)
                act.wait_ge(rden_done, UNITS * i + 2 * t + 2)
                for h in range(2):
                    ins = act.activation(rows_all[0:r, t, bass.ds(i * P + (512 * g + HD * h), HD)],
                                         o_ps[t % 2][0:r, P + HD * h:P + HD * h + HD], ACT.Copy,
                                         scale=rden[0:r, 2 * t + h:2 * t + h + 1])
                ins.then_inc(o_out, 1)

            q_rows(0)
            for t in range(1, TILES):
                q_rows(t)
                upper(t - 1)
            exp(0)
            exp(1)
            upper(TILES - 1)
            upper(TILES)
            for u in range(UNITS):
                if u + 2 < UNITS:
                    exp(u + 2)
                if u % 2 == 1:
                    columns_out(u // 2)
                elif u >= 2:
                    rows_out(u // 2 - 1)
            rows_out(TILES - 1)


def mix_out(nc, s, a, o, k, g2):
    consts, vecs, mod, rows_all, table = k["consts"], k["vecs"], k["mod"], k["rows_all"], k["table"]
    begun = k["begun"]
    ident = consts[:, K_ID:K_ID + P]
    ones = consts[:, K_ONES:K_ONES + P]
    w_out = s.sb("w_out", [P, NC, D])
    w_r = s.sb("w_r", [P, NC, NR])
    b_r = s.sb("b_r", [P, NR])
    g1, sh2, a2 = (s.sb(n, [P, 2, D]) for n in ("gate1_rows", "shift2_rows", "scale2_rows"))
    a2col = s.sb("a2col", [P, NC, 2])
    half = s.sb("minus_half", [P, 2 * NG * 2])
    x = s.sb("x", [P, D])
    osq = s.sb("osq", [P, D])
    hs, hr = s.sb("head_ms", [P, 16]), s.sb("head_rstd", [P, 16])
    on = s.sb("on", [P, D])
    oT = s.sb("oT", [P, NC, P])
    y = s.sb("y", [P, D])
    xsq = s.sb("xsq", [P, D])
    ms, rstd = s.sb("ms", [P, 1]), s.sb("rstd", [P, 1])
    h2 = s.sb("h2", [P, D])
    h2T = s.sb("h2T", [P, NC, P])
    lg = s.sb("lg", [P, NR])
    gmax = s.sb("gmax", [P, 1])
    dg = s.sb("dg", [P, NG])
    eg = s.sb("eg", [P, NG])
    gsum = s.sb("gsum", [P, 1])
    pri_g = s.sb("pri_g", [P, NG])
    best_g = s.sb("best_g", [P, 1])
    pen = s.sb("pen", [P, NG])
    em = s.sb("em", [P, NE])
    em2 = s.sb("em2", [P, NE])
    top = s.sb("top", [P, 8])
    pri_e = s.sb("pri_e", [P, NE])
    best_e = s.sb("best_e", [P, 1])
    oh = s.sb("oh", [P, 2, NE])
    dv, ev, den = s.sb("dv", [P, 1]), s.sb("ev", [P, 1]), s.sb("den", [P, 1])
    picked = s.sb("picked", [P, NE])
    before = s.sb("before", [P, NE])
    slot = s.sb("slot", [P, NE])
    junk = s.sb("junk", [P, NE])
    slot_f = s.sb("slot_f", [P, 2])
    slot_i = s.sb("slot_i", [P, 2], I32)
    tok = s.sb("tok", [P, 2, 2])
    entry = s.sb("entry", [P, 2, 4], I32)
    cnt = s.sb("cnt", [1, NE])
    need = s.sb("need", [1, NE, 9])
    nb, cb = s.sb("nb", [1, NE]), s.sb("cb", [1, NE])
    done = s.sb("done", [1, TABLE, NE])
    eb, bb, start = s.sb("eb", [1, TABLE]), s.sb("bb", [1, TABLE]), s.sb("start", [1, TABLE])
    pairs = s.sb("pairs", [1, NBLK // 2])
    steps = s.sb("steps", [1, 1])

    oT_ps, h2T_ps = s.ps("oT", [P, NC, P]), s.ps("h2T", [P, NC, P])
    y_ps = s.ps("y", [P, D])
    lg_ps, pos_ps = s.ps("lg", [P, 512]), s.ps("pos", [P, 512])

    ld, gate_cols, gate_ready, gate_out = s.sem("ld"), s.sem("gate_cols"), s.sem("gate_ready"), s.sem("gate_out")
    half_set, scaled, zeroed = s.sem("half_set"), s.sem("scaled"), s.sem("zeroed")
    osq_done, hms_done, hr_done, on_ready = s.sem("osq_done"), s.sem("hms_done"), s.sem("hr_done"), s.sem("on_ready")
    oT_ready, oT_out, y_ready, y_used = s.sem("oT_ready"), s.sem("oT_out"), s.sem("y_ready"), s.sem("y_used")
    x_ld, x1_done, xsq_done, ms_done, rstd_done = (s.sem(n) for n in ("x_ld", "x1_done", "xsq_done", "ms_done", "rstd_done"))
    scaled_h2, h2_ready, h2_stored = s.sem("scaled_h2"), s.sem("h2_ready"), s.sem("h2_stored")
    h2T_ready, h2T_out, lg_ready, lg_used = s.sem("h2T_ready"), s.sem("h2T_out"), s.sem("lg_ready"), s.sem("lg_used")
    dg_done, eg_done, dv_done, ev_done = s.sem("dg_done"), s.sem("eg_done"), s.sem("dv_done"), s.sem("ev_done")
    picked_done, pos_ready, slots_done, listed = (s.sem(n) for n in ("picked_done", "pos_ready", "slots_done", "listed"))
    cnt_ready, own_dve, w_own, g_own = s.sem("cnt_ready"), s.sem("own_dve"), s.sem("w_own"), s.sem("g_own")
    xp, xs = a["x_prompt"][0], a["x_sample"][0]
    block = s.ctx.enter_context(nc.Block())
    GATES = [(G1, g1), (SH2, sh2), (SC2, a2), (G2, g2)]

    LOOP = range(0, NT - 3)

    def over_steps(eng, step):
        for n in range(-3, 0):
            step(n)
        with eng.Fori(LOOP.start, LOOP.stop) as n:
            step(n)
        for n in range(LOOP.stop, NT + 1):
            step(n)

    def live(t):
        return not isinstance(t, int) or 0 <= t <= NT

    def tile_rows(t, r):
        return rows_all[0:r, bass.ds(t, 1), :].rearrange("p a n -> p (a n)")

    @block.sync
    def _(sp):
        sp.dma_start(w_out[:, :, :], a["w_out"]).then_inc(ld, 16)
        sp.dma_start(w_r[:, :, :], a["w_r"]).then_inc(ld, 16)
        sp.dma_start(b_r[:, :], rep(a["b_r"], 0, P)).then_inc(ld, 16)

        def step(n):
            t = n + 1
            if live(t):
                r = rows_of(t)
                sp.wait_ge(x1_done, t)
                sp.dma_start(x[0:r, :], xs if r == DEC else xp[bass.ds(t * P, P), :]).then_inc(x_ld, 16)
            if live(n):
                r = rows_of(n)
                sp.wait_ge(h2_ready, n + 1)
                sp.dma_start(k["h2"][bass.ds(n * P, r), :], h2[0:r, :]).then_inc(h2_stored, 16)

        over_steps(sp, step)
        sp.wait_ge(h2_stored, 16 * (NT + 1))

    @block.gpsimd
    def _(pool):
        pool.memset(half[:, :], -0.5).then_inc(half_set, 1)
        pool.memset(entry[:, :, :], 0).then_inc(zeroed, 1)
        pool.memset(before[:, :], 0.0).then_inc(zeroed, 1)
        pool.wait_ge(half_set, 1)

        def step(n):
            if live(n + 1):
                t, r = n + 1, rows_of(n + 1)
                pool.wait_ge(x_ld, 16 * (t + 1))
                pool.wait_ge(y_used, t + 1)
                pool.tensor_tensor(tile_rows(t, r), y[0:r, :], x[0:r, :], ALU.add).then_inc(x1_done, 1)
            if live(n + 3):
                t, r = n + 3, rows_of(n + 3)
                pool.wait_ge(hms_done, t + 1)
                pool.tensor_tensor(hr[0:r, :], hs[0:r, :], half[0:r, :], ALU.pow).then_inc(hr_done, 1)
            if live(n + 1):
                t, r = n + 1, rows_of(n + 1)
                pool.wait_ge(ms_done, t + 1)
                pool.tensor_tensor(rstd[0:r, :], ms[0:r, :], half[0:r, 0:1], ALU.pow).then_inc(rstd_done, 1)
                pool.wait_ge(scaled_h2, t + 1)
                pool.tensor_tensor(h2[0:r, :], h2[0:r, :], sh2[0:r, cond_of(t), :], ALU.add).then_inc(h2_ready, 1)
            if live(n):
                r = rows_of(n)
                alone(pool, slots_done, n + 1, begun)
                for pick in range(2):
                    pool.indirect_dma_start(k["lists"], bass.IndirectOffsetOnAxis(ap=slot_i[0:r, pick:pick + 1], axis=0),
                                            entry[0:r, pick, :], None, bounds_check=LISTS - 1, oob_is_err=False)\
                        .then_inc(listed, 16)

        over_steps(pool, step)
        pool.wait_ge(listed, 32 * (NT + 1))

    @block.tensor
    def _(pe):
        pe.wait_ge(gate_cols, 1)
        for n, (sec, _) in enumerate(GATES):
            for cond in range(2):
                m = 2 * n + cond
                dst = (oT_ps, h2T_ps)[m % 2]
                if m >= 2:
                    pe.wait_ge(gate_out, m - 1)
                for c in range(NC):
                    col = a2col[:, c, cond:cond + 1] if sec == SC2 else mod[:, sec, c, cond:cond + 1]
                    ins = pe.matmul(dst[:, c, :], col.to_broadcast([P, P]), ident, start=True, stop=True)
                ins.then_inc(gate_ready, 1)
        pe.wait_ge(gate_out, 2 * len(GATES))
        pe.wait_ge(scaled, NC)
        pe.wait_ge(ld, 48)

        def transpose_o(t):
            r = rows_of(t)
            pe.wait_ge(on_ready, t + 1)
            for c in range(NC):
                ins = pe.transpose(oT_ps[:, c, 0:r], on[0:r, c * P:(c + 1) * P], ident[0:r, 0:r])
            ins.then_inc(oT_ready, 1)

        def project(t):
            r = rows_of(t)
            pe.wait_ge(oT_out, t + 1)
            pe.wait_ge(y_used, t)
            for n in range(2):
                for c in range(NC):
                    ins = pe.matmul(y_ps[0:r, 512 * n:512 * n + 512], oT[:, c, 0:r], w_out[:, c, 512 * n:512 * n + 512],
                                    start=(c == 0), stop=(c == NC - 1))
            ins.then_inc(y_ready, 1)

        def transpose_h(t):
            r = rows_of(t)
            pe.wait_ge(h2_ready, t + 1)
            for c in range(NC):
                ins = pe.transpose(h2T_ps[:, c, 0:r], h2[0:r, c * P:(c + 1) * P], ident[0:r, 0:r])
            ins.then_inc(h2T_ready, 1)

        def route(t):
            r = rows_of(t)
            pe.wait_ge(h2T_out, t + 1)
            pe.wait_ge(lg_used, t)
            for c in range(NC):
                ins = pe.matmul(lg_ps[0:r, 0:NR], h2T[:, c, 0:r], w_r[:, c, :], start=(c == 0), stop=(c == NC - 1))
            ins.then_inc(lg_ready, 1)

        def positions(t):
            r = rows_of(t)
            pe.wait_ge(picked_done, t + 1)
            pe.wait_ge(slots_done, t)
            pe.matmul(pos_ps[0:r, 0:NE], consts[0:r, K_BEFORE:K_BEFORE + r], picked[0:r, :], start=True, stop=False)
            pe.matmul(pos_ps[0:r, 0:NE], ones[:, 0:r], before[:, :], start=False, stop=True).then_inc(pos_ready, 1)

        def step(n):
            if live(n):
                transpose_h(n)
            if live(n + 2):
                transpose_o(n + 2)
            if live(n):
                route(n)
            if live(n + 2):
                project(n + 2)
            if live(n):
                positions(n)

        over_steps(pe, step)
        pe.wait_ge(slots_done, NT + 1)
        pe.matmul(pos_ps[:, 64:64 + NE], ones, before[:, :], start=True, stop=True).then_inc(cnt_ready, 1)

    @block.scalar
    def _(act):
        for m in range(2 * len(GATES)):
            _, dst = GATES[m // 2]
            src = (oT_ps, h2T_ps)[m % 2]
            act.wait_ge(gate_ready, m + 1)
            act.activation(dst[:, m % 2, :], src[:, :, :].rearrange("p c n -> p (c n)"), ACT.Copy).then_inc(gate_out, 1)

        def step(n):
            if live(n):
                r = rows_of(n)
                act.wait_ge(h2T_ready, n + 1)
                act.activation(h2T[:, :, 0:r], h2T_ps[:, :, 0:r], ACT.Copy).then_inc(h2T_out, 1)
            if live(n + 2):
                r = rows_of(n + 2)
                act.wait_ge(oT_ready, n + 3)
                act.activation(oT[:, :, 0:r], oT_ps[:, :, 0:r], ACT.Copy).then_inc(oT_out, 1)
            if live(n + 3):
                t, r = n + 3, rows_of(n + 3)
                act.wait_ge(hms_done, t)
                act.activation(osq[0:r, :], tile_rows(t, r), ACT.Square).then_inc(osq_done, 1)
            if live(n + 1):
                t, r = n + 1, rows_of(n + 1)
                act.wait_ge(x1_done, t + 1)
                act.wait_ge(rstd_done, t)
                act.activation(xsq[0:r, :], tile_rows(t, r), ACT.Square, accum_out=ms[0:r, :]).then_inc(xsq_done, 1)
            if live(n):
                r = rows_of(n)
                act.wait_ge(dg_done, n + 1)
                act.activation(eg[0:r, :], dg[0:r, :], ACT.Exp, accum_out=gsum[0:r, :]).then_inc(eg_done, 1)
                act.wait_ge(dv_done, n + 1)
                act.activation(ev[0:r, :], dv[0:r, :], ACT.Exp).then_inc(ev_done, 1)

        over_steps(act, step)

    @block.vector
    def _(dve):
        dve.scalar_tensor_tensor(a2col[:, :, :], mod[:, SC2, :, :], 1.0, rep(vecs[:, V_NFFN:V_NFFN + 8], 2, 2),
                                 ALU.add, ALU.mult).then_inc(gate_cols, 1)
        dve.wait_ge(ld, 48)
        for c in range(NC):
            dve.tensor_scalar(w_out[:, c, :], w_out[:, c, :], vecs[:, V_ONORM + c:V_ONORM + c + 1], None, ALU.mult)\
               .then_inc(scaled, 1)
        dve.tensor_copy(tok[:, :, :], consts[:, K_TOK:K_TOK + 4].rearrange("p (a b) -> p a b", a=2)).then_inc(w_own, 1)
        dve.wait_ge(w_own, 1)
        dve.wait_ge(half_set, 1)
        dve.wait_ge(zeroed, 2)
        dve.wait_ge(gate_out, 2 * len(GATES))

        def gated(t):
            r = rows_of(t)
            dve.wait_ge(y_ready, t + 1)
            dve.wait_ge(x1_done, t)
            dve.tensor_tensor(y[0:r, :], y_ps[0:r, :], g1[0:r, cond_of(t), :], ALU.mult).then_inc(y_used, 1)

        def head_sums(t):
            r = rows_of(t)
            dve.wait_ge(osq_done, t + 1)
            dve.tensor_reduce(hs[0:r, :], osq[0:r, :].rearrange("p (h n) -> p h n", n=HD), AX.X, ALU.add)\
               .then_inc(w_own, 1)
            dve.wait_ge(w_own, t + 2)
            dve.tensor_scalar(hs[0:r, :], hs[0:r, :], 1.0 / HD, EPS, ALU.mult, ALU.add).then_inc(hms_done, 1)

        def mean_square(t):
            r = rows_of(t)
            dve.wait_ge(xsq_done, t + 1)
            dve.tensor_scalar(ms[0:r, :], ms[0:r, :], 1.0 / D, EPS, ALU.mult, ALU.add).then_inc(ms_done, 1)

        def scale_h2(t):
            r = rows_of(t)
            dve.wait_ge(rstd_done, t + 1)
            dve.wait_ge(h2_stored, 16 * t)
            dve.wait_ge(h2T_ready, t)
            dve.scalar_tensor_tensor(h2[0:r, :], tile_rows(t, r), rstd[0:r, 0:1], a2[0:r, cond_of(t), :],
                                     ALU.mult, ALU.mult).then_inc(scaled_h2, 1)

        def normalise_o(t):
            r = rows_of(t)
            dve.wait_ge(hr_done, t + 1)
            dve.wait_ge(oT_ready, t)
            dve.tensor_tensor(on[0:r, :].rearrange("p (h n) -> p h n", n=HD),
                              tile_rows(t, r).rearrange("p (h n) -> p h n", n=HD), rep(hr[0:r, :], 2, HD),
                              ALU.mult).then_inc(on_ready, 1)

        PICK = 20

        def pick(t):
            r = rows_of(t)
            own = Own(dve, own_dve, PICK * t)
            dve.wait_ge(lg_ready, t + 1)
            dve.tensor_tensor(lg[0:r, :], lg_ps[0:r, 0:NR], b_r[0:r, :], ALU.add).then_inc(lg_used, 1)
            dve.wait_ge(lg_used, t + 1)
            own(dve.tensor_reduce(gmax[0:r, :], lg[0:r, 0:NG], AX.X, ALU.max))
            dve.tensor_scalar(dg[0:r, :], lg[0:r, 0:NG], gmax[0:r, 0:1], None, ALU.subtract).then_inc(dg_done, 1)
            dve.wait_ge(dg_done, t + 1)
            own(dve.scalar_tensor_tensor(pri_g[0:r, :], dg[0:r, :], 0.0, consts[0:r, K_PRIG:K_PRIG + NG],
                                         ALU.is_equal, ALU.mult))
            own(dve.tensor_reduce(best_g[0:r, :], pri_g[0:r, :], AX.X, ALU.max))
            own(dve.tensor_scalar(pen[0:r, :], pri_g[0:r, :], best_g[0:r, 0:1], -1.0, ALU.is_equal, ALU.add))
            own(dve.scalar_tensor_tensor(em[0:r, :].rearrange("p (g e) -> p g e", g=NG), rep(pen[0:r, :], 2, EPG), 1e30,
                                         lg[0:r, NG:NR].rearrange("p (g e) -> p g e", g=NG), ALU.mult, ALU.add),
                wait=False)
            alone(dve, own_dve, PICK * t + own.n, begun)
            own(dve.max(top[0:r, :], em[0:r, :]))
            dve.tensor_scalar(dv[0:r, :], top[0:r, 1:2], top[0:r, 0:1], None, ALU.subtract).then_inc(dv_done, 1)
            src = em
            for n in range(2):
                own(dve.scalar_tensor_tensor(pri_e[0:r, :], src[0:r, :], top[0:r, n:n + 1],
                                             consts[0:r, K_PRIE:K_PRIE + NE], ALU.is_equal, ALU.mult))
                own(dve.tensor_reduce(best_e[0:r, :], pri_e[0:r, :], AX.X, ALU.max))
                own(dve.tensor_scalar(oh[0:r, n, :], pri_e[0:r, :], best_e[0:r, 0:1], None, ALU.is_equal))
                if n == 0:
                    own(dve.scalar_tensor_tensor(em2[0:r, :], oh[0:r, 0, :], -3e38, em[0:r, :], ALU.mult, ALU.add))
                    src = em2
            dve.tensor_tensor(picked[0:r, :], oh[0:r, 0, :], oh[0:r, 1, :], ALU.add).then_inc(picked_done, 1)
            dve.wait_ge(listed, 32 * t)
            dve.wait_ge(eg_done, t + 1)
            dve.wait_ge(ev_done, t + 1)
            weight = entry[0:r, :, 2].bitcast(F32)
            own(dve.tensor_scalar(den[0:r, :], ev[0:r, :], 1.0, gsum[0:r, 0:1], ALU.add, ALU.mult))
            own(dve.reciprocal(weight[:, 0:1], den[0:r, :]))
            dve.tensor_tensor(weight[:, 1:2], weight[:, 0:1], ev[0:r, :], ALU.mult)
            own(dve.tensor_copy(entry[0:r, :, 0:2], tok[0:r, :, :]))
            own(dve.tensor_scalar(tok[:, :, :], tok[:, :, :], float(P), None, ALU.add))
            dve.wait_ge(pos_ready, t + 1)
            own(dve.tensor_tensor(slot[0:r, :], pos_ps[0:r, 0:NE], consts[0:r, K_BASE:K_BASE + NE], ALU.add))
            for n in range(2):
                own(dve.tensor_tensor_reduce(junk[0:r, :], slot[0:r, :], oh[0:r, n, :], 1.0, 0.0, ALU.mult, ALU.add,
                                             slot_f[0:r, n:n + 1]))
            assert own.n == PICK, own.n
            dve.tensor_tensor(before[0:r, :], before[0:r, :], picked[0:r, :], ALU.add)
            dve.tensor_copy(slot_i[0:r, :], slot_f[0:r, :]).then_inc(slots_done, 1)

        def step(n):
            if live(n + 1):
                gated(n + 1)
            if live(n + 3):
                head_sums(n + 3)
            if live(n + 1):
                mean_square(n + 1)
                scale_h2(n + 1)
            if live(n + 3):
                normalise_o(n + 3)
            if live(n):
                pick(n)

        over_steps(dve, step)
        dve.wait_ge(slots_done, NT + 1)

        own = Own(dve, g_own)
        dve.wait_ge(cnt_ready, 1)
        own(dve.tensor_copy(cnt[:, :], pos_ps[0:1, 64:64 + NE]))
        own(dve.tensor_tensor(need[:, :, :], rep(cnt[:, :], 2, 9), rep(consts[0:1, K_THR:K_THR + 9], 1, NE), ALU.is_gt))
        own(dve.tensor_reduce(nb[:, :], need[:, :, :], AX.X, ALU.add))
        own(dve.tensor_tensor_scan(cb[:, :], ones[0:1, 0:NE], nb[:, :], 0.0, ALU.mult, ALU.add))
        blk = consts[0:1, K_BLK:K_BLK + TABLE]
        own(dve.tensor_tensor(done[:, :, :], rep(cb[:, :], 1, TABLE), rep(blk, 2, NE), ALU.is_le))
        own(dve.tensor_reduce(eb[:, :], done[:, :, :], AX.X, ALU.add))
        own(dve.tensor_tensor(done[:, :, :], done[:, :, :], rep(nb[:, :], 1, TABLE), ALU.mult))
        own(dve.tensor_reduce(bb[:, :], done[:, :, :], AX.X, ALU.add))
        own(dve.tensor_tensor(bb[:, :], blk, bb[:, :], ALU.subtract))
        own(dve.tensor_scalar(bb[:, :], bb[:, :], float(P), None, ALU.mult))
        own(dve.scalar_tensor_tensor(start[:, :], eb[:, :], float(REGION), bb[:, :], ALU.mult, ALU.add))
        own(dve.tensor_scalar(table[:, 2 + TABLE:2 + 2 * TABLE], start[:, :], float(DUMMY), None, ALU.min))
        own(dve.tensor_scalar(table[:, 2:2 + TABLE], eb[:, :], float(NE - 1), None, ALU.min))
        even = consts[0:1, K_BLK:K_BLK + NBLK].rearrange("p (n two) -> p n two", two=2)[:, :, 0]
        own(dve.tensor_scalar(pairs[:, :], even, cb[:, NE - 1:NE], None, ALU.is_lt))
        own(dve.tensor_reduce(steps[:, :], pairs[:, :], AX.X, ALU.add))
        own(dve.tensor_copy(table[:, 0:1], steps[:, :]))


def experts(nc, s, a, k):
    consts, table, begun = k["consts"], k["table"], k["begun"]
    ident = consts[:, K_ID:K_ID + P]
    w_gu = [s.sb(f"w_gu{j}", [P, NC, 2 * DE]) for j in range(2)]
    w_dn = [s.sb(f"w_dn{j}", [P, 2, D]) for j in range(2)]
    g_list = [s.sb(f"gather_list{j}", [P, 4], I32) for j in range(2)]
    s_list = [s.sb(f"scatter_list{j}", [P, 4], I32) for j in range(2)]
    x = [s.sb(f"x{j}", [P, D]) for j in range(2)]
    xT = s.sb("xT", [P, NC, P])
    gate = s.sb("gate", [P, DE])
    hidden = s.sb("hidden", [P, DE])
    hT = s.sb("hT", [P, 2, P])
    y = [s.sb(f"y{j}", [P, D]) for j in range(2)]
    xT_ps = s.ps("xT", [P, NC, P])
    gu_ps = [s.ps(f"gu{j}", [P, 512]) for j in range(2)]
    hT_ps = s.ps("hT", [P, 512])
    y_ps = s.ps("y", [P, D])

    gu_ld, dn_ld, gl_ld, sl_ld, gathered, scattered = (
        [s.sem(f"{n}{j}") for j in range(2)] for n in ("gu_ld", "dn_ld", "gl_ld", "sl_ld", "gathered", "scattered"))
    cleared, xT_ready, xT_out_act, xT_out_dve = (s.sem(n) for n in ("cleared", "xT_ready", "xT_out_act", "xT_out_dve"))
    gu_ready, gate_done, hidden_done, hT_ready, hT_out = (
        s.sem(n) for n in ("gu_ready", "gate_done", "hidden_done", "hT_ready", "hT_out"))
    y_ready, y_out_act, y_out_dve = s.sem("y_ready"), s.sem("y_out_act"), s.sem("y_out_dve")
    block = s.ctx.enter_context(nc.Block())

    def steps(eng, body):
        n = eng.value_load(table[0:1, 0:1], min_val=1, max_val=NBLK // 2)
        with eng.Fori(0, NBLK // 2) as i:
            with eng.If(i < n):
                for j in range(2):
                    body(i, j)
            with eng.Else():
                eng.nop()
        return n

    @block.sync
    def _(sp):
        def expert(b):
            return sp.value_load(table[0:1, bass.ds(b + 2, 1)], min_val=0, max_val=NE - 1)

        def start(b):
            return sp.value_load(table[0:1, bass.ds(b + (2 + TABLE), 1)], min_val=0, max_val=DUMMY)

        def gate_up(ex, j):
            sp.dma_start(w_gu[j][:, :, :], a["w_gu"][bass.ds(ex, 1)].rearrange("a p k n -> p (a k) n")).then_inc(gu_ld[j], 16)

        def down(ex, j):
            sp.dma_start(w_dn[j][:, :, :], a["w_dn"][bass.ds(ex, 1)].rearrange("a p k n -> p (a k) n")).then_inc(dn_ld[j], 16)

        def entries(first, dst, sem):
            sp.dma_start(dst[:, :], k["lists"][bass.ds(first, P), :]).then_inc(sem, 16)

        for j in range(2):
            entries(start(j), g_list[j], gl_ld[j])
            gate_up(expert(j), j)
        for j in range(2):
            first = start(2 + j)
            sp.wait_ge(gathered[j], 16)
            entries(first, g_list[j], gl_ld[j])
        down(expert(0), 0)
        entries(start(0), s_list[0], sl_ld[0])

        def body(i, j):
            b = 2 * i + j
            e2, e1, s4, s1 = expert(b + 2), expert(b + 1), start(b + 4), start(b + 1)
            alone(sp, gu_ready, b + 1, begun)
            gate_up(e2, j)
            alone(sp, y_ready, b, begun)
            down(e1, 1 - j)
            q, n = ahead(i, j, 2)
            alone(sp, gathered[q], 16 * (n + 1), begun)
            entries(s4, g_list[j], gl_ld[j])
            alone(sp, scattered[1 - j], 16 * (i + j), begun)
            entries(s1, s_list[1 - j], sl_ld[1 - j])

        n = steps(sp, body)
        alone(sp, gu_ld[0], 16 * n + 16, begun)
        alone(sp, gu_ld[1], 16 * n + 16, begun)
        alone(sp, dn_ld[0], 16 * n + 16, begun)
        alone(sp, dn_ld[1], 16 * n, begun)
        alone(sp, gl_ld[0], 16 * n + 32, begun)
        alone(sp, gl_ld[1], 16 * n + 32, begun)
        alone(sp, sl_ld[0], 16 * n + 16, begun)
        alone(sp, sl_ld[1], 16 * n, begun)

    @block.gpsimd
    def _(pool):
        for j in range(2):
            pool.memset(x[j][:, :], 0.0).then_inc(cleared, 1)
        pool.wait_ge(cleared, 2)

        def gather(j, nth):
            alone(pool, gl_ld[j], 16 * (nth + 1), begun)
            pool.indirect_dma_start(x[j][:, :], None, k["h2"], bass.IndirectOffsetOnAxis(ap=g_list[j][:, 0:1], axis=0),
                                    bounds_check=TOK - 1, oob_is_err=False).then_inc(gathered[j], 16)

        gather(0, 0)
        gather(1, 0)
        pool.wait_ge(xT_ready, 1)
        gather(0, 1)

        def body(i, j):
            b = 2 * i + j
            pool.wait_ge(xT_ready, b + 2)
            gather(*ahead(i, j, 3))
            pool.wait_ge(sl_ld[j], 16 * (i + 1))
            pool.wait_ge(y_out_act, b + 1)
            alone(pool, y_out_dve, b + 1, begun)
            pool.indirect_dma_start(k["yrows"], bass.IndirectOffsetOnAxis(ap=s_list[j][:, 1:2], axis=0), y[j][:, :], None,
                                    bounds_check=2 * TOK - 1, oob_is_err=False).then_inc(scattered[j], 16)

        n = steps(pool, body)
        alone(pool, scattered[0], 16 * n, begun)
        alone(pool, scattered[1], 16 * n, begun)
        alone(pool, gathered[0], 16 * n + 32, begun)
        alone(pool, gathered[1], 16 * n + 16, begun)

    @block.tensor
    def _(pe):
        def transpose_x(j, nth):
            pe.wait_ge(gathered[j], 16 * (nth + 1))
            for c in range(NC):
                ins = pe.transpose(xT_ps[:, c, :], x[j][:, c * P:(c + 1) * P], ident)
            ins.then_inc(xT_ready, 1)

        def gate_up(j, nth):
            b = 2 * nth + j
            pe.wait_ge(gu_ld[j], 16 * (nth + 1))
            pe.wait_ge(xT_out_act, b + 1)
            pe.wait_ge(xT_out_dve, b + 1)
            for c in range(NC):
                ins = pe.matmul(gu_ps[j][:, :], xT[:, c, :], w_gu[j][:, c, :], start=(c == 0), stop=(c == NC - 1))
            ins.then_inc(gu_ready, 1)

        def transpose_hidden(b):
            pe.wait_ge(hidden_done, b + 1)
            for c in range(2):
                ins = pe.transpose(hT_ps[:, c * P:(c + 1) * P], hidden[:, c * P:(c + 1) * P], ident)
            ins.then_inc(hT_ready, 1)

        def down(j, nth):
            b = 2 * nth + j
            pe.wait_ge(dn_ld[j], 16 * (nth + 1))
            pe.wait_ge(hT_out, b + 1)
            pe.wait_ge(y_out_act, b)
            pe.wait_ge(y_out_dve, b)
            for n in range(2):
                for c in range(2):
                    ins = pe.matmul(y_ps[:, 512 * n:512 * n + 512], hT[:, c, :], w_dn[j][:, c, 512 * n:512 * n + 512],
                                    start=(c == 0), stop=(c == 1))
            ins.then_inc(y_ready, 1)

        transpose_x(0, 0)
        gate_up(0, 0)
        transpose_x(1, 0)

        def body(i, j):
            gate_up(*ahead(i, j, 1))
            transpose_hidden(2 * i + j)
            transpose_x(*ahead(i, j, 2))
            down(j, i)

        steps(pe, body)

    @block.scalar
    def _(act):
        def move_xT(b):
            act.wait_ge(xT_ready, b + 1)
            act.activation(xT[:, 0:4, :], xT_ps[:, 0:4, :], ACT.Copy).then_inc(xT_out_act, 1)

        def silu(b, j):
            act.wait_ge(gu_ready, b + 1)
            act.wait_ge(hidden_done, b)
            act.activation(gate[:, :], gu_ps[j][:, 0:DE], ACT.Silu).then_inc(gate_done, 1)

        move_xT(0)
        silu(0, 0)
        move_xT(1)

        def body(i, j):
            b = 2 * i + j
            move_xT(b + 2)
            act.wait_ge(y_ready, b + 1)
            act.wait_ge(sl_ld[j], 16 * (i + 1))
            act.activation(y[j][:, 0:512], y_ps[:, 0:512], ACT.Copy, scale=s_list[j][:, 2:3].bitcast(F32))\
               .then_inc(y_out_act, 1)
            silu(b + 1, 1 - j)

        steps(act, body)

    @block.vector
    def _(dve):
        def move_xT(b):
            dve.wait_ge(xT_ready, b + 1)
            dve.tensor_copy(xT[:, 4:8, :], xT_ps[:, 4:8, :]).then_inc(xT_out_dve, 1)

        def gate_times_up(b, j):
            dve.wait_ge(gate_done, b + 1)
            dve.wait_ge(hT_ready, b)
            dve.tensor_tensor(hidden[:, :], gate[:, :], gu_ps[j][:, DE:2 * DE], ALU.mult).then_inc(hidden_done, 1)

        move_xT(0)
        gate_times_up(0, 0)
        move_xT(1)

        def body(i, j):
            b = 2 * i + j
            dve.wait_ge(hT_ready, b + 1)
            dve.tensor_copy(hT[:, :, :], hT_ps[:, 0:2 * P].rearrange("p (c n) -> p c n", c=2)).then_inc(hT_out, 1)
            move_xT(b + 2)
            dve.wait_ge(y_ready, b + 1)
            dve.wait_ge(sl_ld[j], 16 * (i + 1))
            dve.tensor_scalar(y[j][:, 512:1024], y_ps[:, 512:1024], s_list[j][:, 2:3].bitcast(F32), None, ALU.mult)\
               .then_inc(y_out_dve, 1)
            gate_times_up(b + 1, 1 - j)

        steps(dve, body)


def finish(nc, s, a, o, k, g2):
    rows_all = k["rows_all"]
    ya = [s.sb(f"ya{j}", [P, D]) for j in range(2)]
    yb = [s.sb(f"yb{j}", [P, D]) for j in range(2)]
    squares = s.sb("squares", [P, D])
    ms, rstd = s.sb("ms", [P, 2]), s.sb("rstd", [P, 2])
    half = s.sb("minus_half", [P, 1])
    norm = s.sb("norm", [P, D])
    norm_ld, half_set = s.sem("norm_ld"), s.sem("half_set")
    y_ld = [s.sem(f"y_ld{j}") for j in range(2)]
    stored = [s.sem(f"stored{j}") for j in range(2)]
    summed, gated, x_done, sq_done, ms_done, rstd_done, out_ready = (
        s.sem(n) for n in ("summed", "gated", "x_done", "sq_done", "ms_done", "rstd_done", "out_ready"))
    block = s.ctx.enter_context(nc.Block())

    def over_tiles(eng, step):
        with eng.Fori(0, NT // 2) as i:
            for j in range(2):
                step(2 * i + j, j, i)
        step(NT, 0, NT // 2)

    def tile_rows(t, r):
        return rows_all[0:r, bass.ds(t, 1), :].rearrange("p a n -> p (a n)")

    @block.sync
    def _(sp):
        sp.dma_start(norm[:, :], rep(a["norm_final"], 0, P)).then_inc(norm_ld, 16)

        def load(t, j):
            r = rows_of(t)
            sp.dma_start(ya[j][0:r, :], k["yrows"][bass.ds(t * P, r), :]).then_inc(y_ld[j], 16)
            sp.dma_start(yb[j][0:r, :], k["yrows"][bass.ds(t * P + TOK, r), :]).then_inc(y_ld[j], 16)

        def store(t, j):
            r = rows_of(t)
            sp.wait_ge(out_ready, t + 1)
            dst = o["y_sample"] if r == DEC else o["y_prompt"][bass.ds(t * P, P), :]
            sp.dma_start(dst, ya[j][0:r, :]).then_inc(stored[j], 16)

        load(0, 0)
        load(1, 1)
        with sp.Fori(0, NT // 2 - 1) as i:
            for j in range(2):
                store(2 * i + j, j)
                sp.wait_ge(stored[j], 16 * (i + 1))
                load(2 * i + j + 2, j)
        store(NT - 2, 0)
        sp.wait_ge(stored[0], 16 * (NT // 2))
        load(NT, 0)
        store(NT - 1, 1)
        store(NT, 0)
        sp.wait_ge(stored[0], 16 * (NT // 2 + 1))
        sp.wait_ge(stored[1], 16 * (NT // 2))

    @block.gpsimd
    def _(pool):
        pool.memset(half[:, :], -0.5).then_inc(half_set, 1)
        pool.wait_ge(half_set, 1)

        def step(t, j, i):
            r = rows_of(t)
            pool.wait_ge(y_ld[j], 32 * (i + 1))
            pool.tensor_tensor(ya[j][0:r, :], ya[j][0:r, :], yb[j][0:r, :], ALU.add).then_inc(summed, 1)
            pool.wait_ge(ms_done, t + 1)
            pool.tensor_tensor(rstd[0:r, j:j + 1], ms[0:r, j:j + 1], half[0:r, :], ALU.pow).then_inc(rstd_done, 1)

        over_tiles(pool, step)

    @block.scalar
    def _(act):
        def step(t, j, i):
            r = rows_of(t)
            act.wait_ge(x_done, t + 1)
            act.activation(squares[0:r, :], ya[j][0:r, :], ACT.Square, accum_out=ms[0:r, j:j + 1]).then_inc(sq_done, 1)

        over_tiles(act, step)

    @block.vector
    def _(dve):
        dve.wait_ge(norm_ld, 16)

        def step(t, j, i):
            r = rows_of(t)
            dve.wait_ge(summed, t + 1)
            dve.tensor_tensor(ya[j][0:r, :], ya[j][0:r, :], g2[0:r, cond_of(t), :], ALU.mult).then_inc(gated, 1)
            dve.wait_ge(gated, t + 1)
            dve.tensor_tensor(ya[j][0:r, :], ya[j][0:r, :], tile_rows(t, r), ALU.add).then_inc(x_done, 1)
            dve.wait_ge(sq_done, t + 1)
            dve.tensor_scalar(ms[0:r, j:j + 1], ms[0:r, j:j + 1], 1.0 / D, EPS, ALU.mult, ALU.add).then_inc(ms_done, 1)
            dve.wait_ge(rstd_done, t + 1)
            dve.scalar_tensor_tensor(ya[j][0:r, :], ya[j][0:r, :], rstd[0:r, j:j + 1], norm[0:r, :],
                                     ALU.mult, ALU.mult).then_inc(out_ready, 1)

        over_tiles(dve, step)


def constants():
    import numpy as np
    c = np.zeros((P, K_END), np.float32)
    i, j = np.arange(P)[:, None], np.arange(P)[None, :]
    c[:, K_ID:K_ID + P] = i == j
    c[:, K_CAUSAL:K_CAUSAL + P] = np.where(j <= i, 0.0, NEG)
    c[:, K_BEFORE:K_BEFORE + P] = i < j
    c[:, K_ONES:K_ONES + P] = 1.0
    c[:, K_PRIG:K_PRIG + NG] = NG - np.arange(NG)
    c[:, K_PRIE:K_PRIE + NE] = NE - np.arange(NE)
    c[:, K_BASE:K_BASE + NE] = REGION * np.arange(NE)
    c[:, K_THR:K_THR + 9] = P * np.arange(9)
    c[:, K_BLK:K_BLK + TABLE] = np.arange(TABLE)
    c[:, K_TOK:K_TOK + 4] = np.arange(P)[:, None] + np.array([0, 0, 0, TOK])
    return c


def kernel(**inputs):
    import numpy as np
    import concourse.bacc as bacc
    from concourse.bass_utils import run_bass_kernel_spmd

    x = {name: np.asarray(v) for name, v in inputs.items()}

    def by_partition(v):
        return v.reshape(-1, NC, P).transpose(2, 0, 1).reshape(P, -1)

    def rows(m):
        return m.reshape(-1, P, m.shape[-1]).transpose(1, 0, 2)

    w_in = x["w_in"][0]
    wa, wb = w_in[:, 0:1536], w_in[:, 1544:3080]
    qkv = np.stack([np.stack([np.concatenate([w[:, 512 * n + P * i:512 * n + P * (i + 1)] for n in range(3)], 1)
                              for i in range(PAIRS)]) for w in (wa, wb)])
    c2 = np.stack([x["c_prompt"][0], x["c_sample"][0]], 1)
    vecs = np.concatenate([
        rows(c2).reshape(P, 16), by_partition(x["b_ada"][0]), by_partition(x["norm_mix"][0]),
        by_partition(np.concatenate([x["onorm_a"][0], x["onorm_b"][0]])), by_partition(x["norm_ffn"][0])], 1)
    m = np.clip(BAND - P + np.arange(P)[:, None] - np.arange(BAND)[None, :], -128, 128) + 128
    arrays = {
        "x_prompt": x["x_prompt"], "x_sample": x["x_sample"],
        "consts": constants(), "vecs": vecs,
        "w_ada": x["w_ada"][0].reshape(NC, P, HALVES, D // 2).transpose(2, 1, 0, 3),
        "w_qkv": qkv.reshape(2 * PAIRS, NC, P, 3 * P).transpose(0, 2, 1, 3),
        "w_f": rows(w_in[:, 1536:1544]), "b_f": x["b_fgate"].reshape(8, 1),
        "cache_logf": x["cache_logf_a"][0, 0].T,
        "rel": x["rel_bias"][0][:, m].transpose(1, 0, 2),
        "w_out": rows(x["w_out"][0]),
        "w_r": rows(np.concatenate([x["w_router_group"][0], x["w_router_expert"][0]], 1)),
        "b_r": np.concatenate([x["b_router_group"][0], x["b_router_expert"][0]]),
        "w_gu": np.concatenate([x["w_gate"][0], x["w_up"][0]], 2).reshape(NE, NC, P, 2 * DE).transpose(0, 2, 1, 3),
        "w_dn": x["w_down"][0].reshape(NE, 2, P, D).transpose(0, 2, 1, 3),
        "norm_final": x["norm_final"],
    }
    for name in ("k_a", "v_a", "k_b", "v_b"):
        arrays["cache_" + name] = x["cache_" + name][0, 0].reshape(PAST, 512)
    lb = min(512, SEQ)
    outs = {"y_prompt": (SEQ, D), "y_sample": (DEC, D),
            "k_a_prompt": (SEQ, 512), "v_a_prompt": (SEQ, 512), "logf_prompt": (SEQ, 8),
            "k_b_prompt": (lb, 512), "v_b_prompt": (lb, 512),
            "k_a_sample": (DEC, 512), "v_a_sample": (DEC, 512), "logf_sample": (DEC, 8),
            "k_b_sample": (DEC, 512), "v_b_sample": (DEC, 512)}

    nc = bacc.Bacc("TRN2", target_bir_lowering=False, num_devices=1)
    arrays = {name: np.ascontiguousarray(v) for name, v in arrays.items()}
    a = {name: nc.dram_tensor(f"in_{name}", v.shape, mybir.dt.from_np(v.dtype), kind="ExternalInput").ap()
         for name, v in arrays.items()}
    o = {name: nc.dram_tensor(f"out_{name}", shape, F32, kind="ExternalOutput").ap() for name, shape in outs.items()}
    build(nc, a, o)
    r = run_bass_kernel_spmd(nc, [{f"in_{name}": v for name, v in arrays.items()}], core_ids=[0])
    got = {name: r.results[0][f"out_{name}"] for name in outs}

    def heads(name):
        v = got[name]
        return v.reshape(1, 1, v.shape[0], 8, HD)

    return (got["y_prompt"][None], got["y_sample"][None],
            heads("k_a_prompt"), heads("v_a_prompt"), got["logf_prompt"][None, None],
            heads("k_b_prompt"), heads("v_b_prompt"),
            heads("k_a_sample"), heads("v_a_sample"), got["logf_sample"][None, None],
            heads("k_b_sample"), heads("v_b_sample"))
```

```python
from contextlib import ExitStack

import concourse.bass as bass
from concourse import mybir

F32 = mybir.dt.float32
F32R = mybir.dt.float32r
I32 = mybir.dt.int32
ALU = mybir.AluOpType
ACT = mybir.ActivationFunctionType
AX = mybir.AxisListType

P = 128
D = 1024
NC = D // P
SEQ, DEC, PAST = 1024, 64, 128
NT = SEQ // P
TOK = SEQ + DEC
HD = 64
PAIRS = 4
UNITS = 2 * (NT + 1)
KEYS = SEQ + PAST + DEC
BAND_TILES = 5
BAND = BAND_TILES * P
NG, EPG, NE = 4, 8, 32
NR = NG + NE
DE = 256
NBLK = (2 * TOK + NE * (P - 1)) // P
REGION = 9 * P
DUMMY = NE * REGION
LISTS = DUMMY + P
TABLE = NBLK + 4
SCALE = HD ** -0.5
EPS = 1e-6
NEG = -1e30 / SCALE
FAR = 1 << 20
BIG = 1e38

V_C, V_BADA, V_NMIX, V_ONORM, V_NFFN, V_END = 0, 16, 64, 72, 80, 88
K_ID, K_CAUSAL, K_BEFORE, K_ONES = 0, P, 2 * P, 3 * P
K_PRIG = 4 * P
K_PRIE = K_PRIG + NG
K_BASE = K_PRIE + NE
K_THR = K_BASE + NE
K_BLK = K_THR + 9
K_TOK = K_BLK + TABLE
K_END = K_TOK + 4
SH1, SC1, G1, SH2, SC2, G2 = range(6)
HALVES = 12


def rows_of(t):
    return DEC if isinstance(t, int) and t == NT else P


def cond_of(t):
    return 1 if isinstance(t, int) and t == NT else 0


def alone(eng, sem, value, waited):
    eng.wait_ge(sem, value)
    eng.sem_inc(waited, 1)


def ahead(i, j, m):
    return (j + m) % 2, i + (j + m) // 2


def rep(ap, dim, n):
    a = ap.unsqueeze(dim)
    shape = list(a.shape)
    shape[dim] = n
    return a.to_broadcast(shape)


class Scope:

    def __init__(self, nc, ctx, name):
        self.nc, self.ctx, self.name = nc, ctx, name

    def sb(self, name, shape, dt=F32):
        return self.ctx.enter_context(self.nc.sbuf_tensor(f"{self.name}_{name}_sb", shape, dt))

    def ps(self, name, shape, dt=F32):
        return self.ctx.enter_context(self.nc.psum_tensor(f"{self.name}_{name}_ps", shape, dt))

    def sem(self, name):
        return self.ctx.enter_context(self.nc.semaphore(f"{self.name}_{name}_sem"))


class Own:

    def __init__(self, eng, sem, base=0):
        self.eng, self.sem, self.base, self.n = eng, sem, base, 0

    def __call__(self, ins, wait=True):
        ins.then_inc(self.sem, 1)
        self.n += 1
        if wait:
            self.eng.wait_ge(self.sem, self.base + self.n)


def build(nc, a, o):
    with ExitStack() as ctx:
        keep = Scope(nc, ctx, "keep")
        consts = keep.sb("consts", [P, K_END])
        vecs = keep.sb("vecs", [P, V_END])
        mod = keep.sb("mod", [P, 6, NC, 2])
        sc = keep.sb("silu_c", [P, NC, 2])
        rows_all = keep.sb("rows_all", [P, NT + 1, D])
        table = keep.sb("table", [1, 2 + 2 * TABLE], I32)
        waited = keep.sem("waited")
        k = dict(
            waited=waited,
            consts=consts, vecs=vecs, mod=mod, sc=sc, rows_all=rows_all, table=table,
            forget=nc.dram_tensor("forget_bias", (8, KEYS), F32, kind="Internal").ap(),
            h2=nc.dram_tensor("h2_rows", (TOK, D), F32, kind="Internal").ap(),
            lists=nc.dram_tensor("lists", (LISTS, 4), I32, kind="Internal").ap(),
            yrows=nc.dram_tensor("expert_rows", (2 * TOK, D), F32, kind="Internal").ap(),
        )
        with ExitStack() as attention:
            hT = [attention.enter_context(nc.sbuf_tensor(f"hT_{n}", [P, NC, TOK], F32R)) for n in ("hi", "lo")]
            with ExitStack() as c:
                modulate_in(nc, Scope(nc, c, "in"), a, o, k, hT)
            w_scope = Scope(nc, attention, "w_qkv")
            w = dict(raw=w_scope.sb("raw", [P, NC // 2, 3 * P]), hi=w_scope.sb("hi", [P, NC, 3 * P], F32R),
                     lo=w_scope.sb("lo", [P, NC, 3 * P], F32R))
            k["w_ld"], k["w_split"] = w_scope.sem("ld"), w_scope.sem("split")
            for group in ("fox", "band"):
                with ExitStack() as c:
                    attend(nc, Scope(nc, c, group), group, a, o, k, hT, w)
        with ExitStack() as c:
            g2 = c.enter_context(nc.sbuf_tensor("gate2_rows", [P, 2, D], F32))
            with ExitStack() as c2:
                mix_out(nc, Scope(nc, c2, "mix"), a, o, k, g2)
            with ExitStack() as c2:
                experts(nc, Scope(nc, c2, "moe"), a, k)
            with ExitStack() as c2:
                finish(nc, Scope(nc, c2, "fin"), a, o, k, g2)


def modulation_rows(pe, w, sc, out):
    for kc in range(NC):
        ins = pe.matmul(out[0:2, :], sc[:, kc, :], w[:, kc, :], start=(kc == 0), stop=(kc == NC - 1))
    return ins


def modulate_in(nc, s, a, o, k, hT):
    consts, vecs, mod, sc = k["consts"], k["vecs"], k["mod"], k["sc"]
    h_hi, h_lo = hT
    w_ada = [s.sb(f"w_ada{j}", [P, NC, D // 2]) for j in range(2)]
    x = [s.sb(f"x{j}", [P, D]) for j in range(2)]
    h = [s.sb(f"h{j}", [P, NC, P]) for j in range(2)]
    squares = s.sb("squares", [P, D])
    ssq = s.sb("ssq", [P, 2])
    rstd = s.sb("rstd", [P, 2])
    half = s.sb("minus_half", [P, 1])
    a1 = s.sb("a1", [P, NC, 2])
    w_f = s.sb("w_f", [P, NC, 8])
    w_f_hi, w_f_lo = s.sb("w_f_hi", [P, NC, 8], F32R), s.sb("w_f_lo", [P, NC, 8], F32R)
    b_f = s.sb("b_f", [8, 1])
    z = s.sb("z", [8, TOK])
    e = s.sb("e", [8, TOK])
    logf = s.sb("logf", [8, TOK])
    logf_s = s.sb("logf_s", [8, PAST + DEC])
    cum = s.sb("cum", [8, KEYS])
    logf_rows = s.sb("logf_rows", [P, NT + 1, 8])
    far = s.sb("far", [P, LISTS // P * 4], I32)
    xT_ps = [s.ps(f"xT{j}", [P, NC, P]) for j in range(2)]
    mod_ps = s.ps("mod", [P, 512])
    f_ps = s.ps("f", [8, 3 * 512])
    mod_rows = [s.sb(f"mod_rows{j}", [2, 512]) for j in range(2)]

    vec_ld, c_ld, wf_ld = s.sem("vec_ld"), s.sem("c_ld"), s.sem("wf_ld")
    w_ld = [s.sem(f"w_ld{j}") for j in range(2)]
    x_ld = [s.sem(f"x_ld{j}") for j in range(2)]
    mrow_ready, mrow_out = s.sem("mrow_ready"), s.sem("mrow_out")
    silu_done, mod_ready, mod_out = s.sem("silu_done"), s.sem("mod_ready"), s.sem("mod_out")
    a1_done = s.sem("a1_done")
    sq_done, ms_done, rstd_done, xn_done = s.sem("sq_done"), s.sem("ms_done"), s.sem("rstd_done"), s.sem("xn_done")
    xT_ready, xT_out_act, xT_out_dve = s.sem("xT_ready"), s.sem("xT_out_act"), s.sem("xT_out_dve")
    hi_done, lo_done, wf_split = s.sem("hi_done"), s.sem("lo_done"), s.sem("wf_split")
    half_set, far_set = s.sem("half_set"), s.sem("far_set")
    f_ready, z_done, e_done, logf_done = s.sem("f_ready"), s.sem("z_done"), s.sem("e_done"), s.sem("logf_done")
    rows_ready, rows_out, cum_done, stored = s.sem("rows_ready"), s.sem("rows_out"), s.sem("cum_done"), s.sem("stored")
    own_dve, own_act = s.sem("own_dve"), s.sem("own_act")
    xp, xs = a["x_prompt"][0], a["x_sample"][0]
    block = s.ctx.enter_context(nc.Block())

    @block.sync
    def _(sp):
        sp.dma_start(vecs[:, :], a["vecs"]).then_inc(vec_ld, 16)
        sp.dma_start(consts[:, :], a["consts"]).then_inc(c_ld, 16)

        def load_half(n, j):
            sp.dma_start(w_ada[j][:, :, :], a["w_ada"][bass.ds(n, 1)].rearrange("a p k n -> p (a k) n")).then_inc(w_ld[j], 16)

        for n in range(4):
            if n >= 2:
                sp.wait_ge(mod_ready, n - 1)
            load_half(n, n % 2)
        sp.dma_start(w_f[:, :, :], a["w_f"]).then_inc(wf_ld, 16)
        sp.dma_start(b_f[:, :], a["b_f"]).then_inc(wf_ld, 16)
        sp.dma_start(logf_s[:, 0:PAST], a["cache_logf"]).then_inc(wf_ld, 16)
        with sp.Fori(2, HALVES // 2) as i:
            for j in range(2):
                sp.wait_ge(mod_ready, 2 * i + (j - 1))
                load_half(2 * i + j, j)
        sp.wait_ge(far_set, 1)
        sp.dma_start(k["lists"].rearrange("(p n) c -> p (n c)", p=P), far[:, :]).then_inc(stored, 16)
        sp.wait_ge(rows_out, 1)
        sp.dma_start(o["logf_prompt"].rearrange("(t p) h -> p t h", p=P), logf_rows[:, 0:NT, :]).then_inc(stored, 16)
        sp.dma_start(o["logf_sample"], logf_rows[0:DEC, NT, :]).then_inc(stored, 16)
        sp.wait_ge(cum_done, 1)
        sp.dma_start(k["forget"], cum[:, :]).then_inc(stored, 16)
        sp.wait_ge(stored, 64)

    @block.gpsimd
    def _(pool):
        pool.memset(half[:, :], -0.5).then_inc(half_set, 1)
        pool.memset(far[:, :], FAR).then_inc(far_set, 1)
        pool.wait_ge(half_set, 1)

        def step(t, j):
            r = rows_of(t)
            pool.wait_ge(ms_done, t + 1)
            pool.tensor_tensor(rstd[0:r, j:j + 1], ssq[0:r, j:j + 1], half[0:r, :], ALU.pow).then_inc(rstd_done, 1)

        def lower(t, j):
            r = rows_of(t)
            pool.wait_ge(hi_done, t + 1)
            cols = bass.ds(t * P, r)
            pool.tensor_tensor(h_lo[:, :, cols], h[j][:, :, 0:r], h_hi[:, :, cols], ALU.subtract).then_inc(lo_done, 1)

        step(0, 0)
        with pool.Fori(0, NT // 2 - 1) as i:
            for j in range(2):
                step(2 * i + j + 1, 1 - j)
                lower(2 * i + j, j)
        step(NT - 1, 1)
        lower(NT - 2, 0)
        step(NT, 0)
        lower(NT - 1, 1)
        lower(NT, 0)

    @block.scalar
    def _(act):
        act.wait_ge(vec_ld, 16)
        act.activation(sc[:, :, :], vecs[:, V_C:V_C + 16].rearrange("p (k n) -> p k n", n=2), ACT.Silu)\
           .then_inc(silu_done, 1)

        def load(t, j):
            r = rows_of(t)
            src = xs if r == DEC else xp[bass.ds(t * P, P), :]
            act.dma_start(x[j][0:r, :], src).then_inc(x_ld[j], 16)

        for t in range(2):
            load(t, t)
        own = Own(act, own_act)

        def square(t, j, nth):
            r = rows_of(t)
            act.wait_ge(sq_done, t)
            act.wait_ge(x_ld[j], 16 * (nth + 1))
            act.activation(squares[0:r, :], x[j][0:r, :], ACT.Square, accum_out=ssq[0:r, j:j + 1]).then_inc(sq_done, 1)

        def move(t, j, more):
            r, n = rows_of(t), cond_of(t)
            act.wait_ge(xT_ready, t + 1)
            if not (isinstance(t, int) and t < 2):
                act.wait_ge(lo_done, t - 1)
            for c in range(0, NC // 2):
                ins = act.activation(h[j][:, c, 0:r], xT_ps[j][:, c, 0:r], ACT.Identity,
                                     bias=mod[:, SH1, c, n:n + 1], scale=a1[:, c, n:n + 1])
            ins.then_inc(xT_out_act, 1)
            act.wait_ge(xT_out_act, t + 1)
            act.wait_ge(xT_out_dve, t + 1)
            act.activation(h_hi[:, :, bass.ds(t * P, r)], h[j][:, :, 0:r], ACT.Copy).then_inc(hi_done, 1)
            if more:
                load(*more)

        def modulation_out(n, j):
            act.wait_ge(mrow_ready, n + 1)
            act.activation(mod_rows[j][:, :], f_ps[0:2, 512 * j:512 * j + 512], ACT.Copy).then_inc(mrow_out, 1)

        square(0, 0, 0)
        for n in range(4):
            modulation_out(n, n % 2)
        act.wait_ge(a1_done, 1)
        for j in range(2):
            square(j + 1, 1 - j, j)
            move(j, j, (j + 2, j))
            modulation_out(4 + j, j)
        with act.Fori(1, NT // 2 - 1) as i:
            for j in range(2):
                square(2 * i + j + 1, 1 - j, i + j)
                move(2 * i + j, j, (2 * i + j + 2, j))
                modulation_out(2 * i + j + 4, j)
        square(NT - 1, 1, NT // 2 - 1)
        move(NT - 2, 0, (NT, 0))
        modulation_out(NT + 2, 0)
        square(NT, 0, NT // 2)
        move(NT - 1, 1, None)
        modulation_out(NT + 3, 1)
        move(NT, 0, None)
        act.wait_ge(wf_ld, 48)
        act.activation(w_f_hi[:, :, :], w_f[:, :, :], ACT.Copy).then_inc(wf_split, 1)
        act.wait_ge(z_done, 1)
        own(act.activation(e[:, :], z[:, :], ACT.Abs))
        own(act.activation(e[:, :], e[:, :], ACT.Exp, scale=-1.0))
        act.activation(e[:, :], e[:, :], ACT.Ln, bias=1.0).then_inc(e_done, 1)

    @block.tensor
    def _(pe):
        pe.wait_ge(silu_done, 1)
        ident = consts[:, K_ID:K_ID + P]

        def modulation(n, j, nth):
            pe.wait_ge(w_ld[j], 16 * (nth + 1))
            modulation_rows(pe, w_ada[j], sc, f_ps[:, 512 * j:512 * j + 512]).then_inc(mrow_ready, 1)
            pe.wait_ge(mrow_out, n + 1)
            for c in range(NC // 2):
                ins = pe.matmul(mod_ps[:, bass.ds(n * 8 + 2 * c, 2)], mod_rows[j][:, c * P:(c + 1) * P], ident[0:2, 0:2],
                                start=True, stop=True)
            ins.then_inc(mod_ready, 1)

        pe.wait_ge(c_ld, 16)
        for n in range(4):
            modulation(n, n % 2, n // 2)

        def step(t, j):
            r = rows_of(t)
            pe.wait_ge(xn_done, t + 1)
            pe.wait_ge(xT_out_act, t)
            pe.wait_ge(xT_out_dve, t)
            for c in range(NC):
                ins = pe.transpose(xT_ps[j][:, c, 0:r], x[j][0:r, c * P:(c + 1) * P], ident[0:r, 0:r])
            ins.then_inc(xT_ready, 1)

        with pe.Fori(0, NT // 2) as i:
            for j in range(2):
                step(2 * i + j, j)
                if j == 0:
                    pe.wait_ge(a1_done, 1)
                modulation(2 * i + j + 4, j, i + 2)
        step(NT, 0)
        pe.wait_ge(wf_split, 2)
        pe.wait_ge(lo_done, NT + 1)
        for n0, n in ((0, 512), (512, 512), (SEQ, DEC)):
            m = 0
            for kc in range(NC):
                for wf, h_part in ((w_f_hi, h_hi), (w_f_hi, h_lo), (w_f_lo, h_hi)):
                    ins = pe.matmul(f_ps[:, n0:n0 + n], wf[:, kc, :], h_part[:, kc, n0:n0 + n],
                                    start=(m == 0), stop=(m == 3 * NC - 1))
                    m += 1
        ins.then_inc(f_ready, 1)
        pe.wait_ge(logf_done, 1)
        pe.wait_ge(mod_out, 1)
        for t in range(NT + 1):
            r = rows_of(t)
            ins = pe.transpose(mod_ps[0:r, 128 + 8 * t:136 + 8 * t], logf[:, t * P:t * P + r], ident[0:8, 0:8])
        ins.then_inc(rows_ready, 1)

    @block.vector
    def _(dve):
        own = Own(dve, own_dve)

        def normalise(t, j):
            r = rows_of(t)
            dve.wait_ge(sq_done, t + 1)
            dve.tensor_scalar(ssq[0:r, j:j + 1], ssq[0:r, j:j + 1], 1.0 / D, EPS, ALU.mult, ALU.add).then_inc(ms_done, 1)
            dve.wait_ge(rstd_done, t + 1)
            dve.tensor_scalar(x[j][0:r, :], x[j][0:r, :], rstd[0:r, j:j + 1], None, ALU.mult).then_inc(xn_done, 1)

        def move(t, j):
            r, n = rows_of(t), cond_of(t)
            dve.wait_ge(xT_ready, t + 1)
            if not (isinstance(t, int) and t < 2):
                dve.wait_ge(lo_done, t - 1)
            for c in range(NC // 2, NC):
                ins = dve.tensor_scalar(h[j][:, c, 0:r], xT_ps[j][:, c, 0:r], a1[:, c, n:n + 1],
                                        mod[:, SH1, c, n:n + 1], ALU.mult, ALU.add)
            ins.then_inc(xT_out_dve, 1)

        dve.wait_ge(vec_ld, 16)
        for sec in (SH1, SC1):
            dve.wait_ge(mod_ready, 4)
            bias = vecs[:, V_BADA + 8 * sec:V_BADA + 8 * sec + 8]
            own(dve.tensor_tensor(mod[:, sec, :, :], mod_ps[:, 16 * sec:16 * sec + 16].rearrange("p (c n) -> p c n", n=2),
                                  rep(bias, 2, 2), ALU.add))
        dve.scalar_tensor_tensor(a1[:, :, :], mod[:, SC1, :, :], 1.0, rep(vecs[:, V_NMIX:V_NMIX + 8], 2, 2),
                                 ALU.add, ALU.mult).then_inc(a1_done, 1)
        dve.wait_ge(a1_done, 1)
        normalise(0, 0)
        for j in range(2):
            normalise(j + 1, 1 - j)
            move(j, j)
        with dve.Fori(1, NT // 2 - 1) as i:
            for j in range(2):
                normalise(2 * i + j + 1, 1 - j)
                move(2 * i + j, j)
        normalise(NT - 1, 1)
        move(NT - 2, 0)
        normalise(NT, 0)
        move(NT - 1, 1)
        move(NT, 0)

        dve.wait_ge(wf_split, 1)
        dve.tensor_tensor(w_f_lo[:, :, :], w_f[:, :, :], w_f_hi[:, :, :], ALU.subtract).then_inc(wf_split, 1)
        dve.wait_ge(mod_ready, HALVES)
        dve.tensor_tensor(mod[:, G1:G2 + 1, :, :].rearrange("p s c n -> p (s c) n"),
                          mod_ps[:, 16 * G1:16 * (G2 + 1)].rearrange("p (c n) -> p c n", n=2),
                          rep(vecs[:, V_BADA + 8 * G1:V_BADA + 8 * (G2 + 1)], 2, 2), ALU.add).then_inc(mod_out, 1)
        dve.wait_ge(f_ready, 1)
        dve.wait_ge(wf_ld, 48)
        dve.tensor_scalar(z[:, :], f_ps[:, 0:TOK], b_f[:, 0:1], None, ALU.add).then_inc(z_done, 1)
        dve.wait_ge(e_done, 1)
        dve.scalar_tensor_tensor(logf[:, :], z[:, :], 0.0, e[:, :], ALU.min, ALU.subtract).then_inc(logf_done, 1)
        dve.wait_ge(logf_done, 1)
        own(dve.tensor_copy(logf_s[:, PAST:PAST + DEC], logf[:, SEQ:TOK]))
        one = consts[0:8, K_ONES:K_ONES + 1]
        own(dve.tensor_tensor_scan(cum[:, 0:SEQ], one.to_broadcast([8, SEQ]), logf[:, 0:SEQ], 0.0, ALU.mult, ALU.add))
        own(dve.tensor_tensor_scan(cum[:, SEQ:KEYS], one.to_broadcast([8, PAST + DEC]), logf_s[:, :], 0.0,
                                   ALU.mult, ALU.add))
        dve.tensor_scalar(cum[:, :], cum[:, :], -1.0 / SCALE, None, ALU.mult).then_inc(cum_done, 1)
        dve.wait_ge(rows_ready, 1)
        dve.tensor_copy(logf_rows[:, 0:NT, :], mod_ps[:, 128:128 + 8 * NT].rearrange("p (t h) -> p t h", h=8))
        dve.tensor_copy(logf_rows[0:DEC, NT, :], mod_ps[0:DEC, 128 + 8 * NT:136 + 8 * NT]).then_inc(rows_out, 1)


def unit_keys(group, t):
    if t == NT:
        return [(SEQ, PAST, "cache"), (SEQ + PAST, DEC, NT)]
    first = max(0, t - BAND_TILES + 1) if group == "band" else 0
    return [(b * P, P, b) for b in range(first, t + 1)]


def attend(nc, s, group, a, o, k, hT, w):
    fox = group == "fox"
    consts, rows_all, waited = k["consts"], k["rows_all"], k["waited"]
    g = 0 if fox else 1
    ident = consts[:, K_ID:K_ID + P]
    h_hi, h_lo = hT
    most = SEQ if fox else BAND
    kv = s.sb("kv", [P, NT + 1, 2, P])
    cache = s.sb("cache", [P, 2, P])
    twice = s.sb("twice", [P, 2, 2, 2, HD])
    q_both = s.sb("q_both", [P, 2, TOK], F32R)
    k_hi = s.sb("k_hi", [P, 2, KEYS], F32R)
    k_lo = s.sb("k_lo", [P, 2, KEYS], F32R)
    probs = [s.sb(f"probs{j}", [P, most]) for j in range(2)]
    pT = [s.sb(f"pT{j}", [P, most // P, P]) for j in range(2)]
    oT = s.sb("oT", [P, P])
    nmax = s.sb("nmax", [P, UNITS])
    denom = s.sb("denom", [P, UNITS])
    rden = s.sb("rden", [P, UNITS])
    if fox:
        bias = s.sb("forget", [P, 2, KEYS])
        ident_r = s.sb("ident_r", [P, P], F32R)
        causal_r = s.sb("causal_r", [P, P], F32R)
    else:
        bias = s.sb("bias", [P, 2, BAND])
    s_ps = [s.ps(f"s{j}", [P, 1024]) for j in range(2)]
    pT_ps = s.ps("pT", [P, NT, P])
    o_ps = [s.ps(f"o{j}", [P, 512]) for j in range(2)]
    banks = [s_ps[n // 2][:, 512 * (n % 2):512 * (n % 2) + 512] for n in range(4)]
    slot = [t % 4 for t in range(NT)] + [1]

    w_ld, w_split = k["w_ld"], k["w_split"]
    cache_ld, bias_ld = s.sem("cache_ld"), s.sem("bias_ld")
    bias_set = None if fox else s.sem("bias_set")
    rows_ready, kv_out, q_twice, k_twice = s.sem("rows_ready"), s.sem("kv_out"), s.sem("q_twice"), s.sem("k_twice")
    T_ready, hi_done, lo_done = s.sem("T_ready"), s.sem("hi_done"), s.sem("lo_done")
    s_ready, max_done, exp_done = s.sem("s_ready"), s.sem("max_done"), s.sem("exp_done")
    pT_ready, pT_out, o_ready, oT_out, back_ready, rden_done, o_out = (
        s.sem(n) for n in ("pT_ready", "pT_out", "o_ready", "oT_out", "back_ready", "rden_done", "o_out"))
    stored, masks_set = s.sem("stored"), s.sem("masks_set")
    block = s.ctx.enter_context(nc.Block())

    TILES, TS = NT + 1, NT + 2
    ORDER = [0, 4, 1, 5, 2, 6, 3, 7, NT]
    units = [(ORDER[u // 2], u % 2) for u in range(UNITS)]
    keys = [unit_keys(group, t) for t, _ in units]
    chunks = [[(b, min(b + 4, len(kb))) for b in range(0, len(kb), 4)] for kb in keys]
    chunk0 = [sum(len(c) for c in chunks[:u]) for u in range(UNITS + 1)]

    @block.sync
    def _(sp):
        def load_w(n):
            for m in range(2):
                if not isinstance(n, int) or m:
                    alone(sp, w_split, 4 * n + 2 * m, waited)
                sp.dma_start(w["raw"][:, :, :], a["w_qkv"][bass.ds(n, 1), :, 4 * m:4 * m + 4, :]
                             .rearrange("a p k n -> p (a k) n")).then_inc(w_ld, 16)

        def store_rows(i):
            t0 = 0 if fox else NT - o["k_b_prompt"].shape[0] // P
            for n, name in enumerate(("k", "v")):
                dst = o[f"{name}_{'a' if fox else 'b'}_prompt"][:, bass.ds(i * P, P)]
                sp.dma_start(dst.rearrange("(t p) n -> p t n", p=P), kv[:, t0:NT, n, :]).then_inc(stored, 16)
                dst = o[f"{name}_{'a' if fox else 'b'}_sample"][:, bass.ds(i * P, P)]
                sp.dma_start(dst, kv[0:DEC, NT, n, :]).then_inc(stored, 16)

        if fox:
            load_w(0)
        with sp.Fori(0, PAIRS) as i:
            sp.wait_ge(o_ready, UNITS * i)
            sp.wait_ge(max_done, UNITS * i)
            src = k["forget"][bass.ds(2 * i, 2), :] if fox else None
            sp.dma_start(bias[:, :, :], rep(src, 0, P) if fox else a["rel"][:, bass.ds(2 * i, 2), :]).then_inc(bias_ld, 16)
            for n, name in enumerate(("k", "v")):
                sp.dma_start(cache[:, n, :], a[f"cache_{name}_{'a' if fox else 'b'}"][:, bass.ds(i * P, P)])\
                  .then_inc(cache_ld, 16)
            sp.wait_ge(kv_out, TILES * (i + 1))
            store_rows(i)
            if fox:
                load_w(i + 1)
            else:
                with sp.If(i < PAIRS - 1):
                    load_w(nc.s_assert_within(i + (PAIRS + 1), 0, 2 * PAIRS - 1,
                                              skip_runtime_bounds_check_because="the branch says i < PAIRS - 1"))
                with sp.Else():
                    sp.nop()
        sp.wait_ge(stored, 64 * PAIRS)

    @block.gpsimd
    def _(pool):
        with pool.Fori(0, PAIRS) as i:
            for t in range(TS):
                r = rows_of(t) if t < TILES else PAST
                if t < TILES:
                    alone(pool, kv_out, TILES * i + t + 1, waited)
                    src = kv[0:r, t, 0, :]
                else:
                    alone(pool, cache_ld, 32 * (i + 1), waited)
                    src = cache[:, 0, :]
                alone(pool, T_ready, TS * i + t, waited)
                pool.tensor_copy(twice[0:r, 1, :, :, :], rep(src.rearrange("p (h n) -> p h n", h=2), 2, 2))\
                    .then_inc(k_twice, 1)

            def split():
                alone(pool, rows_ready, TILES * (i + 1), waited)
                for m in range(2):
                    n, kc = i + (1 + PAIRS * g), slice(4 * m, 4 * m + 4)
                    alone(pool, w_ld, 32 * n + 16 * (m + 1), waited)
                    pool.tensor_copy(w["hi"][:, kc, :], w["raw"][:, :, :]).then_inc(w_split, 1)
                    alone(pool, w_split, 4 * n + 2 * m + 1, waited)
                    pool.tensor_tensor(w["lo"][:, kc, :], w["raw"][:, :, :], w["hi"][:, kc, :], ALU.subtract)\
                        .then_inc(w_split, 1)

            if fox:
                split()
            else:
                with pool.If(i < PAIRS - 1):
                    split()
                with pool.Else():
                    pool.nop()

    @block.tensor
    def _(pe):
        with pe.Fori(0, PAIRS) as i:
            def rows(t):
                r = rows_of(t)
                if t == 0:
                    alone(pe, w_split, 4 * (i + 1 + PAIRS * g), waited)
                last = max((v for v in range(t) if slot[v] == slot[t]), default=None)
                if last is not None:
                    alone(pe, q_twice, TILES * i + last + 1, waited)
                n = 0
                for kc in range(NC):
                    for h, m in ((h_hi, "hi"), (h_hi, "lo"), (h_lo, "hi")):
                        ins = pe.matmul(banks[slot[t]][0:r, 0:3 * P], h[:, kc, t * P:t * P + r], w[m][:, kc, :],
                                        start=(n == 0), stop=(n == 3 * NC - 1))
                        n += 1
                ins.then_inc(rows_ready, 1)

            def to_columns(t):
                r = rows_of(t) if t < TILES else PAST
                if t < TILES:
                    alone(pe, q_twice, TILES * i + t + 1, waited)
                alone(pe, k_twice, TS * i + t + 1, waited)
                if t >= 2:
                    alone(pe, lo_done, TS * i + t - 1, waited)
                for n in range(0 if t < TILES else 2, 4):
                    ins = pe.transpose(pT_ps[:, 4 * (t % 2) + n, 0:r],
                                       twice[0:r, n // 2, n % 2, :, :].rearrange("p a n -> p (a n)"), ident[0:r, 0:r])
                ins.then_inc(T_ready, 1)

            def scores(u):
                (t, h), kb = units[u], keys[u]
                r = rows_of(t)
                if u < 2:
                    alone(pe, q_twice, TILES * i + 7, waited)
                if u < 2:
                    alone(pe, lo_done, TS * i + t + 1, waited)
                if u >= 2:
                    alone(pe, max_done, UNITS * i + u - 1, waited)
                k0, n = kb[0][0], sum(b[1] for b in kb)
                own = n - kb[-1][1]
                q = q_both[:, h, t * P:t * P + r]
                for c in range(0, n, 512):
                    m = min(512, n - c)
                    masked = fox and c <= own < c + m
                    pe.matmul(s_ps[u % 2][0:r, c:c + m], q, k_hi[:, h, k0 + c:k0 + c + m], start=True, stop=False)
                    ins = pe.matmul(s_ps[u % 2][0:r, c:c + m], q, k_lo[:, h, k0 + c:k0 + c + m],
                                    start=False, stop=not masked)
                    if masked:
                        ins = pe.matmul(s_ps[u % 2][0:r, own:n], ident_r[0:r, 0:r], causal_r[0:r, 0:r],
                                        start=False, stop=True)
                ins.then_inc(s_ready, 1)

            def transpose(u):
                (t, h), kb = units[u], keys[u]
                r = rows_of(t)
                alone(pe, exp_done, UNITS * i + u + 1, waited)
                for b0, b1 in chunks[u]:
                    for b in range(b0, b1):
                        m = kb[b][1]
                        ins = pe.transpose(pT_ps[0:m, b, 0:r], probs[u % 2][0:r, b * P:b * P + m], ident[0:r, 0:r])
                    ins.then_inc(pT_ready, 1)

            def values(u):
                (t, h), kb = units[u], keys[u]
                r = rows_of(t)
                at = u // 2
                if at >= 2 and h == 0:
                    alone(pe, o_out, TILES * i + at - 1, waited)
                for n, (b0, b1) in enumerate(chunks[u]):
                    alone(pe, pT_out, chunk0[UNITS] * i + chunk0[u] + n + 1, waited)
                    for b in range(b0, b1):
                        _, m, vt = kb[b]
                        v = cache[0:m, 1, HD * h:HD * h + HD] if vt == "cache" else kv[0:m, vt, 1, HD * h:HD * h + HD]
                        ins = pe.matmul(o_ps[at % 2][HD * h:HD * h + HD, 0:r], v, pT[u % 2][0:m, b, 0:r],
                                        start=(b == 0), stop=(b == len(kb) - 1))
                ins.then_inc(o_ready, 1)

            def to_rows(at):
                r = rows_of(ORDER[at])
                alone(pe, oT_out, TILES * i + at + 1, waited)
                pe.transpose(o_ps[at % 2][0:r, P:2 * P], oT[:, 0:r], ident).then_inc(back_ready, 1)

            rows(0)
            for t in range(1, TILES):
                rows(t)
                to_columns(t - 1)
            if fox:
                alone(pe, masks_set, 2, waited)
            scores(0)
            scores(1)
            to_columns(TILES - 1)
            to_columns(TILES)
            alone(pe, lo_done, TS * (i + 1), waited)
            for u in range(UNITS):
                if u:
                    alone(pe, pT_out, chunk0[UNITS] * i + chunk0[u], waited)
                transpose(u)
                if u + 2 < UNITS:
                    scores(u + 2)
                if u:
                    values(u - 1)
                if u % 2 == 1 and u >= 3:
                    to_rows(u // 2 - 1)
            values(UNITS - 1)
            to_rows(TILES - 1)

    @block.vector
    def _(dve):
        if fox:
            for m in range(2):
                kc = slice(4 * m, 4 * m + 4)
                dve.wait_ge(w_split, 2 * m + 1)
                dve.tensor_tensor(w["lo"][:, kc, :], w["raw"][:, :, :], w["hi"][:, kc, :], ALU.subtract).then_inc(w_split, 1)
        with dve.Fori(0, PAIRS) as i:
            def kv_rows(t):
                r = rows_of(t)
                dve.wait_ge(rows_ready, TILES * i + t + 1)
                dve.tensor_copy(kv[0:r, t, :, :], banks[slot[t]][0:r, P:3 * P].rearrange("p (a n) -> p a n", a=2))\
                   .then_inc(kv_out, 1)

            def lower(t):
                r = rows_of(t) if t < TILES else PAST
                k0 = t * P if t < NT else (SEQ + PAST if t == NT else SEQ)
                alone(dve, hi_done, TS * i + t + 1, waited)
                bank = pT_ps[:, 4 * (t % 2):4 * (t % 2) + 4, 0:r]
                if t < TILES:
                    low = q_both[HD:P, :, t * P:t * P + r]
                    dve.tensor_tensor(low, bank[HD:P, 0:2, :], low, ALU.subtract)
                dve.tensor_tensor(k_lo[:, :, k0:k0 + r], bank[:, 2:4, :], k_hi[:, :, k0:k0 + r], ALU.subtract)\
                   .then_inc(lo_done, 1)

            def row_max(u):
                (t, h), kb = units[u], keys[u]
                r, n = rows_of(t), sum(b[1] for b in kb)
                alone(dve, s_ready, UNITS * i + u + 1, waited)
                j0 = kb[0][0] if fox else ((BAND_TILES - 1) * P - PAST if t == NT else BAND - n)
                dve.tensor_tensor_reduce(probs[u % 2][0:r, 0:n], s_ps[u % 2][0:r, 0:n], bias[0:r, h, j0:j0 + n],
                                         -SCALE, BIG, ALU.add, ALU.min, nmax[0:r, u:u + 1]).then_inc(max_done, 1)

            def move_pT(u):
                (t, h), kb = units[u], keys[u]
                r = rows_of(t)
                if u >= 2:
                    alone(dve, o_ready, UNITS * i + u - 1, waited)
                for n, (b0, b1) in enumerate(chunks[u]):
                    dve.wait_ge(pT_ready, chunk0[UNITS] * i + chunk0[u] + n + 1)
                    if t == NT:
                        dve.tensor_copy(pT[u % 2][:, 0, 0:r], pT_ps[:, 0, 0:r])
                        ins = dve.tensor_copy(pT[u % 2][0:DEC, 1, 0:r], pT_ps[0:DEC, 1, 0:r])
                    else:
                        ins = dve.tensor_copy(pT[u % 2][:, b0:b1, :], pT_ps[:, b0:b1, :])
                    ins.then_inc(pT_out, 1)
                dve.reciprocal(rden[0:r, u:u + 1], denom[0:r, u:u + 1]).then_inc(rden_done, 1)

            alone(dve, bias_ld, 16 * (i + 1), waited)
            if not fox:
                dve.tensor_scalar(bias[:, :, :], bias[:, :, :], 1.0 / SCALE, None, ALU.mult).then_inc(bias_set, 1)
                alone(dve, bias_set, i + 1, waited)
                dve.memset(bias[P // 2:P, :, 0:HD], NEG)
                dve.memset(bias[0:P // 2, :, BAND - HD:BAND], NEG).then_inc(masks_set, 1)
            alone(dve, stored, 64 * i, waited)
            kv_rows(0)
            for t in range(1, TILES):
                kv_rows(t)
                lower(t - 1)
            if not fox:
                alone(dve, masks_set, i + 1, waited)
            alone(dve, o_out, TILES * i, waited)
            row_max(0)
            row_max(1)
            lower(TILES - 1)
            lower(TILES)
            for u in range(UNITS):
                move_pT(u)
                if u + 2 < UNITS:
                    row_max(u + 2)

    @block.scalar
    def _(act):
        if fox:
            for m in range(2):
                act.wait_ge(w_ld, 16 * (m + 1))
                act.activation(w["hi"][:, 4 * m:4 * m + 4, :], w["raw"][:, :, :], ACT.Copy).then_inc(w_split, 1)
            act.activation(ident_r[:, :], ident, ACT.Copy).then_inc(masks_set, 1)
            act.activation(causal_r[:, :], consts[:, K_CAUSAL:K_CAUSAL + P], ACT.Copy).then_inc(masks_set, 1)
        with act.Fori(0, PAIRS) as i:
            def q_rows(t):
                r = rows_of(t)
                act.wait_ge(kv_out, TILES * i + t + 1)
                act.wait_ge(T_ready, TS * i + t)
                act.activation(twice[0:r, 0, :, :, :],
                               rep(banks[slot[t]][0:r, 0:P].rearrange("p (h n) -> p h n", h=2), 2, 2), ACT.Copy)\
                   .then_inc(q_twice, 1)

            def upper(t):
                r = rows_of(t) if t < TILES else PAST
                k0 = t * P if t < NT else (SEQ + PAST if t == NT else SEQ)
                act.wait_ge(T_ready, TS * i + t + 1)
                bank = pT_ps[:, 4 * (t % 2):4 * (t % 2) + 4, 0:r]
                if t < TILES:
                    act.activation(q_both[:, :, t * P:t * P + r], bank[:, 0:2, :], ACT.Copy)
                act.activation(k_hi[:, :, k0:k0 + r], bank[:, 2:4, :], ACT.Copy).then_inc(hi_done, 1)

            def exp(u):
                r, n = rows_of(units[u][0]), sum(b[1] for b in keys[u])
                act.wait_ge(max_done, UNITS * i + u + 1)
                act.activation(probs[u % 2][0:r, 0:n], probs[u % 2][0:r, 0:n], ACT.Exp, bias=nmax[0:r, u:u + 1],
                               scale=-1.0, accum_out=denom[0:r, u:u + 1]).then_inc(exp_done, 1)

            def columns_out(at):
                r = rows_of(ORDER[at])
                act.wait_ge(o_ready, UNITS * i + 2 * at + 2)
                act.activation(oT[:, 0:r], o_ps[at % 2][:, 0:r], ACT.Copy).then_inc(oT_out, 1)

            def rows_out(at):
                t = ORDER[at]
                r = rows_of(t)
                act.wait_ge(back_ready, TILES * i + at + 1)
                act.wait_ge(rden_done, UNITS * i + 2 * at + 2)
                for h in range(2):
                    ins = act.activation(rows_all[0:r, t, bass.ds(i * P + (512 * g + HD * h), HD)],
                                         o_ps[at % 2][0:r, P + HD * h:P + HD * h + HD], ACT.Copy,
                                         scale=rden[0:r, 2 * at + h:2 * at + h + 1])
                ins.then_inc(o_out, 1)

            q_rows(0)
            for t in range(1, TILES):
                q_rows(t)
                upper(t - 1)
            exp(0)
            exp(1)
            upper(TILES - 1)
            upper(TILES)
            for u in range(UNITS):
                if u + 2 < UNITS:
                    exp(u + 2)
                if u % 2 == 1 and u >= 3:
                    rows_out(u // 2 - 1)
                elif u % 2 == 0 and u >= 2:
                    columns_out(u // 2 - 1)
            columns_out(TILES - 1)
            rows_out(TILES - 1)


def mix_out(nc, s, a, o, k, g2):
    consts, vecs, mod, rows_all, table = k["consts"], k["vecs"], k["mod"], k["rows_all"], k["table"]
    waited = k["waited"]
    ident = consts[:, K_ID:K_ID + P]
    ones = consts[:, K_ONES:K_ONES + P]
    w_out = s.sb("w_out", [P, NC, D])
    w_r = s.sb("w_r", [P, NC, NR])
    b_r = s.sb("b_r", [P, NR])
    g1, sh2, a2 = (s.sb(n, [P, 2, D]) for n in ("gate1_rows", "shift2_rows", "scale2_rows"))
    a2col = s.sb("a2col", [P, NC, 2])
    half = s.sb("minus_half", [P, 2 * NG * 2])
    x = s.sb("x", [P, D])
    osq = s.sb("osq", [P, D])
    hs, hr = s.sb("head_ms", [P, 16]), s.sb("head_rstd", [P, 16])
    on = s.sb("on", [P, D])
    oT = s.sb("oT", [P, NC, P])
    y = s.sb("y", [P, D])
    xsq = s.sb("xsq", [P, D])
    ms, rstd = s.sb("ms", [P, 1]), s.sb("rstd", [P, 1])
    h2 = s.sb("h2", [P, D])
    h2T = s.sb("h2T", [P, NC, P])
    lg = s.sb("lg", [P, NR])
    gmax = s.sb("gmax", [P, 1])
    dg = s.sb("dg", [P, NG])
    eg = s.sb("eg", [P, NG])
    gsum = s.sb("gsum", [P, 1])
    pri_g = s.sb("pri_g", [P, NG])
    best_g = s.sb("best_g", [P, 1])
    pen = s.sb("pen", [P, NG])
    em = s.sb("em", [P, NE])
    em2 = s.sb("em2", [P, NE])
    top = s.sb("top", [P, 8])
    pri_e = s.sb("pri_e", [P, NE])
    best_e = s.sb("best_e", [P, 1])
    oh = s.sb("oh", [P, 2, NE])
    dv, ev, den = s.sb("dv", [P, 1]), s.sb("ev", [P, 1]), s.sb("den", [P, 1])
    picked = s.sb("picked", [P, NE])
    before = s.sb("before", [P, NE])
    slot = s.sb("slot", [P, NE])
    junk = s.sb("junk", [P, NE])
    slot_f = s.sb("slot_f", [P, 2])
    slot_i = s.sb("slot_i", [P, 2], I32)
    tok = s.sb("tok", [P, 2, 2])
    entry = s.sb("entry", [P, 2, 4], I32)
    cnt = s.sb("cnt", [1, NE])
    need = s.sb("need", [1, NE, 9])
    nb, cb = s.sb("nb", [1, NE]), s.sb("cb", [1, NE])
    done = s.sb("done", [1, TABLE, NE])
    eb, bb, start = s.sb("eb", [1, TABLE]), s.sb("bb", [1, TABLE]), s.sb("start", [1, TABLE])
    pairs = s.sb("pairs", [1, NBLK // 2])
    steps = s.sb("steps", [1, 1])

    oT_ps, h2T_ps = s.ps("oT", [P, NC, P]), s.ps("h2T", [P, NC, P])
    y_ps = s.ps("y", [P, D])
    lg_ps, pos_ps = s.ps("lg", [P, 512]), s.ps("pos", [P, 512])

    ld, gate_cols, gate_ready, gate_out = s.sem("ld"), s.sem("gate_cols"), s.sem("gate_ready"), s.sem("gate_out")
    half_set, scaled, zeroed = s.sem("half_set"), s.sem("scaled"), s.sem("zeroed")
    osq_done, hms_done, hr_done, on_ready = s.sem("osq_done"), s.sem("hms_done"), s.sem("hr_done"), s.sem("on_ready")
    oT_ready, oT_out, y_ready, y_used = s.sem("oT_ready"), s.sem("oT_out"), s.sem("y_ready"), s.sem("y_used")
    x_ld, x1_done, xsq_done, ms_done, rstd_done = (s.sem(n) for n in ("x_ld", "x1_done", "xsq_done", "ms_done", "rstd_done"))
    scaled_h2, h2_ready, h2_stored = s.sem("scaled_h2"), s.sem("h2_ready"), s.sem("h2_stored")
    h2T_ready, h2T_out, lg_ready, lg_used = s.sem("h2T_ready"), s.sem("h2T_out"), s.sem("lg_ready"), s.sem("lg_used")
    dg_done, eg_done, dv_done, ev_done = s.sem("dg_done"), s.sem("eg_done"), s.sem("dv_done"), s.sem("ev_done")
    picked_done, pos_ready, slots_done, listed = (s.sem(n) for n in ("picked_done", "pos_ready", "slots_done", "listed"))
    cnt_ready, own_dve, w_own, g_own = s.sem("cnt_ready"), s.sem("own_dve"), s.sem("w_own"), s.sem("g_own")
    xp, xs = a["x_prompt"][0], a["x_sample"][0]
    block = s.ctx.enter_context(nc.Block())
    GATES = [(G1, g1), (SH2, sh2), (SC2, a2), (G2, g2)]

    LOOP = range(0, NT - 3)

    def over_steps(eng, step):
        for n in range(-3, 0):
            step(n)
        with eng.Fori(LOOP.start, LOOP.stop) as n:
            step(n)
        for n in range(LOOP.stop, NT + 1):
            step(n)

    def live(t):
        return not isinstance(t, int) or 0 <= t <= NT

    def tile_rows(t, r):
        return rows_all[0:r, bass.ds(t, 1), :].rearrange("p a n -> p (a n)")

    @block.sync
    def _(sp):
        sp.dma_start(w_out[:, :, :], a["w_out"]).then_inc(ld, 16)
        sp.dma_start(w_r[:, :, :], a["w_r"]).then_inc(ld, 16)
        sp.dma_start(b_r[:, :], rep(a["b_r"], 0, P)).then_inc(ld, 16)

        def step(n):
            t = n + 1
            if live(t):
                r = rows_of(t)
                sp.wait_ge(x1_done, t)
                sp.dma_start(x[0:r, :], xs if r == DEC else xp[bass.ds(t * P, P), :]).then_inc(x_ld, 16)
            if live(n):
                r = rows_of(n)
                sp.wait_ge(h2_ready, n + 1)
                sp.dma_start(k["h2"][bass.ds(n * P, r), :], h2[0:r, :]).then_inc(h2_stored, 16)

        over_steps(sp, step)
        sp.wait_ge(h2_stored, 16 * (NT + 1))

    @block.gpsimd
    def _(pool):
        pool.memset(half[:, :], -0.5).then_inc(half_set, 1)
        pool.memset(entry[:, :, :], 0).then_inc(zeroed, 1)
        pool.memset(before[:, :], 0.0).then_inc(zeroed, 1)
        pool.wait_ge(half_set, 1)

        def step(n):
            if live(n + 1):
                t, r = n + 1, rows_of(n + 1)
                pool.wait_ge(x_ld, 16 * (t + 1))
                pool.wait_ge(y_used, t + 1)
                pool.tensor_tensor(tile_rows(t, r), y[0:r, :], x[0:r, :], ALU.add).then_inc(x1_done, 1)
            if live(n + 3):
                t, r = n + 3, rows_of(n + 3)
                pool.wait_ge(hms_done, t + 1)
                pool.tensor_tensor(hr[0:r, :], hs[0:r, :], half[0:r, :], ALU.pow).then_inc(hr_done, 1)
            if live(n + 1):
                t, r = n + 1, rows_of(n + 1)
                pool.wait_ge(ms_done, t + 1)
                pool.tensor_tensor(rstd[0:r, :], ms[0:r, :], half[0:r, 0:1], ALU.pow).then_inc(rstd_done, 1)
                pool.wait_ge(scaled_h2, t + 1)
                pool.tensor_tensor(h2[0:r, :], h2[0:r, :], sh2[0:r, cond_of(t), :], ALU.add).then_inc(h2_ready, 1)
            if live(n):
                r = rows_of(n)
                alone(pool, slots_done, n + 1, waited)
                for pick in range(2):
                    pool.indirect_dma_start(k["lists"], bass.IndirectOffsetOnAxis(ap=slot_i[0:r, pick:pick + 1], axis=0),
                                            entry[0:r, pick, :], None, bounds_check=LISTS - 1, oob_is_err=False)\
                        .then_inc(listed, 16)

        over_steps(pool, step)
        pool.wait_ge(listed, 32 * (NT + 1))

    @block.tensor
    def _(pe):
        pe.wait_ge(gate_cols, 1)
        for n, (sec, _) in enumerate(GATES):
            for cond in range(2):
                m = 2 * n + cond
                dst = (oT_ps, h2T_ps)[m % 2]
                if m >= 2:
                    pe.wait_ge(gate_out, m - 1)
                for c in range(NC):
                    col = a2col[:, c, cond:cond + 1] if sec == SC2 else mod[:, sec, c, cond:cond + 1]
                    ins = pe.matmul(dst[:, c, :], col.to_broadcast([P, P]), ident, start=True, stop=True)
                ins.then_inc(gate_ready, 1)
        pe.wait_ge(gate_out, 2 * len(GATES))
        pe.wait_ge(scaled, NC)
        pe.wait_ge(ld, 48)

        def transpose_o(t):
            r = rows_of(t)
            pe.wait_ge(on_ready, t + 1)
            for c in range(NC):
                ins = pe.transpose(oT_ps[:, c, 0:r], on[0:r, c * P:(c + 1) * P], ident[0:r, 0:r])
            ins.then_inc(oT_ready, 1)

        def project(t):
            r = rows_of(t)
            pe.wait_ge(oT_out, t + 1)
            pe.wait_ge(y_used, t)
            for n in range(2):
                for c in range(NC):
                    ins = pe.matmul(y_ps[0:r, 512 * n:512 * n + 512], oT[:, c, 0:r], w_out[:, c, 512 * n:512 * n + 512],
                                    start=(c == 0), stop=(c == NC - 1))
            ins.then_inc(y_ready, 1)

        def transpose_h(t):
            r = rows_of(t)
            pe.wait_ge(h2_ready, t + 1)
            for c in range(NC):
                ins = pe.transpose(h2T_ps[:, c, 0:r], h2[0:r, c * P:(c + 1) * P], ident[0:r, 0:r])
            ins.then_inc(h2T_ready, 1)

        def route(t):
            r = rows_of(t)
            pe.wait_ge(h2T_out, t + 1)
            pe.wait_ge(lg_used, t)
            for c in range(NC):
                ins = pe.matmul(lg_ps[0:r, 0:NR], h2T[:, c, 0:r], w_r[:, c, :], start=(c == 0), stop=(c == NC - 1))
            ins.then_inc(lg_ready, 1)

        def positions(t):
            r = rows_of(t)
            pe.wait_ge(picked_done, t + 1)
            pe.wait_ge(slots_done, t)
            pe.matmul(pos_ps[0:r, 0:NE], consts[0:r, K_BEFORE:K_BEFORE + r], picked[0:r, :], start=True, stop=False)
            pe.matmul(pos_ps[0:r, 0:NE], ones[:, 0:r], before[:, :], start=False, stop=True).then_inc(pos_ready, 1)

        def step(n):
            if live(n):
                transpose_h(n)
            if live(n + 2):
                transpose_o(n + 2)
            if live(n):
                route(n)
            if live(n + 2):
                project(n + 2)
            if live(n):
                positions(n)

        over_steps(pe, step)
        pe.wait_ge(slots_done, NT + 1)
        pe.matmul(pos_ps[:, 64:64 + NE], ones, before[:, :], start=True, stop=True).then_inc(cnt_ready, 1)

    @block.scalar
    def _(act):
        for m in range(2 * len(GATES)):
            _, dst = GATES[m // 2]
            src = (oT_ps, h2T_ps)[m % 2]
            act.wait_ge(gate_ready, m + 1)
            act.activation(dst[:, m % 2, :], src[:, :, :].rearrange("p c n -> p (c n)"), ACT.Copy).then_inc(gate_out, 1)

        def step(n):
            if live(n):
                r = rows_of(n)
                act.wait_ge(h2T_ready, n + 1)
                act.activation(h2T[:, :, 0:r], h2T_ps[:, :, 0:r], ACT.Copy).then_inc(h2T_out, 1)
            if live(n + 2):
                r = rows_of(n + 2)
                act.wait_ge(oT_ready, n + 3)
                act.activation(oT[:, :, 0:r], oT_ps[:, :, 0:r], ACT.Copy).then_inc(oT_out, 1)
            if live(n + 3):
                t, r = n + 3, rows_of(n + 3)
                act.wait_ge(hms_done, t)
                act.activation(osq[0:r, :], tile_rows(t, r), ACT.Square).then_inc(osq_done, 1)
            if live(n + 1):
                t, r = n + 1, rows_of(n + 1)
                act.wait_ge(x1_done, t + 1)
                act.wait_ge(rstd_done, t)
                act.activation(xsq[0:r, :], tile_rows(t, r), ACT.Square, accum_out=ms[0:r, :]).then_inc(xsq_done, 1)
            if live(n):
                r = rows_of(n)
                act.wait_ge(dg_done, n + 1)
                act.activation(eg[0:r, :], dg[0:r, :], ACT.Exp, accum_out=gsum[0:r, :]).then_inc(eg_done, 1)
                act.wait_ge(dv_done, n + 1)
                act.activation(ev[0:r, :], dv[0:r, :], ACT.Exp).then_inc(ev_done, 1)

        over_steps(act, step)

    @block.vector
    def _(dve):
        dve.scalar_tensor_tensor(a2col[:, :, :], mod[:, SC2, :, :], 1.0, rep(vecs[:, V_NFFN:V_NFFN + 8], 2, 2),
                                 ALU.add, ALU.mult).then_inc(gate_cols, 1)
        dve.wait_ge(ld, 48)
        for c in range(NC):
            dve.tensor_scalar(w_out[:, c, :], w_out[:, c, :], vecs[:, V_ONORM + c:V_ONORM + c + 1], None, ALU.mult)\
               .then_inc(scaled, 1)
        dve.tensor_copy(tok[:, :, :], consts[:, K_TOK:K_TOK + 4].rearrange("p (a b) -> p a b", a=2)).then_inc(w_own, 1)
        dve.wait_ge(w_own, 1)
        dve.wait_ge(half_set, 1)
        dve.wait_ge(zeroed, 2)
        dve.wait_ge(gate_out, 2 * len(GATES))

        def gated(t):
            r = rows_of(t)
            dve.wait_ge(y_ready, t + 1)
            dve.wait_ge(x1_done, t)
            dve.tensor_tensor(y[0:r, :], y_ps[0:r, :], g1[0:r, cond_of(t), :], ALU.mult).then_inc(y_used, 1)

        def head_sums(t):
            r = rows_of(t)
            dve.wait_ge(osq_done, t + 1)
            dve.tensor_reduce(hs[0:r, :], osq[0:r, :].rearrange("p (h n) -> p h n", n=HD), AX.X, ALU.add)\
               .then_inc(w_own, 1)
            dve.wait_ge(w_own, t + 2)
            dve.tensor_scalar(hs[0:r, :], hs[0:r, :], 1.0 / HD, EPS, ALU.mult, ALU.add).then_inc(hms_done, 1)

        def mean_square(t):
            r = rows_of(t)
            dve.wait_ge(xsq_done, t + 1)
            dve.tensor_scalar(ms[0:r, :], ms[0:r, :], 1.0 / D, EPS, ALU.mult, ALU.add).then_inc(ms_done, 1)

        def scale_h2(t):
            r = rows_of(t)
            dve.wait_ge(rstd_done, t + 1)
            dve.wait_ge(h2_stored, 16 * t)
            dve.wait_ge(h2T_ready, t)
            dve.scalar_tensor_tensor(h2[0:r, :], tile_rows(t, r), rstd[0:r, 0:1], a2[0:r, cond_of(t), :],
                                     ALU.mult, ALU.mult).then_inc(scaled_h2, 1)

        def normalise_o(t):
            r = rows_of(t)
            dve.wait_ge(hr_done, t + 1)
            dve.wait_ge(oT_ready, t)
            dve.tensor_tensor(on[0:r, :].rearrange("p (h n) -> p h n", n=HD),
                              tile_rows(t, r).rearrange("p (h n) -> p h n", n=HD), rep(hr[0:r, :], 2, HD),
                              ALU.mult).then_inc(on_ready, 1)

        PICK = 20

        def pick(t):
            r = rows_of(t)
            own = Own(dve, own_dve, PICK * t)
            dve.wait_ge(lg_ready, t + 1)
            dve.tensor_tensor(lg[0:r, :], lg_ps[0:r, 0:NR], b_r[0:r, :], ALU.add).then_inc(lg_used, 1)
            dve.wait_ge(lg_used, t + 1)
            own(dve.tensor_reduce(gmax[0:r, :], lg[0:r, 0:NG], AX.X, ALU.max))
            dve.tensor_scalar(dg[0:r, :], lg[0:r, 0:NG], gmax[0:r, 0:1], None, ALU.subtract).then_inc(dg_done, 1)
            dve.wait_ge(dg_done, t + 1)
            own(dve.scalar_tensor_tensor(pri_g[0:r, :], dg[0:r, :], 0.0, consts[0:r, K_PRIG:K_PRIG + NG],
                                         ALU.is_equal, ALU.mult))
            own(dve.tensor_reduce(best_g[0:r, :], pri_g[0:r, :], AX.X, ALU.max))
            own(dve.tensor_scalar(pen[0:r, :], pri_g[0:r, :], best_g[0:r, 0:1], -1.0, ALU.is_equal, ALU.add))
            own(dve.scalar_tensor_tensor(em[0:r, :].rearrange("p (g e) -> p g e", g=NG), rep(pen[0:r, :], 2, EPG), 1e30,
                                         lg[0:r, NG:NR].rearrange("p (g e) -> p g e", g=NG), ALU.mult, ALU.add),
                wait=False)
            alone(dve, own_dve, PICK * t + own.n, waited)
            own(dve.max(top[0:r, :], em[0:r, :]))
            dve.tensor_scalar(dv[0:r, :], top[0:r, 1:2], top[0:r, 0:1], None, ALU.subtract).then_inc(dv_done, 1)
            src = em
            for n in range(2):
                own(dve.scalar_tensor_tensor(pri_e[0:r, :], src[0:r, :], top[0:r, n:n + 1],
                                             consts[0:r, K_PRIE:K_PRIE + NE], ALU.is_equal, ALU.mult))
                own(dve.tensor_reduce(best_e[0:r, :], pri_e[0:r, :], AX.X, ALU.max))
                own(dve.tensor_scalar(oh[0:r, n, :], pri_e[0:r, :], best_e[0:r, 0:1], None, ALU.is_equal))
                if n == 0:
                    own(dve.scalar_tensor_tensor(em2[0:r, :], oh[0:r, 0, :], -3e38, em[0:r, :], ALU.mult, ALU.add))
                    src = em2
            dve.tensor_tensor(picked[0:r, :], oh[0:r, 0, :], oh[0:r, 1, :], ALU.add).then_inc(picked_done, 1)
            dve.wait_ge(listed, 32 * t)
            dve.wait_ge(eg_done, t + 1)
            dve.wait_ge(ev_done, t + 1)
            weight = entry[0:r, :, 2].bitcast(F32)
            own(dve.tensor_scalar(den[0:r, :], ev[0:r, :], 1.0, gsum[0:r, 0:1], ALU.add, ALU.mult))
            own(dve.reciprocal(weight[:, 0:1], den[0:r, :]))
            dve.tensor_tensor(weight[:, 1:2], weight[:, 0:1], ev[0:r, :], ALU.mult)
            own(dve.tensor_copy(entry[0:r, :, 0:2], tok[0:r, :, :]))
            own(dve.tensor_scalar(tok[:, :, :], tok[:, :, :], float(P), None, ALU.add))
            dve.wait_ge(pos_ready, t + 1)
            own(dve.tensor_tensor(slot[0:r, :], pos_ps[0:r, 0:NE], consts[0:r, K_BASE:K_BASE + NE], ALU.add))
            for n in range(2):
                own(dve.tensor_tensor_reduce(junk[0:r, :], slot[0:r, :], oh[0:r, n, :], 1.0, 0.0, ALU.mult, ALU.add,
                                             slot_f[0:r, n:n + 1]))
            assert own.n == PICK, own.n
            dve.tensor_tensor(before[0:r, :], before[0:r, :], picked[0:r, :], ALU.add)
            dve.tensor_copy(slot_i[0:r, :], slot_f[0:r, :]).then_inc(slots_done, 1)

        def step(n):
            if live(n + 1):
                gated(n + 1)
            if live(n + 3):
                head_sums(n + 3)
            if live(n + 1):
                mean_square(n + 1)
                scale_h2(n + 1)
            if live(n + 3):
                normalise_o(n + 3)
            if live(n):
                pick(n)

        over_steps(dve, step)
        dve.wait_ge(slots_done, NT + 1)

        own = Own(dve, g_own)
        dve.wait_ge(cnt_ready, 1)
        own(dve.tensor_copy(cnt[:, :], pos_ps[0:1, 64:64 + NE]))
        own(dve.tensor_tensor(need[:, :, :], rep(cnt[:, :], 2, 9), rep(consts[0:1, K_THR:K_THR + 9], 1, NE), ALU.is_gt))
        own(dve.tensor_reduce(nb[:, :], need[:, :, :], AX.X, ALU.add))
        own(dve.tensor_tensor_scan(cb[:, :], ones[0:1, 0:NE], nb[:, :], 0.0, ALU.mult, ALU.add))
        blk = consts[0:1, K_BLK:K_BLK + TABLE]
        own(dve.tensor_tensor(done[:, :, :], rep(cb[:, :], 1, TABLE), rep(blk, 2, NE), ALU.is_le))
        own(dve.tensor_reduce(eb[:, :], done[:, :, :], AX.X, ALU.add))
        own(dve.tensor_tensor(done[:, :, :], done[:, :, :], rep(nb[:, :], 1, TABLE), ALU.mult))
        own(dve.tensor_reduce(bb[:, :], done[:, :, :], AX.X, ALU.add))
        own(dve.tensor_tensor(bb[:, :], blk, bb[:, :], ALU.subtract))
        own(dve.tensor_scalar(bb[:, :], bb[:, :], float(P), None, ALU.mult))
        own(dve.scalar_tensor_tensor(start[:, :], eb[:, :], float(REGION), bb[:, :], ALU.mult, ALU.add))
        own(dve.tensor_scalar(table[:, 2 + TABLE:2 + 2 * TABLE], start[:, :], float(DUMMY), None, ALU.min))
        own(dve.tensor_scalar(table[:, 2:2 + TABLE], eb[:, :], float(NE - 1), None, ALU.min))
        even = consts[0:1, K_BLK:K_BLK + NBLK].rearrange("p (n two) -> p n two", two=2)[:, :, 0]
        own(dve.tensor_scalar(pairs[:, :], even, cb[:, NE - 1:NE], None, ALU.is_lt))
        own(dve.tensor_reduce(steps[:, :], pairs[:, :], AX.X, ALU.add))
        own(dve.tensor_copy(table[:, 0:1], steps[:, :]))


def experts(nc, s, a, k):
    consts, table, waited = k["consts"], k["table"], k["waited"]
    ident = consts[:, K_ID:K_ID + P]
    w_gu = [s.sb(f"w_gu{j}", [P, NC, 2 * DE]) for j in range(2)]
    w_dn = [s.sb(f"w_dn{j}", [P, 2, D]) for j in range(2)]
    g_list = [s.sb(f"gather_list{j}", [P, 4], I32) for j in range(2)]
    s_list = [s.sb(f"scatter_list{j}", [P, 4], I32) for j in range(2)]
    x = [s.sb(f"x{j}", [P, D]) for j in range(2)]
    xT = s.sb("xT", [P, NC, P])
    gate = s.sb("gate", [P, DE])
    hidden = s.sb("hidden", [P, DE])
    hT = s.sb("hT", [P, 2, P])
    y = [s.sb(f"y{j}", [P, D]) for j in range(2)]
    xT_ps = s.ps("xT", [P, NC, P])
    gu_ps = [s.ps(f"gu{j}", [P, 512]) for j in range(2)]
    hT_ps = s.ps("hT", [P, 512])
    y_ps = s.ps("y", [P, D])

    gu_ld, dn_ld, gl_ld, sl_ld, gathered, scattered = (
        [s.sem(f"{n}{j}") for j in range(2)] for n in ("gu_ld", "dn_ld", "gl_ld", "sl_ld", "gathered", "scattered"))
    cleared, xT_ready, xT_out_act, xT_out_dve = (s.sem(n) for n in ("cleared", "xT_ready", "xT_out_act", "xT_out_dve"))
    gu_ready, gate_done, hidden_done, hT_ready, hT_out = (
        s.sem(n) for n in ("gu_ready", "gate_done", "hidden_done", "hT_ready", "hT_out"))
    y_ready, y_out_act, y_out_dve = s.sem("y_ready"), s.sem("y_out_act"), s.sem("y_out_dve")
    block = s.ctx.enter_context(nc.Block())

    def steps(eng, body):
        n = eng.value_load(table[0:1, 0:1], min_val=1, max_val=NBLK // 2)
        with eng.Fori(0, NBLK // 2) as i:
            with eng.If(i < n):
                for j in range(2):
                    body(i, j)
            with eng.Else():
                eng.nop()
        return n

    @block.sync
    def _(sp):
        def expert(b):
            return sp.value_load(table[0:1, bass.ds(b + 2, 1)], min_val=0, max_val=NE - 1)

        def start(b):
            return sp.value_load(table[0:1, bass.ds(b + (2 + TABLE), 1)], min_val=0, max_val=DUMMY)

        def gate_up(ex, j):
            sp.dma_start(w_gu[j][:, :, :], a["w_gu"][bass.ds(ex, 1)].rearrange("a p k n -> p (a k) n")).then_inc(gu_ld[j], 16)

        def down(ex, j):
            sp.dma_start(w_dn[j][:, :, :], a["w_dn"][bass.ds(ex, 1)].rearrange("a p k n -> p (a k) n")).then_inc(dn_ld[j], 16)

        def entries(first, dst, sem):
            sp.dma_start(dst[:, :], k["lists"][bass.ds(first, P), :]).then_inc(sem, 16)

        for j in range(2):
            entries(start(j), g_list[j], gl_ld[j])
            gate_up(expert(j), j)
        for j in range(2):
            first = start(2 + j)
            sp.wait_ge(gathered[j], 16)
            entries(first, g_list[j], gl_ld[j])
        down(expert(0), 0)
        entries(start(0), s_list[0], sl_ld[0])

        def body(i, j):
            b = 2 * i + j
            e2, e1, s4, s1 = expert(b + 2), expert(b + 1), start(b + 4), start(b + 1)
            alone(sp, gu_ready, b + 1, waited)
            gate_up(e2, j)
            alone(sp, y_ready, b, waited)
            down(e1, 1 - j)
            q, n = ahead(i, j, 2)
            alone(sp, gathered[q], 16 * (n + 1), waited)
            entries(s4, g_list[j], gl_ld[j])
            alone(sp, scattered[1 - j], 16 * (i + j), waited)
            entries(s1, s_list[1 - j], sl_ld[1 - j])

        n = steps(sp, body)
        alone(sp, gu_ld[0], 16 * n + 16, waited)
        alone(sp, gu_ld[1], 16 * n + 16, waited)
        alone(sp, dn_ld[0], 16 * n + 16, waited)
        alone(sp, dn_ld[1], 16 * n, waited)
        alone(sp, gl_ld[0], 16 * n + 32, waited)
        alone(sp, gl_ld[1], 16 * n + 32, waited)
        alone(sp, sl_ld[0], 16 * n + 16, waited)
        alone(sp, sl_ld[1], 16 * n, waited)

    @block.gpsimd
    def _(pool):
        for j in range(2):
            pool.memset(x[j][:, :], 0.0).then_inc(cleared, 1)
        pool.wait_ge(cleared, 2)

        def gather(j, nth):
            alone(pool, gl_ld[j], 16 * (nth + 1), waited)
            pool.indirect_dma_start(x[j][:, :], None, k["h2"], bass.IndirectOffsetOnAxis(ap=g_list[j][:, 0:1], axis=0),
                                    bounds_check=TOK - 1, oob_is_err=False).then_inc(gathered[j], 16)

        gather(0, 0)
        gather(1, 0)
        pool.wait_ge(xT_ready, 1)
        gather(0, 1)

        def body(i, j):
            b = 2 * i + j
            pool.wait_ge(xT_ready, b + 2)
            gather(*ahead(i, j, 3))
            pool.wait_ge(sl_ld[j], 16 * (i + 1))
            pool.wait_ge(y_out_act, b + 1)
            alone(pool, y_out_dve, b + 1, waited)
            pool.indirect_dma_start(k["yrows"], bass.IndirectOffsetOnAxis(ap=s_list[j][:, 1:2], axis=0), y[j][:, :], None,
                                    bounds_check=2 * TOK - 1, oob_is_err=False).then_inc(scattered[j], 16)

        n = steps(pool, body)
        alone(pool, scattered[0], 16 * n, waited)
        alone(pool, scattered[1], 16 * n, waited)
        alone(pool, gathered[0], 16 * n + 32, waited)
        alone(pool, gathered[1], 16 * n + 16, waited)

    @block.tensor
    def _(pe):
        def transpose_x(j, nth):
            pe.wait_ge(gathered[j], 16 * (nth + 1))
            for c in range(NC):
                ins = pe.transpose(xT_ps[:, c, :], x[j][:, c * P:(c + 1) * P], ident)
            ins.then_inc(xT_ready, 1)

        def gate_up(j, nth):
            b = 2 * nth + j
            pe.wait_ge(gu_ld[j], 16 * (nth + 1))
            pe.wait_ge(xT_out_act, b + 1)
            pe.wait_ge(xT_out_dve, b + 1)
            for c in range(NC):
                ins = pe.matmul(gu_ps[j][:, :], xT[:, c, :], w_gu[j][:, c, :], start=(c == 0), stop=(c == NC - 1))
            ins.then_inc(gu_ready, 1)

        def transpose_hidden(b):
            pe.wait_ge(hidden_done, b + 1)
            for c in range(2):
                ins = pe.transpose(hT_ps[:, c * P:(c + 1) * P], hidden[:, c * P:(c + 1) * P], ident)
            ins.then_inc(hT_ready, 1)

        def down(j, nth):
            b = 2 * nth + j
            pe.wait_ge(dn_ld[j], 16 * (nth + 1))
            pe.wait_ge(hT_out, b + 1)
            pe.wait_ge(y_out_act, b)
            pe.wait_ge(y_out_dve, b)
            for n in range(2):
                for c in range(2):
                    ins = pe.matmul(y_ps[:, 512 * n:512 * n + 512], hT[:, c, :], w_dn[j][:, c, 512 * n:512 * n + 512],
                                    start=(c == 0), stop=(c == 1))
            ins.then_inc(y_ready, 1)

        transpose_x(0, 0)
        gate_up(0, 0)
        transpose_x(1, 0)

        def body(i, j):
            gate_up(*ahead(i, j, 1))
            transpose_hidden(2 * i + j)
            transpose_x(*ahead(i, j, 2))
            down(j, i)

        steps(pe, body)

    @block.scalar
    def _(act):
        def move_xT(b):
            act.wait_ge(xT_ready, b + 1)
            act.activation(xT[:, 0:4, :], xT_ps[:, 0:4, :], ACT.Copy).then_inc(xT_out_act, 1)

        def silu(b, j):
            act.wait_ge(gu_ready, b + 1)
            act.wait_ge(hidden_done, b)
            act.activation(gate[:, :], gu_ps[j][:, 0:DE], ACT.Silu).then_inc(gate_done, 1)

        move_xT(0)
        silu(0, 0)
        move_xT(1)

        def body(i, j):
            b = 2 * i + j
            move_xT(b + 2)
            act.wait_ge(y_ready, b + 1)
            act.wait_ge(sl_ld[j], 16 * (i + 1))
            act.activation(y[j][:, 0:512], y_ps[:, 0:512], ACT.Copy, scale=s_list[j][:, 2:3].bitcast(F32))\
               .then_inc(y_out_act, 1)
            silu(b + 1, 1 - j)

        steps(act, body)

    @block.vector
    def _(dve):
        def move_xT(b):
            dve.wait_ge(xT_ready, b + 1)
            dve.tensor_copy(xT[:, 4:8, :], xT_ps[:, 4:8, :]).then_inc(xT_out_dve, 1)

        def gate_times_up(b, j):
            dve.wait_ge(gate_done, b + 1)
            dve.wait_ge(hT_ready, b)
            dve.tensor_tensor(hidden[:, :], gate[:, :], gu_ps[j][:, DE:2 * DE], ALU.mult).then_inc(hidden_done, 1)

        move_xT(0)
        gate_times_up(0, 0)
        move_xT(1)

        def body(i, j):
            b = 2 * i + j
            dve.wait_ge(hT_ready, b + 1)
            dve.tensor_copy(hT[:, :, :], hT_ps[:, 0:2 * P].rearrange("p (c n) -> p c n", c=2)).then_inc(hT_out, 1)
            move_xT(b + 2)
            dve.wait_ge(y_ready, b + 1)
            dve.wait_ge(sl_ld[j], 16 * (i + 1))
            dve.tensor_scalar(y[j][:, 512:1024], y_ps[:, 512:1024], s_list[j][:, 2:3].bitcast(F32), None, ALU.mult)\
               .then_inc(y_out_dve, 1)
            gate_times_up(b + 1, 1 - j)

        steps(dve, body)


def finish(nc, s, a, o, k, g2):
    rows_all = k["rows_all"]
    ya = s.sb("ya", [P, NT + 1, D])
    yb = [s.sb(f"yb{j}", [P, D]) for j in range(2)]
    squares = s.sb("squares", [P, D])
    ms, rstd = s.sb("ms", [P, 2]), s.sb("rstd", [P, 2])
    half = s.sb("minus_half", [P, 1])
    norm = s.sb("norm", [P, D])
    norm_ld, half_set = s.sem("norm_ld"), s.sem("half_set")
    y_ld = [s.sem(f"y_ld{j}") for j in range(2)]
    stored = s.sem("stored")
    summed, gated, x_done, sq_done, ms_done, rstd_done, out_ready = (
        s.sem(n) for n in ("summed", "gated", "x_done", "sq_done", "ms_done", "rstd_done", "out_ready"))
    block = s.ctx.enter_context(nc.Block())

    def in_turn(eng, first, second):
        first(0, 0, 0)
        with eng.Fori(0, NT // 2 - 1) as i:
            for j in range(2):
                first(2 * i + j + 1, 1 - j, i + j)
                second(2 * i + j, j, i)
        first(NT - 1, 1, NT // 2 - 1)
        second(NT - 2, 0, NT // 2 - 1)
        first(NT, 0, NT // 2)
        second(NT - 1, 1, NT // 2 - 1)
        second(NT, 0, NT // 2)

    def tile_rows(rows, t):
        return rows[0:rows_of(t), bass.ds(t, 1), :].rearrange("p a n -> p (a n)")

    @block.sync
    def _(sp):
        sp.dma_start(norm[:, :], rep(a["norm_final"], 0, P)).then_inc(norm_ld, 16)

        def load(t, j):
            r = rows_of(t)
            sp.dma_start(tile_rows(ya, t), k["yrows"][bass.ds(t * P, r), :]).then_inc(y_ld[j], 16)
            sp.dma_start(yb[j][0:r, :], k["yrows"][bass.ds(t * P + TOK, r), :]).then_inc(y_ld[j], 16)

        load(0, 0)
        load(1, 1)
        with sp.Fori(0, NT // 2 - 1) as i:
            for j in range(2):
                sp.wait_ge(summed, 2 * i + j + 1)
                load(2 * i + j + 2, j)
        sp.wait_ge(summed, NT - 1)
        load(NT, 0)

    @block.gpsimd
    def _(pool):
        pool.memset(half[:, :], -0.5).then_inc(half_set, 1)
        pool.wait_ge(half_set, 1)

        def add(t, j, nth):
            pool.wait_ge(y_ld[j], 32 * (nth + 1))
            pool.tensor_tensor(tile_rows(ya, t), tile_rows(ya, t), yb[j][0:rows_of(t), :], ALU.add).then_inc(summed, 1)

        def power(t, j, nth):
            r = rows_of(t)
            pool.wait_ge(ms_done, t + 1)
            pool.tensor_tensor(rstd[0:r, j:j + 1], ms[0:r, j:j + 1], half[0:r, :], ALU.pow).then_inc(rstd_done, 1)

        in_turn(pool, add, power)

    @block.scalar
    def _(act):
        def square(t, j, nth):
            r = rows_of(t)
            act.wait_ge(sq_done, t)
            act.wait_ge(x_done, t + 1)
            act.activation(squares[0:r, :], tile_rows(ya, t), ACT.Square, accum_out=ms[0:r, j:j + 1]).then_inc(sq_done, 1)

        def store(t, j, nth):
            r = rows_of(t)
            dst = o["y_sample"] if r == DEC else o["y_prompt"][bass.ds(t * P, P), :]
            act.wait_ge(out_ready, t + 1)
            act.dma_start(dst, tile_rows(ya, t)).then_inc(stored, 16)

        in_turn(act, square, store)
        act.wait_ge(stored, 16 * (NT + 1))

    @block.vector
    def _(dve):
        dve.wait_ge(norm_ld, 16)

        def residual(t, j, nth):
            r = rows_of(t)
            dve.wait_ge(summed, t + 1)
            dve.tensor_tensor(tile_rows(ya, t), tile_rows(ya, t), g2[0:r, cond_of(t), :], ALU.mult).then_inc(gated, 1)
            dve.wait_ge(gated, t + 1)
            dve.tensor_tensor(tile_rows(ya, t), tile_rows(ya, t), tile_rows(rows_all, t), ALU.add).then_inc(x_done, 1)

        def normalise(t, j, nth):
            r = rows_of(t)
            dve.wait_ge(sq_done, t + 1)
            dve.tensor_scalar(ms[0:r, j:j + 1], ms[0:r, j:j + 1], 1.0 / D, EPS, ALU.mult, ALU.add).then_inc(ms_done, 1)
            dve.wait_ge(rstd_done, t + 1)
            dve.scalar_tensor_tensor(tile_rows(ya, t), tile_rows(ya, t), rstd[0:r, j:j + 1], norm[0:r, :],
                                     ALU.mult, ALU.mult).then_inc(out_ready, 1)

        in_turn(dve, residual, normalise)


def constants():
    import numpy as np
    c = np.zeros((P, K_END), np.float32)
    i, j = np.arange(P)[:, None], np.arange(P)[None, :]
    c[:, K_ID:K_ID + P] = i == j
    c[:, K_CAUSAL:K_CAUSAL + P] = np.where(j <= i, 0.0, NEG)
    c[:, K_BEFORE:K_BEFORE + P] = i < j
    c[:, K_ONES:K_ONES + P] = 1.0
    c[:, K_PRIG:K_PRIG + NG] = NG - np.arange(NG)
    c[:, K_PRIE:K_PRIE + NE] = NE - np.arange(NE)
    c[:, K_BASE:K_BASE + NE] = REGION * np.arange(NE)
    c[:, K_THR:K_THR + 9] = P * np.arange(9)
    c[:, K_BLK:K_BLK + TABLE] = np.arange(TABLE)
    c[:, K_TOK:K_TOK + 4] = np.arange(P)[:, None] + np.array([0, 0, 0, TOK])
    return c


def kernel(**inputs):
    import numpy as np
    import concourse.bacc as bacc
    from concourse.bass_utils import run_bass_kernel_spmd

    x = {name: np.asarray(v) for name, v in inputs.items()}

    def by_partition(v):
        return v.reshape(-1, NC, P).transpose(2, 0, 1).reshape(P, -1)

    def rows(m):
        return m.reshape(-1, P, m.shape[-1]).transpose(1, 0, 2)

    w_in = x["w_in"][0]
    wa, wb = w_in[:, 0:1536], w_in[:, 1544:3080]
    qkv = np.stack([np.stack([np.concatenate([w[:, 512 * n + P * i:512 * n + P * (i + 1)] for n in range(3)], 1)
                              for i in range(PAIRS)]) for w in (wa, wb)])
    c2 = np.stack([x["c_prompt"][0], x["c_sample"][0]], 1)
    vecs = np.concatenate([
        rows(c2).reshape(P, 16), by_partition(x["b_ada"][0]), by_partition(x["norm_mix"][0]),
        by_partition(np.concatenate([x["onorm_a"][0], x["onorm_b"][0]])), by_partition(x["norm_ffn"][0])], 1)
    m = np.clip(BAND - P + np.arange(P)[:, None] - np.arange(BAND)[None, :], -128, 128) + 128
    arrays = {
        "x_prompt": x["x_prompt"], "x_sample": x["x_sample"],
        "consts": constants(), "vecs": vecs,
        "w_ada": x["w_ada"][0].reshape(NC, P, HALVES, D // 2).transpose(2, 1, 0, 3),
        "w_qkv": qkv.reshape(2 * PAIRS, NC, P, 3 * P).transpose(0, 2, 1, 3),
        "w_f": rows(w_in[:, 1536:1544]), "b_f": x["b_fgate"].reshape(8, 1),
        "cache_logf": x["cache_logf_a"][0, 0].T,
        "rel": x["rel_bias"][0][:, m].transpose(1, 0, 2),
        "w_out": rows(x["w_out"][0]),
        "w_r": rows(np.concatenate([x["w_router_group"][0], x["w_router_expert"][0]], 1)),
        "b_r": np.concatenate([x["b_router_group"][0], x["b_router_expert"][0]]),
        "w_gu": np.concatenate([x["w_gate"][0], x["w_up"][0]], 2).reshape(NE, NC, P, 2 * DE).transpose(0, 2, 1, 3),
        "w_dn": x["w_down"][0].reshape(NE, 2, P, D).transpose(0, 2, 1, 3),
        "norm_final": x["norm_final"],
    }
    for name in ("k_a", "v_a", "k_b", "v_b"):
        arrays["cache_" + name] = x["cache_" + name][0, 0].reshape(PAST, 512)
    lb = min(512, SEQ)
    outs = {"y_prompt": (SEQ, D), "y_sample": (DEC, D),
            "k_a_prompt": (SEQ, 512), "v_a_prompt": (SEQ, 512), "logf_prompt": (SEQ, 8),
            "k_b_prompt": (lb, 512), "v_b_prompt": (lb, 512),
            "k_a_sample": (DEC, 512), "v_a_sample": (DEC, 512), "logf_sample": (DEC, 8),
            "k_b_sample": (DEC, 512), "v_b_sample": (DEC, 512)}

    nc = bacc.Bacc("TRN2", target_bir_lowering=False, num_devices=1)
    arrays = {name: np.ascontiguousarray(v) for name, v in arrays.items()}
    a = {name: nc.dram_tensor(f"in_{name}", v.shape, mybir.dt.from_np(v.dtype), kind="ExternalInput").ap()
         for name, v in arrays.items()}
    o = {name: nc.dram_tensor(f"out_{name}", shape, F32, kind="ExternalOutput").ap() for name, shape in outs.items()}
    build(nc, a, o)
    r = run_bass_kernel_spmd(nc, [{f"in_{name}": v for name, v in arrays.items()}], core_ids=[0])
    got = {name: r.results[0][f"out_{name}"] for name in outs}

    def heads(name):
        v = got[name]
        return v.reshape(1, 1, v.shape[0], 8, HD)

    return (got["y_prompt"][None], got["y_sample"][None],
            heads("k_a_prompt"), heads("v_a_prompt"), got["logf_prompt"][None, None],
            heads("k_b_prompt"), heads("v_b_prompt"),
            heads("k_a_sample"), heads("v_a_sample"), got["logf_sample"][None, None],
            heads("k_b_sample"), heads("v_b_sample"))
```
